# Optimizing a Trainium2 kernel written in Bass

```python
import jax, jax.numpy as jnp
from jax import lax
import numpy as np

D_MODEL = 1024
BATCH = 1
SEQ = 512
DEPTH = 1

CHUNK = 64
N_MEM = 256
EPS = 1e-6

HG_EXPAND = 128
HG_HEADS = D_MODEL // HG_EXPAND
HG_DK = HG_EXPAND
HG_DV = D_MODEL // HG_HEADS
HG_WIDTH = HG_HEADS * HG_DV
HG_CHUNK = 32

SSM_EXPAND = 2
SSM_INNER = SSM_EXPAND * D_MODEL
SSM_HEADDIM = 64
SSM_HEADS = SSM_INNER // SSM_HEADDIM
SSM_STATE = 128
SSM_GROUPS = 8
SSM_HPG = SSM_HEADS // SSM_GROUPS
SSM_CONV = 4
SSM_CONV_DIM = SSM_INNER + 2 * SSM_GROUPS * SSM_STATE
SSM_NORM_GROUP = SSM_INNER // SSM_GROUPS

XA_HEADS = 4
XA_HEADDIM = D_MODEL // XA_HEADS
XA_WIDTH = XA_HEADS * XA_HEADDIM

N_BRANCH = 3
FFN_HIDDEN = ((8 * D_MODEL // 3 + 255) // 256) * 256

IN_SIZES = (HG_WIDTH, HG_WIDTH, HG_WIDTH, HG_WIDTH,
            SSM_INNER, SSM_CONV_DIM, SSM_HEADS,
            XA_WIDTH,
            N_BRANCH * D_MODEL)
IN_COLS = sum(IN_SIZES)

kernel_name = "hybrid_hgrn2_ssd_memxattn_block"

def rmsnorm(x, w):
    xf = x.astype(jnp.float32)
    y = xf * lax.rsqrt(jnp.mean(xf * xf, axis=-1, keepdims=True) + EPS)
    return (y * w.astype(jnp.float32)).astype(x.dtype)

def hgrn2_mixer(q, f_logit, i, og, lb, gn_w):
    f32 = jnp.float32
    bsz, s, _ = q.shape
    L = HG_CHUNK
    n = s // L
    q = jax.nn.silu(q.astype(f32))
    f = lb + (1.0 - lb) * jax.nn.sigmoid(f_logit.astype(f32))
    k = 1.0 - f
    g = jnp.log(f)
    shp = (bsz, n, L, HG_HEADS, HG_DK)
    q = q.reshape(shp)
    k = k.reshape(shp)
    g = g.reshape(shp)
    v = i.astype(f32).reshape(bsz, n, L, HG_HEADS, HG_DV)
    b = jnp.cumsum(g, axis=2)
    b_ref = b[:, :, L // 2:L // 2 + 1]
    b_last = b[:, :, -1:]
    qr = q * jnp.exp(b - b_ref)
    kr = k * jnp.exp(b_ref - b)
    A = jnp.einsum('bntzd,bnszd->bnzts', qr, kr)
    causal = jnp.tril(jnp.ones((L, L), dtype=bool))
    A = jnp.where(causal, A, 0.0)
    o_intra = jnp.einsum('bnzts,bnszv->bntzv', A, v)
    qi = q * jnp.exp(b)
    ki = k * jnp.exp(b_last - b)
    dchunk = jnp.exp(b_last[:, :, 0])

    def step(state, inp):
        qc, kc, vc, dc = inp
        o = jnp.einsum('btzd,bzdv->btzv', qc, state)
        state = dc[..., None] * state + jnp.einsum('bszd,bszv->bzdv', kc, vc)
        return state, o

    s0 = jnp.zeros((bsz, HG_HEADS, HG_DK, HG_DV), f32)
    _, o_inter = lax.scan(step, s0, (qi.swapaxes(0, 1), ki.swapaxes(0, 1),
                                     v.swapaxes(0, 1), dchunk.swapaxes(0, 1)))
    o = o_intra + o_inter.swapaxes(0, 1)
    o = o * lax.rsqrt(jnp.mean(o * o, axis=-1, keepdims=True) + EPS)
    o = o.reshape(bsz, s, HG_WIDTH) * gn_w.astype(f32)
    return o * jax.nn.silu(og.astype(f32))

def mamba2_mixer(z, xbc, dt, conv_w, conv_b, dt_bias, a_log, d_skip, norm_w):
    f32 = jnp.float32
    bsz, s, _ = z.shape
    L = CHUNK
    n = s // L
    conv = lax.conv_general_dilated(
        xbc.astype(f32), conv_w.astype(f32)[:, None, :], window_strides=(1,),
        padding=[(SSM_CONV - 1, 0)], dimension_numbers=('NWC', 'WIO', 'NWC'),
        feature_group_count=SSM_CONV_DIM)
    xbc = jax.nn.silu(conv + conv_b.astype(f32))
    xs, bm, cm = jnp.split(xbc, [SSM_INNER, SSM_INNER + SSM_GROUPS * SSM_STATE], axis=-1)
    xs = xs.reshape(bsz, n, L, SSM_GROUPS, SSM_HPG, SSM_HEADDIM)
    bm = bm.reshape(bsz, n, L, SSM_GROUPS, SSM_STATE)
    cm = cm.reshape(bsz, n, L, SSM_GROUPS, SSM_STATE)
    dt = jax.nn.softplus(dt.astype(f32) + dt_bias.astype(f32)).reshape(bsz, n, L, SSM_GROUPS, SSM_HPG)
    a = -jnp.exp(a_log.astype(f32)).reshape(SSM_GROUPS, SSM_HPG)
    cum = jnp.cumsum(dt * a, axis=2)
    X = xs * dt[..., None]
    causal = jnp.tril(jnp.ones((L, L), dtype=bool))
    seg = cum[:, :, :, None] - cum[:, :, None, :]
    ldec = jnp.exp(jnp.where(causal[:, :, None, None], seg, -jnp.inf))
    cb = jnp.einsum('bctgn,bcsgn->bctsg', cm, bm)
    y_diag = jnp.einsum('bctsg,bctsgh,bcsghp->bctghp', cb, ldec, X)
    din = jnp.exp(cum)
    dout = jnp.exp(cum[:, :, -1:] - cum)
    dchunk = jnp.exp(cum[:, :, -1])

    def step(state, inp):
        cc, bc, xc, di, do, dc = inp
        y = jnp.einsum('btgn,bghpn,btgh->btghp', cc, state, di)
        state = dc[..., None, None] * state + jnp.einsum('bsgn,bsgh,bsghp->bghpn', bc, do, xc)
        return state, y

    s0 = jnp.zeros((bsz, SSM_GROUPS, SSM_HPG, SSM_HEADDIM, SSM_STATE), f32)
    _, y_off = lax.scan(step, s0, (cm.swapaxes(0, 1), bm.swapaxes(0, 1), X.swapaxes(0, 1),
                                   din.swapaxes(0, 1), dout.swapaxes(0, 1), dchunk.swapaxes(0, 1)))
    y = y_diag + y_off.swapaxes(0, 1) + d_skip.astype(f32).reshape(SSM_GROUPS, SSM_HPG)[..., None] * xs
    y = y.reshape(bsz, s, SSM_INNER) * jax.nn.silu(z.astype(f32))
    y = y.reshape(bsz, s, SSM_GROUPS, SSM_NORM_GROUP)
    y = y * lax.rsqrt(jnp.mean(y * y, axis=-1, keepdims=True) + EPS)
    return y.reshape(bsz, s, SSM_INNER) * norm_w.astype(f32)

def memory_cross_attention(q, mem_n, w_mem_kv):
    bsz, s, _ = q.shape
    m = mem_n.shape[1]
    k, v = jnp.split(mem_n @ w_mem_kv, 2, axis=-1)
    q = q.reshape(bsz, s, XA_HEADS, XA_HEADDIM)
    k = k.reshape(bsz, m, XA_HEADS, XA_HEADDIM)
    v = v.reshape(bsz, m, XA_HEADS, XA_HEADDIM)
    scores = jnp.einsum('bshd,bmhd->bhsm', q, k).astype(jnp.float32) * (XA_HEADDIM ** -0.5)
    p = jax.nn.softmax(scores, axis=-1).astype(v.dtype)
    o = jnp.einsum('bhsm,bmhd->bshd', p, v)
    return o.reshape(bsz, s, XA_WIDTH)

def setup_inputs(seed: int = 0) -> dict:
    key = jax.random.key(seed)
    ks = jax.random.split(key, 24)
    f32 = jnp.float32

    def nrm(k, shape, scale):
        return jax.random.normal(k, shape, f32) * scale

    def gain(k, shape):
        return 1.0 + 0.05 * jax.random.normal(k, shape, f32)

    dt0 = jnp.exp(jax.random.uniform(ks[12], (DEPTH, SSM_HEADS), f32)
                  * (np.log(0.1) - np.log(0.001)) + np.log(0.001))
    dt_bias = dt0 + jnp.log(-jnp.expm1(-dt0))
    a_log = jnp.log(jax.random.uniform(ks[13], (DEPTH, SSM_HEADS), f32, 1.0, 16.0))
    return {
        "x": jax.random.normal(ks[0], (BATCH, SEQ, D_MODEL), f32),
        "mem": jax.random.normal(ks[1], (BATCH, N_MEM, D_MODEL), f32),
        "norm_mix_pre": gain(ks[2], (DEPTH, D_MODEL)),
        "norm_mix_post": gain(ks[3], (DEPTH, D_MODEL)),
        "norm_ffn_pre": gain(ks[4], (DEPTH, D_MODEL)),
        "norm_ffn_post": gain(ks[5], (DEPTH, D_MODEL)),
        "norm_mem": gain(ks[6], (DEPTH, D_MODEL)),
        "w_in": nrm(ks[7], (DEPTH, D_MODEL, IN_COLS), D_MODEL ** -0.5),
        "hg_lb_param": 1.0 + 0.1 * jax.random.normal(ks[8], (DEPTH + 1, HG_WIDTH), f32),
        "hg_norm_w": gain(ks[9], (DEPTH, HG_WIDTH)),
        "conv_w": nrm(ks[10], (DEPTH, SSM_CONV, SSM_CONV_DIM), SSM_CONV ** -0.5),
        "conv_b": nrm(ks[11], (DEPTH, SSM_CONV_DIM), 0.02),
        "dt_bias": dt_bias,
        "a_log": a_log,
        "d_skip": 1.0 + 0.1 * jax.random.normal(ks[14], (DEPTH, SSM_HEADS), f32),
        "ssm_norm_w": gain(ks[15], (DEPTH, SSM_INNER)),
        "w_mem_kv": nrm(ks[16], (DEPTH, D_MODEL, 2 * XA_WIDTH), D_MODEL ** -0.5),
        "w_br_hg": nrm(ks[17], (DEPTH, HG_WIDTH, D_MODEL), HG_WIDTH ** -0.5),
        "w_br_ssm": nrm(ks[18], (DEPTH, SSM_INNER, D_MODEL), SSM_INNER ** -0.5),
        "w_br_xa": nrm(ks[19], (DEPTH, XA_WIDTH, D_MODEL), XA_WIDTH ** -0.5),
        "w_out": nrm(ks[20], (DEPTH, D_MODEL, D_MODEL), D_MODEL ** -0.5),
        "w_ffn_up": nrm(ks[21], (DEPTH, D_MODEL, 2 * FFN_HIDDEN), D_MODEL ** -0.5),
        "w_ffn_down": nrm(ks[22], (DEPTH, FFN_HIDDEN, D_MODEL), FFN_HIDDEN ** -0.5),
    }

def reference(x, mem, norm_mix_pre, norm_mix_post, norm_ffn_pre, norm_ffn_post, norm_mem,
              w_in, hg_lb_param, hg_norm_w, conv_w, conv_b, dt_bias, a_log, d_skip,
              ssm_norm_w, w_mem_kv, w_br_hg, w_br_ssm, w_br_xa, w_out, w_ffn_up, w_ffn_down):
    bsz, s, _ = x.shape
    split_pts = list(np.cumsum(IN_SIZES)[:-1])
    lb_all = jnp.cumsum(jax.nn.softmax(hg_lb_param.astype(jnp.float32), axis=0), axis=0)
    for l in range(DEPTH):
        h = rmsnorm(x, norm_mix_pre[l])
        proj = h @ w_in[l]
        (hq, hf, hi, hog, sz, sxbc, sdt, xq, gate_logits) = jnp.split(proj, split_pts, axis=-1)
        y_hg = hgrn2_mixer(hq, hf, hi, hog, lb_all[l], hg_norm_w[l]).astype(x.dtype)
        y_ssm = mamba2_mixer(sz, sxbc, sdt, conv_w[l], conv_b[l], dt_bias[l], a_log[l],
                             d_skip[l], ssm_norm_w[l]).astype(x.dtype)
        mem_n = rmsnorm(mem, norm_mem[l])
        y_xa = memory_cross_attention(xq, mem_n, w_mem_kv[l])
        gates = jax.nn.sigmoid(gate_logits.astype(jnp.float32)).astype(x.dtype)
        gates = gates.reshape(bsz, s, N_BRANCH, D_MODEL)
        merged = (gates[:, :, 0] * (y_hg @ w_br_hg[l])
                  + gates[:, :, 1] * (y_ssm @ w_br_ssm[l])
                  + gates[:, :, 2] * (y_xa @ w_br_xa[l]))
        x = x + rmsnorm(merged @ w_out[l], norm_mix_post[l])
        h = rmsnorm(x, norm_ffn_pre[l])
        g, u = jnp.split(h @ w_ffn_up[l], 2, axis=-1)
        x = x + rmsnorm((jax.nn.silu(g) * u) @ w_ffn_down[l], norm_ffn_post[l])
    return x


_drawn_inputs = setup_inputs


def setup_inputs(seed=0):
    import zlib

    import numpy as np

    out = dict(_drawn_inputs(seed))
    spreads = {}
    factors = {'norm_mem': 8.0,
     'hg_lb_param': 26.547,
     'hg_norm_w': 15.466,
     'conv_b': 16.42,
     'd_skip': 8.0,
     'ssm_norm_w': 8.0}
    for name, (base, spread) in spreads.items():
        noise = np.random.default_rng([zlib.crc32(name.encode()), seed]).standard_normal(out[name].shape)
        drawn = base * np.exp(spread * noise) if base else spread * noise
        out[name] = __import__('jax').numpy.asarray(drawn.astype(out[name].dtype))
    for name, factor in factors.items():
        out[name] = (out[name] * factor).astype(out[name].dtype)
    return out
```

```python
from contextlib import ExitStack

import concourse.bass as bass
from concourse import mybir

ALU = mybir.AluOpType
ACT = mybir.ActivationFunctionType
F32 = mybir.dt.float32
F32R = mybir.dt.float32r
U32 = mybir.dt.uint32

P = 128
KB = 1024
EPS = 1e-6
HG_CHUNK = 32
SSM_CHUNK = 64
GROUPS = 8
XA_HEADS = 4


def hybrid_layer(nc, x, mem, norm_mix_pre, norm_mix_post, norm_ffn_pre, norm_ffn_post, norm_mem,
                 w_in, hg_lb_param, hg_norm_w, conv_w, conv_b, dt_bias, a_log, d_skip,
                 ssm_norm_w, w_mem_kv, w_br_hg, w_br_ssm, w_br_xa, w_out, w_ffn_up, w_ffn_down, out):
    T, D = x.shape[1], x.shape[2]
    NM = mem.shape[1]
    HG = hg_norm_w.shape[1]
    INNER = ssm_norm_w.shape[1]
    CONV = conv_b.shape[1]
    TAPS = conv_w.shape[1]
    H = dt_bias.shape[1]
    FF = w_ffn_down.shape[1]
    KT = D // P
    TT = T // P
    NC = T // SSM_CHUNK
    HC = T // HG_CHUNK
    BC = P // HG_CHUNK
    HPG = H // GROUPS
    HD = INNER // H
    GT = INNER // GROUPS // P
    MT = NM // P
    QT = D // XA_HEADS // P
    FT = FF // P
    SCALE = float(D // XA_HEADS) ** -0.5
    assert T == 512 and D == 1024 and HG == D and HPG * HD == 2 * P and GT == 2 and QT == 2 and MT == 2

    C_Q, C_F, C_I, C_OG = 0, HG, 2 * HG, 3 * HG
    C_Z = 4 * HG
    C_XS = C_Z + INNER
    C_B = C_XS + INNER
    C_C = C_B + GROUPS * P
    C_DT = C_XS + CONV
    C_XQ = C_DT + H
    C_G = C_XQ + D

    with ExitStack() as ctx:
        base = -(-nc.sbuf_base // 32) * 32
        arena = ctx.enter_context(nc.sbuf_tensor("arena", [P, (207 * KB) // 4], F32))

        class Region:
            def __init__(self, start, size):
                self.at, self.end = base + start * KB, base + (start + size) * KB

            def __call__(self, name, shape, dt=F32):
                n = 4
                for s in shape[1:]:
                    n *= s
                t = nc.alloc_sbuf_tensor_at(name, shape, dt, offset=self.at)
                self.at += -(-n // 32) * 32
                assert self.at <= self.end, (name, self.at - self.end)
                return t

        const = Region(0, 13)
        rings = Region(13, 24)
        acts = Region(37, 32)
        ssm_out = Region(69, 32)
        hg_out = Region(101, 16)
        SCR = 117

        ident = const("ident", [P, P])
        ones = const("ones", [P, P])
        hg_mask = const("hg_mask", [P, P])
        cum_mask = const("cum_mask", [P, P])
        after_mask = const("after_mask", [P, P])
        hg_start = const("hg_start", [P, T])
        conv_ch = const("conv_ch", [P, TAPS * CONV // P])
        vec_ch = const("vec_ch", [P, P])
        lb = const("lb", [P, KT])
        one_lb = const("one_lb", [P, KT])
        dskip_ch = const("dskip_ch", [P, INNER // P])
        dt_tok = const("dt_tok", [P, TT, H])
        dta = const("dta", [P, TT, H])
        dout_dt = const("dout_dt", [P, TT, H])
        dchunk = const("dchunk", [P, 2, TT, H])
        eps_col = const("eps_col", [P, 1])
        zero_col = const("zero_col", [P, 1])

        raw = rings("raw", [P, 2, KT, P])
        w_hi = [rings(f"w_hi{s}", [P, KT, P], F32R) for s in range(2)]
        w_lo = [rings(f"w_lo{s}", [P, KT, P], F32R) for s in range(2)]
        h_hi = acts("h_hi", [P, KT, T], F32R)
        h_lo = acts("h_lo", [P, KT, T], F32R)
        y_ssm = ssm_out("y_ssm", [P, INNER // P, T])
        y_hg = hg_out("y_hg", [P, KT, T])

        r = Region(SCR, 90)
        x_tok = r("x_tok", [P, TT, D])
        x_ch = r("x_ch", [P, KT, T])
        sq0 = r("sq0", [P, 2, T])
        rstd0 = r("rstd0", [P, T])
        scaled0 = r("scaled0", [P, 2, T])
        vec_rows = r("vec_rows", [P, P])
        conv_rows = r("conv_rows", [P, P])
        dskip_bc = r("dskip_bc", [P, H])
        dtb_bc = r("dtb_bc", [P, H])
        alog_bc = r("alog_bc", [P, H])
        wdt = r("wdt", [P, KT, H])
        wdt_hi = r("wdt_hi", [P, KT, H], F32R)
        wdt_lo = r("wdt_lo", [P, KT, H], F32R)
        dtx = r("dtx", [P, TT, H])
        dte = r("dte", [P, TT, H])
        dsk_tmp = r("dsk_tmp", [P, KT])

        r = Region(SCR, 90)
        hq = r("hq", [P, T])
        hf = r("hf", [P, T])
        hi_ = r("hi_", [P, T])
        hog = r("hog", [P, T])
        hsig = r("hsig", [P, T])
        hk = r("hk", [P, T])
        hb = r("hb", [P, T])
        hd = r("hd", [P, T])
        hd2 = hsig
        e_q = r("e_q", [P, T])
        e_k = r("e_k", [P, T])
        e_i = r("e_i", [P, T])
        e_l = r("e_l", [P, T])
        hdc = r("hdc", [P, HC])
        v_tok = r("v_tok", [P, TT, P])
        v_blk = r("v_blk", [P, 2, BC, P])
        ki_tok = r("ki_tok", [P, TT, P])
        hgA = r("hgA", [P, TT, P])
        hgS = r("hgS", [P, HC, P])
        ho = e_q
        zs = r("zs", [P, GT, T])
        zsig = hd
        xpad = r("xpad", [P, 516])
        cv = r("cv", [P, 4, T])
        csig = r("csig", [P, T])
        xdt = r("xdt", [P, GT, TT, P])
        xdo = r("xdo", [P, GT, TT, P])
        b_tok = r("b_tok", [P, TT, P])
        cbm = r("cbm", [P, TT, P])
        udta = r("udta", [P, HPG, P])
        ldec = r("ldec", [P, 2, HPG, P])
        smS = r("smS", [P, NC, HPG * HD])
        smT = csig[:, 0:HPG * HD]
        dta_rep = xdo[:].rearrange("p c t d -> p (c t d)").rearrange("p (t d) -> p t d", d=HPG * HD)
        din = r("din", [P, GT, T])
        sy = xdt[:].rearrange("p c t d -> p c (t d)")
        ssq = csig
        srs = zsig
        g_dta = r("g_dta", [P, TT, HPG])
        g_dt = r("g_dt", [P, TT, HPG])
        g_do = r("g_do", [P, TT, HPG])
        g_dc = r("g_dc", [P, 2, TT, HPG])

        r = Region(SCR, 90)
        xa_hi = r("xa_hi", [P, KT, T], F32R)
        xa_lo = r("xa_lo", [P, KT, T], F32R)
        m_hi = r("m_hi", [P, KT, NM], F32R)
        m_lo = r("m_lo", [P, KT, NM], F32R)
        mark = r.at
        m_tok = r("m_tok", [P, MT, D])
        m_sq = r("m_sq", [P, 2, NM])
        m_rstd = r("m_rstd", [P, NM])
        m_ch = r("m_ch", [P, KT, NM])
        r.at = mark
        q_sb = r("q_sb", [P, QT, T])
        k_sb = r("k_sb", [P, QT, NM])
        v_sb = r("v_sb", [P, QT, NM])
        v_mt = r("v_mt", [P, MT, QT * P])
        prob = r("prob", [P, 2, NM])
        pT = r("pT", [P, MT, T])
        xo = r("xo", [P, T])
        st_max = r("st_max", [P, 2])
        st_sum = r("st_sum", [P, 2])
        st_inv = r("st_inv", [P, 2])
        r = Region(SCR + 32, 58)
        hg_hi = r("hg_hi", [P, KT, T], F32R)
        hg_lo = r("hg_lo", [P, KT, T], F32R)
        merged = r("merged", [P, KT, T])
        gate = r("gate", [P, 2, T])
        part = r("part", [P, 2, T])
        r = Region(SCR, 64)
        sm_hi = r("sm_hi", [P, INNER // P, T], F32R)
        sm_lo = r("sm_lo", [P, INNER // P, T], F32R)
        r = Region(69, 32)
        mg_hi = r("mg_hi", [P, KT, T], F32R)
        mg_lo = r("mg_lo", [P, KT, T], F32R)
        x2 = nc.alloc_sbuf_tensor_at("x2", [P, KT, T], F32, offset=base + 101 * KB)
        r = Region(SCR, 64)
        x_tok2 = r("x_tok2", [P, TT, D])
        wo = r("wo", [P, KT, T])
        nsq = r("nsq", [P, 2, T])
        nrs = r("nrs", [P, T])
        nsc = r("nsc", [P, 2, T])
        nsq2 = r("nsq2", [P, 2, T])
        nrs2 = r("nrs2", [P, T])
        r = Region(SCR, 90)
        a_hi = r("a_hi", [P, FT, T], F32R)
        a_lo = r("a_lo", [P, FT, T], F32R)
        fo = nc.alloc_sbuf_tensor_at("fo", [P, KT, T], F32, offset=base + 69 * KB)
        r = Region(85, 16)
        up_sig = r("up_sig", [P, T])
        up_a = r("up_a", [P, T])
        fsq = r("fsq", [P, 2, T])
        frs = r("frs", [P, T])
        fsc = r("fsc", [P, 2, T])
        o_tok = nc.alloc_sbuf_tensor_at("o_tok", [P, TT, D], F32, offset=base + 37 * KB)

        bank = [ctx.enter_context(nc.psum_tensor(f"bank{b}", [P, 512], F32)) for b in range(8)]

        def tiles(b, n=TT):
            return bank[b][:, 0:n * P].rearrange("p (t c) -> p t c", c=P)

        sems = {}

        def sem(name):
            if name not in sems:
                sems[name] = ctx.enter_context(nc.semaphore(name))
            return sems[name]

        def wait_alone(eng, s, value):
            eng.wait_ge(s, value)
            eng.sem_inc(sem("waits_passed"), 1)

        class Chain:

            def __init__(self, eng, name):
                self.eng, self.sem, self.n = eng, sem(name), 0

            def restart(self):
                if self.n:
                    self.settle()
                    self.eng.sem_clear(self.sem)
                self.n = 0

            def did(self, ins):
                ins.then_inc(self.sem, 1)
                self.n += 1

            def settle(self):
                self.eng.wait_ge(self.sem, self.n)

            def step(self, ins):
                self.did(ins)
                self.settle()

        def rows(w):
            return w[0].rearrange("(k p) n -> p k n", p=P)

        win_v, kv_v = rows(w_in), rows(w_mem_kv)
        bhg_v, bssm_v, bxa_v = rows(w_br_hg), rows(w_br_ssm), rows(w_br_xa)
        wo_v, up_v, down_v = rows(w_out), rows(w_ffn_up), rows(w_ffn_down)

        hg_slabs = [(win_v, C_Q, P), (win_v, C_F, P), (win_v, C_I, P), (win_v, C_OG, P)]
        ssm_slabs = [(win_v, C_Z, 2 * P), (win_v, C_Z + P, 2 * P), (win_v, C_XS, 2 * P),
                     (win_v, C_XS + P, 2 * P), (win_v, C_B, P), (win_v, C_C, P)]

        def slab(w, start, stride, k0=0, k1=KT, shift=0):
            return (w, start, stride, k0, k1, shift)

        SECTIONS = [
            ("hg0", 1, [slab(*s) for s in hg_slabs]),
            ("mix", GROUPS - 1, [slab(*s) for s in ssm_slabs] + [slab(*s, shift=1) for s in hg_slabs]),
            ("mix_last", 1, [slab(*s, shift=GROUPS - 1) for s in ssm_slabs]),
            ("xa", XA_HEADS, [slab(win_v, C_XQ + c * P, QT * P) for c in range(QT)]
             + [slab(kv_v, c * P, QT * P) for c in range(QT)]
             + [slab(kv_v, D + c * P, QT * P) for c in range(QT)]),
            ("merge1", KT, [slab(win_v, C_G, P), slab(bhg_v, 0, P),
                            slab(win_v, C_G + 2 * D, P), slab(bxa_v, 0, P)]),
            ("merge2", KT // 2, [slab(w, s + c * P, 2 * P, *k) for c in range(2) for w, s, k in
                                 ((win_v, C_G + D, ()), (bssm_v, 0, (0, KT)), (bssm_v, 0, (KT, 2 * KT)))]),
            ("wout", KT // 2, [slab(wo_v, c * P, 2 * P) for c in range(2)]),
            ("up", FT, [slab(up_v, 0, P), slab(up_v, FF, P)]),
            ("down", KT // 2, [slab(down_v, c * P, 2 * P, k, min(k + KT, FT))
                               for c in range(2) for k in range(0, FT, KT)]),
        ]
        first, n = {}, 0
        for name, its, slabs in SECTIONS:
            assert n % 2 == 0 and len(slabs) % 2 == 0
            first[name] = n
            n += its * len(slabs)
        size = {name: len(slabs) for name, _, slabs in SECTIONS}
        tiles_of = {name: len(slabs) for name, _, slabs in SECTIONS} | {"merge2": 4, "down": 2}
        first_tile, n = {}, 0
        for name, its, _ in SECTIONS:
            first_tile[name] = n
            n += its * tiles_of[name]

        def slab_count(name, i, k):
            return first[name] // 2 + i * (size[name] // 2) + k // 2 + 1

        def tile_count(name, i, t):
            return first_tile[name] // 2 + i * (tiles_of[name] // 2) + t // 2 + 1

        raw_full = [sem(f"raw_full{s}") for s in range(2)]
        split_full = [sem(f"split_full{s}") for s in range(2)]
        slab_done = [sem(f"slab_done{s}") for s in range(2)]
        bank_free = [sem(f"bank_free{s}") for s in range(2)]

        def loop(eng, name, body, chain=None):
            its = next(s[1] for s in SECTIONS if s[0] == name)
            if chain:
                chain.restart()
            if its == 1:
                body(0)
            else:
                with eng.Fori(0, its) as i:
                    body(i)
                    if chain:
                        chain.restart()

        block = ctx.enter_context(nc.Block())

        x_v = x[0].rearrange("(t p) d -> p t d", p=P)
        mem_v = mem[0].rearrange("(t p) d -> p t d", p=P)
        out_v = out[0].rearrange("(t p) d -> p t d", p=P)
        V, n = {}, 0
        for name, ap in (("pre", norm_mix_pre[0]), ("post", norm_mix_post[0]), ("fpre", norm_ffn_pre[0]),
                         ("fpost", norm_ffn_post[0]), ("mem", norm_mem[0]), ("lb0", hg_lb_param[0]),
                         ("lb1", hg_lb_param[1]), ("hg", hg_norm_w[0]), ("cb", conv_b[0]),
                         ("ssm", ssm_norm_w[0])):
            V[name] = (n, ap.shape[0] // P, ap)
            n += ap.shape[0] // P
        VR = n
        assert VR <= P and TAPS * CONV // P == P

        def vcol(name, c):
            return vec_ch[:, bass.ds(V[name][0] + c, 1)]

        @block.sync
        def _(sp):
            for s in range(2):
                sp.sem_inc(bank_free[s], 1)
            sp.dma_start(x_tok[:], x_v).then_inc(sem("x_in"), 16)

            def load(name, i, k):
                w, start, stride, k0, k1, shift = next(s[2] for s in SECTIONS if s[0] == name)[k]
                c = start + stride * (i + shift)
                if not (name == "hg0" and k < 2):
                    wait_alone(sp, split_full[k % 2], slab_count(name, i, k) - 1)
                sp.dma_start(raw[:, k % 2, 0:k1 - k0, :], w[:, k0:k1, bass.ds(c, P)])\
                  .then_inc(raw_full[k % 2], 16)

            for name in ("hg0", "mix", "mix_last"):
                loop(sp, name, lambda i: [load(name, i, k) for k in range(size[name])])
            sp.wait_ge(sem("sm_done"), GROUPS + 1)
            sp.wait_ge(slab_done[1], first["xa"] // 2)
            sp.dma_start(m_tok[:], mem_v).then_inc(sem("mem_in"), 16)
            for name in ("xa", "merge1", "merge2"):
                loop(sp, name, lambda i: [load(name, i, k) for k in range(size[name])])
            sp.wait_ge(slab_done[1], first["wout"] // 2)
            sp.dma_start(x_tok2[:], x_v).then_inc(sem("x_again"), 16)
            for name in ("wout", "up", "down"):
                loop(sp, name, lambda i: [load(name, i, k) for k in range(size[name])])
            for t in range(TT):
                sp.wait_ge(sem("o_copied"), 2 * t + 2)
                sp.dma_start(out_v[:, t, :], o_tok[:, t, :]).then_inc(sem("stored"), 16)
            sp.wait_ge(sem("stored"), 16 * TT)

        @block.gpsimd
        def _(pool):
            g = nc.gpsimd
            ch = Chain(pool, "pool_chain")
            ch.did(g.memset(ident[:], 0.0))
            ch.did(g.memset(ones[:], 1.0))
            ch.did(g.memset(eps_col[:], EPS))
            ch.did(g.memset(zero_col[:], 0.0))
            for m in (hg_mask, cum_mask, after_mask):
                ch.did(g.memset(m[:], 1.0))
            ch.did(g.memset(hg_start[:], 1.0))
            ch.settle()
            ch.did(g.affine_select(out=ident[:], in_=ident[:], compare_op=ALU.not_equal, fill=1.0,
                                   base=0, pattern=[[-1, P]], channel_multiplier=1))

            def same_chunk(m, n):
                v = m[:].rearrange("p (b c) -> p b c", c=n)
                ch.settle()
                ch.step(g.affine_select(out=v, in_=v, compare_op=ALU.is_ge, fill=0.0, base=0,
                                        pattern=[[-n, P // n], [0, n]], channel_multiplier=1))
                ch.step(g.affine_select(out=v, in_=v, compare_op=ALU.is_ge, fill=0.0, base=n - 1,
                                        pattern=[[n, P // n], [0, n]], channel_multiplier=-1))

            same_chunk(hg_mask, HG_CHUNK)
            same_chunk(cum_mask, SSM_CHUNK)
            same_chunk(after_mask, SSM_CHUNK)
            for m in (hg_mask, cum_mask):
                ch.did(g.affine_select(out=m[:], in_=m[:], compare_op=ALU.is_ge, fill=0.0, base=0,
                                       pattern=[[1, P]], channel_multiplier=-1))
            ch.did(g.affine_select(out=after_mask[:], in_=after_mask[:], compare_op=ALU.is_ge, fill=0.0,
                                   base=-1, pattern=[[-1, P]], channel_multiplier=1))
            v = hg_start[:].rearrange("p (b c) -> p b c", c=HG_CHUNK)
            g.affine_select(out=v, in_=v, compare_op=ALU.is_ge, fill=0.0, base=-1,
                            pattern=[[0, HC], [1, HG_CHUNK]], channel_multiplier=0).then_inc(sem("consts"), 1)

            def split(name, i, k):
                ks = next(s[2] for s in SECTIONS if s[0] == name)[k]
                n, s = ks[4] - ks[3], k % 2
                src = raw[:, s, 0:n, :]
                pool.wait_ge(raw_full[s], 16 * slab_count(name, i, k))
                if not (name == "hg0" and k < 2):
                    pool.wait_ge(slab_done[s], slab_count(name, i, k) - 1)
                ch.step(g.tensor_tensor(w_hi[s][:, 0:n, :], src,
                                        zero_col[:].unsqueeze(2).to_broadcast([P, n, P]), ALU.add))
                g.tensor_tensor(w_lo[s][:, 0:n, :], src, w_hi[s][:, 0:n, :].bitcast(F32), ALU.subtract)\
                 .then_inc(split_full[s], 1)

            def section(name):
                def body(i):
                    for k in range(size[name]):
                        split(name, i, k)
                loop(pool, name, body, ch)

            for name, _, _ in SECTIONS:
                section(name)

        @block.tensor
        def _(pe):
            mm = nc.tensor.matmul

            def gemm_slab(name, i, k, t, rhs_hi, rhs_lo, k_first, k_last, N=T):
                ks = next(s[2] for s in SECTIONS if s[0] == name)[k]
                s, b = k % 2, t % 2
                pe.wait_ge(split_full[s], slab_count(name, i, k))
                if k_first:
                    pe.wait_ge(bank_free[b], tile_count(name, i, t))
                k0, n = ks[3], ks[4] - ks[3]
                for kk in range(n):
                    for w, r in ((w_hi, rhs_hi), (w_hi, rhs_lo), (w_lo, rhs_hi)):
                        last = mm(bank[b][:, 0:N], w[s][:, kk, :], r[:, k0 + kk, :],
                                  start=(k_first and kk == 0 and w is w_hi and r is rhs_hi),
                                  stop=(k_last and kk == n - 1 and w is w_lo))
                last.then_inc(slab_done[s], 1)

            def one(name, i, k, hi=h_hi, lo=h_lo, N=T):
                gemm_slab(name, i, k, k, hi, lo, True, True, N)

            pe.wait_ge(sem("consts"), 1)
            pe.wait_ge(sem("vecs_in"), 16 * (1 + len(V)))
            nc.tensor.transpose(bank[2][:, 0:P], conv_rows[:], ident[:])
            nc.tensor.transpose(bank[2][:, P:2 * P], vec_rows[:], ident[:]).then_inc(sem("vecs_T"), 1)
            pe.wait_ge(sem("x_in"), 16)
            for k in range(KT):
                b = 3 + k % 2
                if k >= 2:
                    pe.wait_ge(sem("x_T_read"), k - 1)
                for t in range(TT):
                    last = nc.tensor.transpose(bank[b][:, t * P:(t + 1) * P],
                                               x_tok[:, t, k * P:(k + 1) * P], ident[:])
                last.then_inc(sem("x_T"), 1)
            for k in range(KT):
                pe.wait_ge(sem("x_sq"), k + 1)
                mm(bank[5][:], ones[:], sq0[:, k % 2, :], start=(k == 0), stop=(k == KT - 1))\
                    .then_inc(sem("x_ss"), 1)
            pe.wait_ge(sem("h_ready"), 1)
            for t in range(TT):
                for kk in range(KT):
                    for l, w in ((h_hi, wdt_hi), (h_lo, wdt_hi), (h_hi, wdt_lo)):
                        last = mm(bank[6][:, t * H:(t + 1) * H], l[:, kk, t * P:(t + 1) * P], w[:, kk, :],
                                  start=(kk == 0 and l is h_hi and w is wdt_hi),
                                  stop=(kk == KT - 1 and w is wdt_lo))
            last.then_inc(sem("dt_mm"), 1)
            pe.wait_ge(sem("dta_ready"), 1)
            dta_f = dta[:].rearrange("p t h -> p (t h)")
            mm(bank[6][:, 0:TT * H], after_mask[:], dta_f, start=True, stop=True).then_inc(sem("dt_mm"), 1)
            mm(bank[7][:, 0:TT * H], ones[0:64, :], dta[0:64].rearrange("p t h -> p (t h)"),
               start=True, stop=True)
            pe.wait_ge(sem("x_T_read"), KT)
            mm(bank[4][:, 0:TT * H], ones[64:128, :], dta[64:128].rearrange("p t h -> p (t h)"),
               start=True, stop=True).then_inc(sem("dt_mm"), 1)
            for k in range(4):
                one("hg0", 0, k)

            def hg_transposes(i):
                pe.wait_ge(sem("hg_pre"), i + 1)
                for t in range(TT):
                    nc.tensor.transpose(bank[2][:, t * P:(t + 1) * P], hi_[:, t * P:(t + 1) * P], ident[:])
                for t in range(TT):
                    last = nc.tensor.transpose(bank[3][:, t * P:(t + 1) * P],
                                               e_l[:, t * P:(t + 1) * P], ident[:])
                last.then_inc(sem("hg_T"), 1)

            def hg_scores(i):
                pe.wait_ge(sem("hg_tok"), i + 1)
                for t in range(TT):
                    c = slice(t * P, (t + 1) * P)
                    last = mm(bank[2][:, c], e_k[:, c], e_q[:, c], start=True, stop=True)
                last.then_inc(sem("hg_A"), 1)

            def hg_kv(i, t):
                pe.wait_ge(sem("hg_vblk"), 4 * i + t + 1)
                if t == 1:
                    pe.wait_ge(sem("hg_masked"), i + 1)
                if t >= 2:
                    pe.wait_ge(sem("hg_state"), 4 * i + t - 1)
                mm(bank[3 - t % 2][:], ki_tok[:, t, :], v_blk[:, t % 2].rearrange("p c v -> p (c v)"),
                   start=True, stop=True).then_inc(sem("hg_kv"), 1)

            def hg_out_mm(i):
                pe.wait_ge(sem("hg_state"), 4 * i + 4)
                for t in range(TT):
                    c0 = t * P
                    mm(bank[3][:, c0:c0 + P], v_tok[:, t, :], hgA[:, t, :], start=True, stop=False)
                    for c in range(BC):
                        a = c0 + c * HG_CHUNK
                        last = mm(bank[3][:, a:a + HG_CHUNK], hgS[:, t * BC + c, :], e_i[:, a:a + HG_CHUNK],
                                  start=False, stop=(c == BC - 1))
                last.then_inc(sem("hg_o"), 1)

            def hg_norm(i):
                pe.wait_ge(sem("hg_osq"), i + 1)
                mm(bank[2][:], ones[:], hsig[:], start=True, stop=True).then_inc(sem("hg_n"), 1)

            def sm_transposes(i):
                pe.wait_ge(sem("sm_conv"), i + 1)
                pe.wait_ge(sem("sm_done"), i + 1)
                for c in range(GT):
                    for t in range(TT):
                        nc.tensor.transpose(bank[4 + c][:, t * P:(t + 1) * P],
                                            cv[:, c, t * P:(t + 1) * P], ident[:])
                for t in range(TT):
                    last = nc.tensor.transpose(bank[6][:, t * P:(t + 1) * P],
                                               cv[:, 2, t * P:(t + 1) * P], ident[:])
                last.then_inc(sem("sm_T"), 1)
                for t in range(TT):
                    c = slice(t * P, (t + 1) * P)
                    last = mm(bank[7][:, c], cv[:, 2, c], cv[:, 3, c], start=True, stop=True)
                last.then_inc(sem("sm_cb"), 1)

            def sm_din(i):
                pe.wait_ge(sem("sm_btok"), i + 1)
                pe.wait_ge(sem("sm_masked"), i + 1)
                for c in range(GT):
                    for t in range(TT):
                        last = mm(bank[6 + c][:, t * P:(t + 1) * P], dta_rep[:, t, c * P:(c + 1) * P],
                                  cum_mask[:], start=True, stop=True)
                last.then_inc(sem("sm_cum"), 1)

            def sm_seg(i, t):
                pe.wait_ge(sem("sm_udta"), 4 * i + t + 1)
                if t < 2:
                    pe.wait_ge(sem("sm_din"), i + 1)
                else:
                    pe.wait_ge(sem("sm_ldec"), 4 * i + t - 1)
                mm(bank[6 + t % 2][:], after_mask[:], udta[:].rearrange("p h t -> p (h t)"),
                   start=True, stop=True).then_inc(sem("sm_seg"), 1)

            def sm_diag(i, t):
                pe.wait_ge(sem("sm_M"), 4 * i + t + 1)
                for h in range(HPG):
                    c, o = h // 2, (h % 2) * HD
                    last = mm(bank[4 + c][o:o + HD, t * P:(t + 1) * P], xdt[:, c, t, o:o + HD],
                              ldec[:, t % 2, h, :], start=True, stop=True)
                last.then_inc(sem("sm_yd"), 1)

            def sm_kv(i, half):
                if half == 0:
                    pe.wait_ge(sem("sm_ldec"), 4 * i + 4)
                else:
                    pe.wait_ge(sem("sm_state"), 2 * i + 1)
                for c in range(4 * half, 4 * half + 4 - half):
                    p = 64 * (c % 2)
                    q = (c // 2) % 2 * HPG * HD
                    last = mm(bank[6 + c % 2][:, q:q + HPG * HD], b_tok[p:p + 64, c // 2, :],
                              xdo[p:p + 64, :, c // 2, :], start=True, stop=True)
                last.then_inc(sem("sm_kv"), 1)

            def sm_off(i):
                pe.wait_ge(sem("sm_state"), 2 * i + 2)
                for c in range(GT):
                    for k in range(NC):
                        a = k * SSM_CHUNK
                        last = mm(bank[6 + c][:, a:a + SSM_CHUNK], smS[:, k, c * P:(c + 1) * P],
                                  cv[:, 3, a:a + SSM_CHUNK], start=True, stop=True)
                last.then_inc(sem("sm_yo"), 1)

            def sm_norm(i):
                for c in range(GT):
                    pe.wait_ge(sem("sm_sq"), 2 * i + c + 1)
                    mm(bank[6][:], ones[:], ssq[:] if c == 0 else din[:, 0, :], start=(c == 0), stop=(c == 1))\
                        .then_inc(sem("sm_n"), 1)

            def mix(name, j, i, nxt):
                one(name, j, 0)
                one(name, j, 1)
                hg_transposes(i)
                one(name, j, 2)
                hg_scores(i)
                hg_kv(i, 0)
                hg_kv(i, 1)
                one(name, j, 3)
                hg_kv(i, 2)
                hg_kv(i, 3)
                one(name, j, 4)
                hg_out_mm(i)
                one(name, j, 5)
                hg_norm(i)
                sm_transposes(i)
                if nxt:
                    one(name, j, 6)
                sm_din(i)
                sm_seg(i, 0)
                sm_seg(i, 1)
                if nxt:
                    one(name, j, 7)
                sm_diag(i, 0)
                sm_diag(i, 1)
                sm_seg(i, 2)
                sm_seg(i, 3)
                if nxt:
                    one(name, j, 8)
                sm_diag(i, 2)
                sm_diag(i, 3)
                sm_kv(i, 0)
                if nxt:
                    one(name, j, 9)
                sm_kv(i, 1)
                sm_off(i)
                sm_norm(i)

            loop(pe, "mix", lambda j: mix("mix", j, j, True))
            mix("mix_last", 0, GROUPS - 1, False)

            pe.wait_ge(sem("mem_in"), 16)
            for k in range(KT):
                b = 2 + k % 2
                if k >= 2:
                    pe.wait_ge(sem("m_T_read"), k - 1)
                for t in range(MT):
                    last = nc.tensor.transpose(bank[b][:, t * P:(t + 1) * P],
                                               m_tok[:, t, k * P:(k + 1) * P], ident[:])
                last.then_inc(sem("m_T"), 1)
            for k in range(KT):
                pe.wait_ge(sem("m_sq"), k + 1)
                mm(bank[4][:, 0:NM], ones[:], m_sq[:, k % 2, :], start=(k == 0), stop=(k == KT - 1))\
                    .then_inc(sem("m_ss"), 1)
            pe.wait_ge(sem("m_ready"), 1)

            def attend(h):
                for c in range(QT):
                    one("xa", h, c)
                for c in range(2 * QT):
                    one("xa", h, QT + c, m_hi, m_lo, NM)
                pe.wait_ge(bank_free[1], tile_count("xa", h, 5) + 1)
                for c in range(QT):
                    for t in range(MT):
                        last = nc.tensor.transpose(bank[2][:, (t * QT + c) * P:(t * QT + c + 1) * P],
                                                   v_sb[:, c, t * P:(t + 1) * P], ident[:])
                last.then_inc(sem("xa_vT"), 1)
                for t in range(TT):
                    if t >= 2:
                        pe.wait_ge(sem("xa_exp"), 4 * h + t - 1)
                    for c in range(QT):
                        last = mm(bank[4 + t % 2][:, 0:NM], q_sb[:, c, t * P:(t + 1) * P], k_sb[:, c, :],
                                  start=(c == 0), stop=(c == QT - 1))
                    last.then_inc(sem("xa_s"), 1)
                    if t >= 1:
                        probs_T(h, t - 1)
                probs_T(h, TT - 1)
                pe.wait_ge(sem("xa_p"), 4 * h + 4)
                for c in range(QT):
                    for m in range(MT):
                        last = mm(bank[2 + c][:], v_mt[:, m, c * P:(c + 1) * P], pT[:, m, :],
                                  start=(m == 0), stop=(m == MT - 1))
                    last.then_inc(sem("xa_o"), 1)

            def probs_T(h, t):
                pe.wait_ge(sem("xa_norm"), 4 * h + t + 1)
                if t >= 2:
                    pe.wait_ge(sem("xa_p"), 4 * h + t - 1)
                for m in range(MT):
                    last = nc.tensor.transpose(bank[6 + t % 2][:, m * P:(m + 1) * P],
                                               prob[:, t % 2, m * P:(m + 1) * P], ident[:])
                last.then_inc(sem("xa_pT"), 1)

            loop(pe, "xa", attend)

            pe.wait_ge(sem("hg_split"), 1)

            def merge1(i):
                one("merge1", i, 0)
                one("merge1", i, 1, hg_hi, hg_lo)
                one("merge1", i, 2)
                one("merge1", i, 3, xa_hi, xa_lo)

            loop(pe, "merge1", merge1)
            pe.wait_ge(sem("sm_split"), 1)

            def merge2(i):
                for c in range(2):
                    gemm_slab("merge2", i, 3 * c, 2 * c, h_hi, h_lo, True, True)
                    gemm_slab("merge2", i, 3 * c + 1, 2 * c + 1, sm_hi, sm_lo, True, False)
                    gemm_slab("merge2", i, 3 * c + 2, 2 * c + 1, sm_hi, sm_lo, False, True)

            loop(pe, "merge2", merge2)

            pe.wait_ge(sem("merged_split"), 1)
            loop(pe, "wout", lambda i: [one("wout", i, c, mg_hi, mg_lo) for c in range(2)])

            def square_sum(b, sq, squares, sums):
                for k in range(KT):
                    pe.wait_ge(sem(squares), k + 1)
                    mm(bank[b][:], ones[:], sq[:, k % 2, :], start=(k == 0), stop=(k == KT - 1))\
                        .then_inc(sem(sums), 1)

            pe.wait_ge(sem("x_again"), 16)
            for k in range(KT):
                b = 4 + k % 2
                if k >= 2:
                    pe.wait_ge(sem("x2_read"), k - 1)
                for t in range(TT):
                    last = nc.tensor.transpose(bank[b][:, t * P:(t + 1) * P],
                                               x_tok2[:, t, k * P:(k + 1) * P], ident[:])
                last.then_inc(sem("x2_T"), 1)
            square_sum(2, nsq, "wo_sq", "wo_ss")
            square_sum(3, nsq2, "x2_sq", "x2_ss")
            pe.wait_ge(sem("h2_ready"), 1)
            loop(pe, "up", lambda i: [one("up", i, c) for c in range(2)])
            pe.wait_ge(sem("act_ready"), FT + 1)

            def down(i):
                n = size["down"] // 2
                for c in range(2):
                    for k in range(n):
                        gemm_slab("down", i, n * c + k, c, a_hi, a_lo, k == 0, k == n - 1)

            loop(pe, "down", down)
            square_sum(2, fsq, "fo_sq", "fo_ss")
            for t in range(TT):
                for half in range(2):
                    pe.wait_ge(sem("y_ready"), KT)
                    b = 4 + (2 * t + half) % 4
                    if 2 * t + half >= 4:
                        pe.wait_ge(sem("o_copied"), 2 * t + half - 3)
                    for k in range(4):
                        last = nc.tensor.transpose(bank[b][:, k * P:(k + 1) * P],
                                                   x2[:, 4 * half + k, t * P:(t + 1) * P], ident[:])
                    last.then_inc(sem("o_T"), 1)

        @block.scalar
        def _(act):
            f = nc.scalar.activation
            ch = Chain(act, "act_chain")
            act.dma_start(conv_rows[:], conv_w[0].rearrange("k (c p) -> (k c) p", p=P)).then_inc(sem("vecs_in"), 16)
            act.wait_ge(sem("vec_zero"), 1)
            for at, n, ap in V.values():
                act.dma_start(vec_rows[at:at + n, :], ap.rearrange("(c p) -> c p", p=P)).then_inc(sem("vecs_in"), 16)
            act.dma_start(dtb_bc[:], dt_bias.to_broadcast([P, H])).then_inc(sem("dtv_in"), 16)
            act.dma_start(alog_bc[:], a_log.to_broadcast([P, H])).then_inc(sem("dtv_in"), 16)
            act.dma_start(dskip_bc[:], d_skip.to_broadcast([P, H])).then_inc(sem("dtv_in"), 16)
            act.dma_start(wdt[:], win_v[:, :, C_DT:C_DT + H]).then_inc(sem("wdt_in"), 16)

            def rstd(dst, src, n):
                ch.step(f(dst, src, ACT.Ln, scale=1.0 / n, bias=eps_col[:]))
                return f(dst, dst, ACT.Exp, scale=-0.5)

            act.wait_ge(sem("consts"), 1)
            act.wait_ge(sem("dtv_in"), 48)
            ch.step(f(alog_bc[:], alog_bc[:], ACT.Exp))
            for k in range(KT):
                act.wait_ge(sem("x_T_read"), k + 1)
                if k >= 2:
                    act.wait_ge(sem("x_ss"), k - 1)
                f(sq0[:, k % 2, :], x_ch[:, k, :], ACT.Square).then_inc(sem("x_sq"), 1)
            act.wait_ge(sem("x_ss"), KT)
            rstd(rstd0[:], bank[5][:], D).then_inc(sem("x_rstd"), 1)
            act.wait_ge(sem("lb_diff"), 1)
            f(dsk_tmp[:], dsk_tmp[:], ACT.Exp).then_inc(sem("lb_exp"), 1)
            act.wait_ge(sem("dt_abs"), 1)
            ch.step(f(dte[:], dte[:], ACT.Exp, scale=-1.0))
            f(dte[:], dte[:], ACT.Ln, bias=ones[:, 0:1]).then_inc(sem("dt_ln"), 1)
            act.wait_ge(sem("dt_mm"), 2)
            f(dout_dt[:].rearrange("p t h -> p (t h)"), bank[6][:, 0:TT * H], ACT.Exp)\
                .then_inc(sem("dout_exp"), 1)
            act.wait_ge(sem("dt_mm"), 3)
            ch.did(f(dchunk[:, 0].rearrange("p t h -> p (t h)"), bank[7][:, 0:TT * H], ACT.Exp))
            f(dchunk[:, 1].rearrange("p t h -> p (t h)"), bank[4][:, 0:TT * H], ACT.Exp)\
                .then_inc(sem("dchunk_exp"), 1)

            def read_tile(name, i, k, dst, N=T, before=None):
                if before:
                    act.wait_ge(*before)
                act.wait_ge(slab_done[k % 2], slab_count(name, i, k))
                f(dst, bank[k % 2][:, 0:N], ACT.Copy).then_inc(bank_free[k % 2], 1)

            hg_dst = (hq, hf, hi_, hog)

            def hg_sigmoids(u):
                for k, (src, name) in enumerate(((hf, "hg_sf"), (hq, "hg_sq"), (hog, "hg_sog"))):
                    if k:
                        act.wait_ge(sem("hg_sig_used"), 3 * u + k)
                    f(hsig[:], src[:], ACT.Sigmoid).then_inc(sem("hg_sig"), 1)

            def hg_exps(i):
                act.wait_ge(sem("hg_f"), i + 1)
                f(hf[:], hf[:], ACT.Ln).then_inc(sem("hg_g"), 1)
                act.wait_ge(sem("hg_b"), i + 1)
                ch.did(f(e_i[:], hb[:], ACT.Exp))
                ch.did(f(e_q[:], hd[:], ACT.Exp))
                ch.did(f(e_k[:], hd[:], ACT.Exp, scale=-1.0))
                f(e_l[:], hd2[:], ACT.Exp).then_inc(sem("hg_e"), 1)

            act.wait_ge(sem("start_done"), 1)
            for k in range(4):
                read_tile("hg0", 0, k, hg_dst[k][:])
            ch.settle()
            act.wait_ge(bank_free[1], tile_count("hg0", 0, 3) + 1)
            hg_sigmoids(0)

            def v_by_chunk(i, t):
                for c in range(BC):
                    p = c * HG_CHUNK
                    last = f(v_blk[p:p + HG_CHUNK, t % 2, c, :], v_tok[p:p + HG_CHUNK, t, :], ACT.Copy)
                    if c < BC - 1:
                        ch.did(last)
                last.then_inc(sem("hg_vblk"), 1)

            def mix(name, j, i, nxt):
                hg_exps(i)
                for k in range(2):
                    act.wait_ge(slab_done[k], slab_count(name, j, k))
                    if k == 0:
                        act.wait_ge(sem("hg_e"), i + 1)
                        act.wait_ge(sem("sm_done"), i + 1)
                    else:
                        act.wait_ge(bank_free[0], tile_count(name, j, 0) + 1)
                    f(zsig[:], bank[k][:], ACT.Sigmoid).then_inc(sem("sm_zsig"), 1)

                def conv_in(k):
                    before = (sem("sm_cv"), 4 * i + k) if k else None
                    read_tile(name, j, 2 + k, xpad[:, 3:3 + T], before=before)

                def conv_sig(k):
                    act.wait_ge(sem("sm_cv"), 4 * i + k + 1)
                    if k:
                        act.wait_ge(sem("sm_cx"), 3 * i + k)
                    f(csig[:], cv[:, k, :], ACT.Sigmoid).then_inc(sem("sm_csig"), 1)

                conv_in(0)
                act.wait_ge(sem("hg_T"), i + 1)
                ch.did(f(v_tok[:].rearrange("p t c -> p (t c)"), bank[2][:], ACT.Copy))
                f(ki_tok[:].rearrange("p t c -> p (t c)"), bank[3][:], ACT.Copy).then_inc(sem("hg_tok"), 1)
                act.wait_ge(sem("hg_tok"), i + 1)
                v_by_chunk(i, 0)
                v_by_chunk(i, 1)
                conv_sig(0)
                conv_in(1)
                act.wait_ge(sem("hg_kv"), 4 * i + 1)
                v_by_chunk(i, 2)
                act.wait_ge(sem("hg_kv"), 4 * i + 2)
                v_by_chunk(i, 3)
                conv_sig(1)
                conv_in(2)
                conv_sig(2)
                conv_in(3)
                conv_sig(3)
                act.wait_ge(sem("hg_o"), i + 1)
                f(hsig[:], bank[3][:], ACT.Square).then_inc(sem("hg_osq"), 1)
                act.wait_ge(sem("hg_n"), i + 1)
                rstd(hd[:], bank[2][:], P).then_inc(sem("hg_rs"), 1)
                act.wait_ge(sem("sm_T"), i + 1)
                f(b_tok[:].rearrange("p t c -> p (t c)"), bank[6][:], ACT.Copy).then_inc(sem("sm_btok"), 1)
                act.wait_ge(sem("sm_cum"), i + 1)
                ch.did(f(din[:, 0, :], bank[6][:], ACT.Exp))
                f(din[:, 1, :], bank[7][:], ACT.Exp).then_inc(sem("sm_din"), 1)

                def decay(t):
                    act.wait_ge(sem("sm_seg"), 4 * i + t + 1)
                    if t >= 2:
                        act.wait_ge(sem("sm_yd"), 4 * i + t - 1)
                    f(ldec[:, t % 2].rearrange("p h t -> p (h t)"), bank[6 + t % 2][:], ACT.Exp)\
                        .then_inc(sem("sm_ldec"), 1)

                decay(0)
                decay(1)
                if nxt:
                    act.wait_ge(sem("hg_y"), i + 1)
                    read_tile(name, j, 6, hq[:])
                    read_tile(name, j, 7, hf[:])
                decay(2)
                decay(3)
                if nxt:
                    read_tile(name, j, 8, hi_[:])
                    read_tile(name, j, 9, hog[:])
                act.wait_ge(sem("sm_y"), i + 1)
                f(ssq[:], sy[:, 0, :], ACT.Square).then_inc(sem("sm_sq"), 1)
                f(din[:, 0, :], sy[:, 1, :], ACT.Square).then_inc(sem("sm_sq"), 1)
                act.wait_ge(sem("sm_n"), 2 * i + 2)
                rstd(srs[:], bank[6][:], GT * P).then_inc(sem("sm_rs"), 1)
                if nxt:
                    act.wait_ge(bank_free[1], tile_count(name, j, 9) + 1)
                    hg_sigmoids(i + 1)
                ch.settle()

            loop(act, "mix", lambda j: mix("mix", j, j, True), ch)
            mix("mix_last", 0, GROUPS - 1, False)

            for k in range(KT):
                act.wait_ge(sem("m_T_read"), k + 1)
                if k >= 2:
                    act.wait_ge(sem("m_ss"), k - 1)
                f(m_sq[:, k % 2, :], m_ch[:, k, :], ACT.Square).then_inc(sem("m_sq"), 1)
            act.wait_ge(sem("m_ss"), KT)
            rstd(m_rstd[:], bank[4][:, 0:NM], D).then_inc(sem("m_rs"), 1)
            ch.settle()

            def attend(h):
                for k in range(6):
                    if k == 0:
                        act.wait_ge(sem("m_ready"), 1)
                        act.wait_ge(sem("xa_y"), 2 * h + 1)
                    dst, n = ((q_sb, T), (k_sb, NM), (v_sb, NM))[k // 2]
                    read_tile("xa", h, k, dst[:, k % 2, :], n)
                act.wait_ge(sem("xa_vT"), h + 1)
                ch.did(f(v_mt[:].rearrange("p m c -> p (m c)"), bank[2][:], ACT.Copy))
                for t in range(TT):
                    act.wait_ge(sem("xa_max"), 4 * h + t + 1)
                    if t >= 2:
                        act.wait_ge(sem("xa_pT"), 4 * h + t - 1)
                    f(prob[:, t % 2, :], bank[4 + t % 2][:, 0:NM], ACT.Exp, scale=SCALE,
                      bias=st_max[:, t % 2:t % 2 + 1], accum_out=st_sum[:, t % 2:t % 2 + 1])\
                        .then_inc(sem("xa_exp"), 1)
                ch.settle()

            loop(act, "xa", attend, ch)

            def gate_tile(name, i, k, t, g):
                act.wait_ge(slab_done[k % 2], slab_count(name, i, k))
                act.wait_ge(bank_free[1], tile_count(name, i, t + 1) - 1)
                f(gate[:, g, :], bank[t % 2][:], ACT.Sigmoid).then_inc(bank_free[t % 2], 1)

            def merge1(i):
                gate_tile("merge1", i, 0, 0, 0)
                gate_tile("merge1", i, 2, 2, 1)

            act.wait_ge(sem("hg_split"), 1)
            loop(act, "merge1", merge1, ch)

            def merge2(i):
                gate_tile("merge2", i, 0, 0, 0)
                gate_tile("merge2", i, 3, 2, 1)

            loop(act, "merge2", merge2, ch)

            for k in range(KT):
                if k == 0:
                    act.wait_ge(bank_free[1], tile_count("wout", KT // 2 - 1, 1) + 1)
                if k >= 2:
                    act.wait_ge(sem("wo_ss"), k - 1)
                f(nsq[:, k % 2, :], wo[:, k, :], ACT.Square).then_inc(sem("wo_sq"), 1)
            act.wait_ge(sem("wo_ss"), KT)
            rstd(nrs[:], bank[2][:], D).then_inc(sem("wo_rs"), 1)
            for k in range(KT):
                act.wait_ge(sem("x2_new"), k + 1)
                if k >= 2:
                    act.wait_ge(sem("x2_ss"), k - 1)
                f(nsq2[:, k % 2, :], x2[:, k, :], ACT.Square).then_inc(sem("x2_sq"), 1)
            act.wait_ge(sem("x2_ss"), KT)
            rstd(nrs2[:], bank[3][:], D).then_inc(sem("x2_rs"), 1)

            def up(i):
                act.wait_ge(slab_done[0], slab_count("up", i, 0))
                act.wait_ge(bank_free[0], tile_count("up", i, 0))
                f(up_sig[:], bank[0][:], ACT.Sigmoid).then_inc(sem("up_sg"), 1)

            act.wait_ge(sem("h2_ready"), 1)
            loop(act, "up", up, ch)
            for k in range(KT):
                if k == 0:
                    act.wait_ge(bank_free[1], tile_count("down", KT // 2 - 1, 1) + 1)
                if k >= 2:
                    act.wait_ge(sem("fo_ss"), k - 1)
                f(fsq[:, k % 2, :], fo[:, k, :], ACT.Square).then_inc(sem("fo_sq"), 1)
            act.wait_ge(sem("fo_ss"), KT)
            ch.settle()
            rstd(frs[:], bank[2][:], D).then_inc(sem("fo_rs"), 1)
            for n in range(2 * TT):
                act.wait_ge(sem("o_T"), n + 1)
                f(o_tok[:, n // 2, (n % 2) * 512:(n % 2 + 1) * 512], bank[4 + n % 4][:], ACT.Copy)\
                    .then_inc(sem("o_copied"), 1)

        @block.vector
        def _(dve):
            v = nc.vector
            TTO, TS, STT = v.tensor_tensor, v.tensor_scalar, v.scalar_tensor_tensor
            ch = Chain(dve, "dve_chain")

            def split(hi, lo, src, w=None):
                ch.step(TS(hi, src, 1.0 if w is None else w, None, ALU.mult))
                if w is None:
                    return TTO(lo, src, hi.bitcast(F32), ALU.subtract)
                return STT(lo, src, w, hi.bitcast(F32), ALU.mult, ALU.subtract)

            v.memset(vec_rows[:], 0.0).then_inc(sem("vec_zero"), 1)
            dve.wait_ge(sem("wdt_in"), 16)
            ch.did(split(wdt_hi[:], wdt_lo[:], wdt[:]))
            dve.wait_ge(sem("vecs_T"), 1)
            ch.did(v.tensor_copy(conv_ch[:], bank[2][:, 0:P]))
            ch.step(v.tensor_copy(vec_ch[:], bank[2][:, P:2 * P]))
            for k in range(KT):
                dve.wait_ge(sem("x_T"), k + 1)
                v.tensor_copy(x_ch[:, k, :], bank[3 + k % 2][:]).then_inc(sem("x_T_read"), 1)
            a0, n0, _ = V["lb0"]
            a1, _, _ = V["lb1"]
            dve.wait_ge(sem("consts"), 1)
            ch.step(TTO(lb[:], vec_ch[:, a0:a0 + KT], vec_ch[:, a1:a1 + KT], ALU.subtract))
            ch.step(TS(one_lb[:], lb[:], -1.0, None, ALU.mult))
            TTO(dsk_tmp[:], lb[:], one_lb[:], ALU.min).then_inc(sem("lb_diff"), 1)
            dve.wait_ge(sem("x_rstd"), 1)
            for k in range(KT):
                ch.step(TTO(scaled0[:, k % 2, :], x_ch[:, k, :], rstd0[:], ALU.mult))
                last = split(h_hi[:, k, :], h_lo[:, k, :], scaled0[:, k % 2, :], vcol("pre", k))
                if k < KT - 1:
                    ch.did(last)
                else:
                    last.then_inc(sem("h_ready"), 1)
            dve.wait_ge(sem("lb_exp"), 1)
            ch.step(TS(one_lb[:], dsk_tmp[:], 1.0, None, ALU.add))
            ch.step(v.reciprocal(one_lb[:], one_lb[:]))
            ch.step(TTO(dsk_tmp[:], dsk_tmp[:], one_lb[:], ALU.mult))
            ch.step(TS(lb[:], lb[:], 0.0, None, ALU.is_ge))
            ch.step(TTO(one_lb[:], one_lb[:], dsk_tmp[:], ALU.subtract))
            ch.step(TTO(lb[:], lb[:], one_lb[:], ALU.mult))
            ch.step(TTO(lb[:], lb[:], dsk_tmp[:], ALU.add))
            ch.step(TS(one_lb[:], lb[:], -1.0, 1.0, ALU.mult, ALU.add))
            dve.wait_ge(sem("dtv_in"), 48)
            for o in range(2):
                ch.step(v.tensor_copy(dskip_ch[64 * o:64 * o + 64, :],
                                      dskip_bc[64 * o:64 * o + 64, :].rearrange("p (c o) -> p o c", o=2)[:, o, :]))
            dve.wait_ge(sem("dt_mm"), 1)
            ch.step(TTO(dtx[:], bank[6][:, 0:TT * H].rearrange("p (t h) -> p t h", h=H),
                        dtb_bc[:].unsqueeze(1).to_broadcast([P, TT, H]), ALU.add))
            ch.step(TS(dte[:], dtx[:], -1.0, None, ALU.mult))
            TTO(dte[:], dte[:], dtx[:], ALU.max).then_inc(sem("dt_abs"), 1)
            dve.wait_ge(sem("dt_ln"), 1)
            ch.step(STT(dt_tok[:], dtx[:], 0.0, dte[:], ALU.max, ALU.add))
            STT(dta[:], dt_tok[:], -1.0, alog_bc[:].unsqueeze(1).to_broadcast([P, TT, H]),
                ALU.mult, ALU.mult).then_inc(sem("dta_ready"), 1)
            dve.wait_ge(sem("dout_exp"), 1)
            ch.step(TTO(dout_dt[:], dout_dt[:], dt_tok[:], ALU.mult))
            dve.wait_ge(sem("dchunk_exp"), 1)
            dve.wait_ge(sem("dta_ready"), 1)
            for name in ("sm_done", "xa_y", "act_ready"):
                dve.sem_inc(sem(name), 1)
            for t in (hgA, v_blk, hgS, smS, cbm):
                ch.step(v.memset(t[:], 0.0))
            v.memset(xpad[:], 0.0).then_inc(sem("start_done"), 1)
            dve.wait_ge(sem("start_done"), 1)

            def chunked(t):
                return t[:].rearrange("p (c l) -> p c l", l=HG_CHUNK)

            def hg_pre(u, name, j, k3):
                dve.wait_ge(sem("hg_sig"), 3 * u + 1)
                TS(hf[:], hsig[:], one_lb[:, bass.ds(u, 1)], lb[:, bass.ds(u, 1)], ALU.mult, ALU.add)\
                    .then_inc(sem("hg_sig_used"), 1)
                dve.wait_ge(sem("hg_sig_used"), 3 * u + 1)
                TS(hk[:], hf[:], -1.0, 1.0, ALU.mult, ALU.add).then_inc(sem("hg_f"), 1)
                dve.wait_ge(sem("hg_sig"), 3 * u + 2)
                TTO(hq[:], hq[:], hsig[:], ALU.mult).then_inc(sem("hg_sig_used"), 1)
                dve.wait_ge(sem("hg_sig"), 3 * u + 3)
                TTO(hog[:], hog[:], hsig[:], ALU.mult).then_inc(sem("hg_sig_used"), 1)

            hg_pre(0, "hg0", 0, 3)
            ch.settle()

            def mix(name, j, i, nxt):
                dve.wait_ge(sem("hg_g"), i + 1)
                ch.step(v.tensor_tensor_scan(hb[:], hg_start[:], hf[:], 0.0, ALU.mult, ALU.add))
                b3 = chunked(hb)
                ref = b3[:, :, HG_CHUNK // 2:HG_CHUNK // 2 + 1].to_broadcast([P, HC, HG_CHUNK])
                lst = b3[:, :, HG_CHUNK - 1:HG_CHUNK].to_broadcast([P, HC, HG_CHUNK])
                ch.did(TTO(chunked(hd), b3, ref, ALU.subtract))
                TTO(chunked(hd2), lst, b3, ALU.subtract).then_inc(sem("hg_b"), 1)
                dve.wait_ge(sem("hg_e"), i + 1)
                dve.wait_ge(sem("hg_sig_used"), 3 * i + 3)
                ch.did(v.tensor_copy(hdc[:].unsqueeze(2), chunked(e_i)[:, :, HG_CHUNK - 1:HG_CHUNK]))
                ch.settle()
                ch.did(TTO(e_i[:], e_i[:], hq[:], ALU.mult))
                ch.did(TTO(e_q[:], e_q[:], hq[:], ALU.mult))
                ch.did(TTO(e_k[:], e_k[:], hk[:], ALU.mult))
                TTO(e_l[:], e_l[:], hk[:], ALU.mult).then_inc(sem("hg_pre"), 1)
                for k in range(2):
                    dve.wait_ge(sem("sm_zsig"), 2 * i + k + 1)
                    TTO(zs[:, k, :], bank[k][:], zsig[:], ALU.mult).then_inc(bank_free[k], 1)

                def conv(k, ct):
                    dve.wait_ge(bank_free[k % 2], tile_count(name, j, 2 + k) + 1)

                    def tap(n):
                        return conv_ch[:, bass.ds(n * (CONV // P) + ct, 1)]
                    ch.step(TS(cv[:, k, :], xpad[:, 0:T], tap(0), vcol("cb", ct), ALU.mult, ALU.add))
                    for n in range(1, TAPS):
                        last = STT(cv[:, k, :], xpad[:, n:n + T], tap(n), cv[:, k, :], ALU.mult, ALU.add)
                        if n < TAPS - 1:
                            ch.step(last)
                    last.then_inc(sem("sm_cv"), 1)

                def conv_silu(k):
                    dve.wait_ge(sem("sm_csig"), 4 * i + k + 1)
                    TTO(cv[:, k, :], cv[:, k, :], csig[:], ALU.mult).then_inc(sem("sm_cx" if k < 3 else "sm_conv"), 1)

                def hg_states(t):
                    dve.wait_ge(sem("hg_kv"), 4 * i + t + 1)
                    b = 3 - t % 2
                    steps = BC if t < TT - 1 else BC - 1
                    for c in range(steps):
                        n = t * BC + c
                        ins = STT(hgS[:, n + 1, :], hgS[:, n, :], hdc[:, n:n + 1],
                                  bank[b][:, c * P:(c + 1) * P], ALU.mult, ALU.add)
                        if c < steps - 1:
                            ch.step(ins)
                    ins.then_inc(sem("hg_state"), 1)
                    dve.wait_ge(sem("hg_state"), 4 * i + t + 1)

                conv(0, 2 * i)
                wait_alone(dve, sem("hg_A"), i + 1)
                v.copy_predicated(hgA[:],
                                  hg_mask[:].bitcast(U32).unsqueeze(1).to_broadcast([P, TT, P]), tiles(2)).then_inc(sem("hg_masked"), 1)
                conv_silu(0)
                hg_states(0)
                hg_states(1)
                conv(1, 2 * i + 1)
                hg_states(2)
                hg_states(3)
                conv_silu(1)
                conv(2, 2 * GROUPS + i)
                conv_silu(2)
                conv(3, 3 * GROUPS + i)
                conv_silu(3)
                cols = bass.ds(i * HPG, HPG)
                ch.did(v.tensor_copy(g_dta[:], dta[:, :, cols]))
                ch.did(v.tensor_copy(g_dt[:], dt_tok[:, :, cols]))
                ch.did(v.tensor_copy(g_do[:], dout_dt[:, :, cols]))
                ch.did(v.tensor_copy(g_dc[:], dchunk[:, :, :, cols]))
                dve.wait_ge(sem("hg_rs"), i + 1)
                ch.step(TTO(ho[:], bank[3][:], hd[:], ALU.mult))
                STT(y_hg[:, bass.ds(i, 1), :].rearrange("p a t -> p (a t)"), ho[:], vcol("hg", i), hog[:],
                    ALU.mult, ALU.mult).then_inc(sem("hg_y"), 1)
                ch.settle()
                ch.did(v.tensor_copy(dta_rep.rearrange("p t (h d) -> p t h d", d=HD),
                                     g_dta[:].unsqueeze(3).to_broadcast([P, TT, HPG, HD])))
                wait_alone(dve, sem("sm_cb"), i + 1)
                v.copy_predicated(cbm[:], cum_mask[:].bitcast(U32).unsqueeze(1).to_broadcast([P, TT, P]), tiles(7))\
                    .then_inc(sem("sm_masked"), 1)

                def u_dta(t):
                    if t:
                        dve.wait_ge(sem("sm_seg"), 4 * i + t)
                    TTO(udta[:], cum_mask[:].unsqueeze(1).to_broadcast([P, HPG, P]),
                        g_dta[:, t, :].unsqueeze(2).to_broadcast([P, HPG, P]), ALU.mult)\
                        .then_inc(sem("sm_udta"), 1)

                def decay_cb(t):
                    dve.wait_ge(sem("sm_ldec"), 4 * i + t + 1)
                    TTO(ldec[:, t % 2], ldec[:, t % 2], cbm[:, t, :].unsqueeze(1).to_broadcast([P, HPG, P]),
                        ALU.mult).then_inc(sem("sm_M"), 1)

                u_dta(0)
                u_dta(1)
                for c in range(GT):
                    src = bank[4 + c][:].rearrange("p (t h d) -> p t h d", t=TT, d=HD)
                    for dst, g in ((xdt, g_dt), (xdo, g_do)):
                        ch.did(TTO(dst[:, c].rearrange("p t (h d) -> p t h d", d=HD), src,
                                   g[:, :, 2 * c:2 * c + 2].unsqueeze(3).to_broadcast([P, TT, 2, HD]), ALU.mult))
                ch.settle()
                decay_cb(0)
                decay_cb(1)
                u_dta(2)
                u_dta(3)
                decay_cb(2)
                decay_cb(3)

                def states(half):
                    dve.wait_ge(sem("sm_kv"), 2 * i + half + 1)
                    for c in range(4 * half, 4 * half + 4 - half):
                        q = (c // 2) % 2 * HPG * HD
                        src = bank[6 + c % 2][:, q:q + HPG * HD]
                        if c == 0:
                            ch.step(v.tensor_copy(smS[:, 1, :], src))
                            continue
                        ch.step(TTO(smT.rearrange("p (h d) -> p h d", d=HD),
                                    smS[:, c, :].rearrange("p (h d) -> p h d", d=HD),
                                    g_dc[:, c % 2, c // 2, :].unsqueeze(2).to_broadcast([P, HPG, HD]), ALU.mult))
                        last = TTO(smS[:, c + 1, :], smT, src, ALU.add)
                        if c < 4 * half + 3 - half:
                            ch.step(last)
                    last.then_inc(sem("sm_state"), 1)
                    dve.wait_ge(sem("sm_state"), 2 * i + half + 1)

                states(0)
                states(1)
                dve.wait_ge(sem("sm_yo"), i + 1)
                for c in range(GT):
                    y = sy[:, c, :]
                    ch.step(TTO(y, bank[6 + c][:], din[:, c, :], ALU.mult))
                    ch.step(TTO(y, y, bank[4 + c][:], ALU.add))
                    ch.step(STT(y, cv[:, c, :], dskip_ch[:, bass.ds(2 * i + c, 1)], y, ALU.mult, ALU.add))
                    last = TTO(y, y, zs[:, c, :], ALU.mult)
                    if c == 0:
                        ch.did(last)
                last.then_inc(sem("sm_y"), 1)
                dve.wait_ge(sem("sm_rs"), i + 1)
                for c in range(GT):
                    last = STT(y_ssm[:, bass.ds(2 * i + c, 1), :].rearrange("p a t -> p (a t)"), sy[:, c, :],
                               vcol("ssm", 2 * i + c), srs[:], ALU.mult, ALU.mult)
                    if c == 0:
                        ch.did(last)
                last.then_inc(sem("sm_done"), 1)
                if nxt:
                    hg_pre(i + 1, name, j, 9)
                ch.settle()

            loop(dve, "mix", lambda j: mix("mix", j, j, True), ch)
            mix("mix_last", 0, GROUPS - 1, False)
            dve.wait_ge(sem("sm_done"), GROUPS + 1)

            for k in range(KT):
                dve.wait_ge(sem("m_T"), k + 1)
                v.tensor_copy(m_ch[:, k, :], bank[2 + k % 2][:, 0:NM]).then_inc(sem("m_T_read"), 1)
            dve.wait_ge(sem("m_rs"), 1)
            for k in range(KT):
                ch.step(TTO(m_ch[:, k, :], m_ch[:, k, :], m_rstd[:], ALU.mult))
                last = split(m_hi[:, k, :], m_lo[:, k, :], m_ch[:, k, :], vcol("mem", k))
                if k < KT - 1:
                    ch.did(last)
            last.then_inc(sem("m_ready"), 1)

            def attend(h):
                for t in range(TT):
                    s = t % 2
                    dve.wait_ge(sem("xa_s"), 4 * h + t + 1)
                    if t >= 2:
                        ch.settle()
                    ch.step(v.reduce_max(st_inv[:, s:s + 1], bank[4 + s][:, 0:NM], mybir.AxisListType.X))
                    TS(st_max[:, s:s + 1], st_inv[:, s:s + 1], -SCALE, None, ALU.mult).then_inc(sem("xa_max"), 1)
                    dve.wait_ge(sem("xa_exp"), 4 * h + t + 1)
                    ch.step(v.reciprocal(st_inv[:, s:s + 1], st_sum[:, s:s + 1]))
                    TS(prob[:, s, :], prob[:, s, :], st_inv[:, s:s + 1], None, ALU.mult).then_inc(sem("xa_norm"), 1)
                    if t:
                        probs_in(h, t - 1)
                probs_in(h, TT - 1)
                for c in range(QT):
                    dve.wait_ge(sem("xa_o"), 2 * h + c + 1)
                    dve.wait_ge(sem("xa_y"), 2 * h + c + 1)
                    ch.step(v.tensor_copy(xo[:], bank[2 + c][:]))
                    d = bass.ds(2 * h + c, 1)
                    hi = xa_hi[:, d, :].rearrange("p a t -> p (a t)")
                    split(hi, xa_lo[:, d, :].rearrange("p a t -> p (a t)"), xo[:]).then_inc(sem("xa_y"), 1)

            def probs_in(h, t):
                dve.wait_ge(sem("xa_pT"), 4 * h + t + 1)
                v.tensor_copy(pT[:, :, t * P:(t + 1) * P],
                              bank[6 + t % 2][:, 0:NM].rearrange("p (m t) -> p m t", t=P))\
                    .then_inc(sem("xa_p"), 1)

            loop(dve, "xa", attend, ch)
            dve.wait_ge(sem("xa_y"), 2 * XA_HEADS + 1)
            for k in range(KT):
                last = split(hg_hi[:, k, :], hg_lo[:, k, :], y_hg[:, k, :])
                if k < KT - 1:
                    ch.did(last)
            last.then_inc(sem("hg_split"), 1)
            dve.wait_ge(sem("hg_split"), 1)

            def flat(t, i):
                return t[:, bass.ds(i, 1), :].rearrange("p a t -> p (a t)")

            def under_gate(name, i, k, t, g, dst):
                dve.wait_ge(slab_done[k % 2], slab_count(name, i, k))
                gt, gk = t - 1, k - (2 if name == "merge2" else 1)
                dve.wait_ge(bank_free[gt % 2], tile_count(name, i, gt) + 1)
                TTO(dst, bank[t % 2][:], gate[:, g, :], ALU.mult).then_inc(bank_free[t % 2], 1)

            def merge1(i):
                under_gate("merge1", i, 1, 1, 0, part[:, 0, :])
                under_gate("merge1", i, 3, 3, 1, part[:, 1, :])
                dve.wait_ge(bank_free[1], tile_count("merge1", i, 3) + 1)
                ch.step(TTO(flat(merged, i), part[:, 0, :], part[:, 1, :], ALU.add))

            loop(dve, "merge1", merge1, ch)
            dve.wait_ge(slab_done[1], first["merge2"] // 2)
            for k in range(INNER // P):
                last = split(sm_hi[:, k, :], sm_lo[:, k, :], y_ssm[:, k, :])
                if k < INNER // P - 1:
                    ch.did(last)
            last.then_inc(sem("sm_split"), 1)
            dve.wait_ge(sem("sm_split"), 1)

            def merge2(i):
                for c in range(2):
                    under_gate("merge2", i, 3 * c + 2, 2 * c + 1, c, part[:, c, :])
                    dve.wait_ge(bank_free[1], tile_count("merge2", i, 2 * c + 1) + 1)
                    ch.step(TTO(flat(merged, 2 * i + c), flat(merged, 2 * i + c), part[:, c, :], ALU.add))

            loop(dve, "merge2", merge2, ch)
            for k in range(KT):
                last = split(mg_hi[:, k, :], mg_lo[:, k, :], merged[:, k, :])
                if k < KT - 1:
                    ch.did(last)
            last.then_inc(sem("merged_split"), 1)
            dve.wait_ge(sem("merged_split"), 1)

            def copy_out(name, dst):
                def body(i):
                    n = size[name] // 2
                    for c in range(2):
                        k = n * c + n - 1
                        dve.wait_ge(slab_done[k % 2], slab_count(name, i, k))
                        TS(flat(dst, 2 * i + c), bank[c][:], 1.0, None, ALU.mult).then_inc(bank_free[c], 1)
                return body

            dve.wait_ge(slab_done[1], first["wout"] // 2)
            loop(dve, "wout", copy_out("wout", wo), ch)
            dve.wait_ge(bank_free[1], tile_count("wout", KT // 2 - 1, 1) + 1)
            for k in range(KT):
                dve.wait_ge(sem("x2_T"), k + 1)
                v.tensor_copy(x2[:, k, :], bank[4 + k % 2][:]).then_inc(sem("x2_read"), 1)
            dve.wait_ge(sem("wo_rs"), 1)
            dve.wait_ge(sem("x2_read"), KT)
            for k in range(KT):
                ch.step(TTO(nsc[:, k % 2, :], wo[:, k, :], nrs[:], ALU.mult))
                STT(x2[:, k, :], nsc[:, k % 2, :], vcol("post", k), x2[:, k, :], ALU.mult, ALU.add)\
                    .then_inc(sem("x2_new"), 1)
            dve.wait_ge(sem("x2_rs"), 1)
            dve.wait_ge(sem("x2_new"), KT)
            for k in range(KT):
                ch.step(TTO(nsc[:, k % 2, :], x2[:, k, :], nrs2[:], ALU.mult))
                last = split(h_hi[:, k, :], h_lo[:, k, :], nsc[:, k % 2, :], vcol("fpre", k))
                if k < KT - 1:
                    ch.did(last)
            last.then_inc(sem("h2_ready"), 1)
            dve.wait_ge(sem("h2_ready"), 1)

            def up(i):
                dve.wait_ge(sem("act_ready"), i + 1)
                dve.wait_ge(sem("up_sg"), i + 1)
                TTO(up_a[:], bank[0][:], up_sig[:], ALU.mult).then_inc(bank_free[0], 1)
                dve.wait_ge(bank_free[0], tile_count("up", i, 0) + 1)
                dve.wait_ge(slab_done[1], slab_count("up", i, 1))
                TTO(up_a[:], up_a[:], bank[1][:], ALU.mult).then_inc(bank_free[1], 1)
                dve.wait_ge(bank_free[1], tile_count("up", i, 1) + 1)
                split(flat(a_hi, i), flat(a_lo, i), up_a[:]).then_inc(sem("act_ready"), 1)

            loop(dve, "up", up, ch)
            dve.wait_ge(sem("act_ready"), FT + 1)
            loop(dve, "down", copy_out("down", fo), ch)
            dve.wait_ge(bank_free[1], tile_count("down", KT // 2 - 1, 1) + 1)
            dve.wait_ge(sem("fo_rs"), 1)
            for k in range(KT):
                ch.step(TTO(fsc[:, k % 2, :], fo[:, k, :], frs[:], ALU.mult))
                STT(x2[:, k, :], fsc[:, k % 2, :], vcol("fpost", k), x2[:, k, :], ALU.mult, ALU.add)\
                    .then_inc(sem("y_ready"), 1)


_OUT = (1, 512, 1024)


def kernel(**inputs):
    import numpy as np
    import concourse.bacc as bacc
    from concourse.bass_utils import run_bass_kernel_spmd as run

    nc = bacc.Bacc("TRN2", target_bir_lowering=False, num_devices=1)
    arrays, args = {}, {}
    for name, value in inputs.items():
        a = np.ascontiguousarray(value)
        arrays[f"in_{name}"] = a
        args[name] = nc.dram_tensor(f"in_{name}", a.shape, mybir.dt.from_np(a.dtype), kind="ExternalInput").ap()
    args["out"] = nc.dram_tensor("out_0", _OUT, F32, kind="ExternalOutput").ap()
    hybrid_layer(nc, **args)
    result = run(nc, [arrays], core_ids=[0])
    return result.results[0]["out_0"]
```

```python
from contextlib import ExitStack

import concourse.bass as bass
from concourse import mybir

ALU = mybir.AluOpType
ACT = mybir.ActivationFunctionType
F32 = mybir.dt.float32
F32R = mybir.dt.float32r
U32 = mybir.dt.uint32

P = 128
KB = 1024
EPS = 1e-6
HG_CHUNK = 32
SSM_CHUNK = 64
GROUPS = 8
XA_HEADS = 4


def hybrid_layer(nc, x, mem, norm_mix_pre, norm_mix_post, norm_ffn_pre, norm_ffn_post, norm_mem,
                 w_in, hg_lb_param, hg_norm_w, conv_w, conv_b, dt_bias, a_log, d_skip,
                 ssm_norm_w, w_mem_kv, w_br_hg, w_br_ssm, w_br_xa, w_out, w_ffn_up, w_ffn_down, out):
    T, D = x.shape[1], x.shape[2]
    NM = mem.shape[1]
    HG = hg_norm_w.shape[1]
    INNER = ssm_norm_w.shape[1]
    CONV = conv_b.shape[1]
    TAPS = conv_w.shape[1]
    H = dt_bias.shape[1]
    FF = w_ffn_down.shape[1]
    KT = D // P
    TT = T // P
    NC = T // SSM_CHUNK
    HC = T // HG_CHUNK
    BC = P // HG_CHUNK
    HPG = H // GROUPS
    HD = INNER // H
    GT = INNER // GROUPS // P
    MT = NM // P
    QT = D // XA_HEADS // P
    FT = FF // P
    SCALE = float(D // XA_HEADS) ** -0.5
    assert T == 512 and D == 1024 and HG == D and HPG * HD == 2 * P and GT == 2 and QT == 2 and MT == 2

    C_Q, C_F, C_I, C_OG = 0, HG, 2 * HG, 3 * HG
    C_Z = 4 * HG
    C_XS = C_Z + INNER
    C_B = C_XS + INNER
    C_C = C_B + GROUPS * P
    C_DT = C_XS + CONV
    C_XQ = C_DT + H
    C_G = C_XQ + D

    with ExitStack() as ctx:
        base = -(-nc.sbuf_base // 32) * 32
        arena = ctx.enter_context(nc.sbuf_tensor("arena", [P, (207 * KB) // 4], F32))

        class Region:
            def __init__(self, start, size):
                self.at, self.end = base + start * KB, base + (start + size) * KB

            def __call__(self, name, shape, dt=F32):
                n = 4
                for s in shape[1:]:
                    n *= s
                t = nc.alloc_sbuf_tensor_at(name, shape, dt, offset=self.at)
                self.at += -(-n // 32) * 32
                assert self.at <= self.end, (name, self.at - self.end)
                return t

        RINGS, ACTS, SSM_OUT, HG_OUT, SCR, END = 9, 33, 65, 97, 113, 207
        const = Region(0, RINGS)
        rings = Region(RINGS, ACTS - RINGS)
        acts = Region(ACTS, SSM_OUT - ACTS)
        ssm_out = Region(SSM_OUT, HG_OUT - SSM_OUT)
        hg_out = Region(HG_OUT, SCR - HG_OUT)

        ident = const("ident", [P, P])
        ones = const("ones", [P, P])
        hg_mask = const("hg_mask", [P, P])
        cum_mask = const("cum_mask", [P, P])
        after_mask = const("after_mask", [P, P])
        hg_start = const("hg_start", [P, T])
        conv_ch = const("conv_ch", [P, TAPS * CONV // P])
        vec_ch = const("vec_ch", [P, P])
        lb = const("lb", [P, KT])
        one_lb = const("one_lb", [P, KT])
        dskip_ch = const("dskip_ch", [P, INNER // P])
        dt_tok = const("dt_tok", [P, TT, H])
        dta = const("dta", [P, TT, H])
        dout_dt = const("dout_dt", [P, TT, H])
        dchunk = const("dchunk", [P, 2, TT, H])
        eps_col = const("eps_col", [P, 1])
        zero_col = const("zero_col", [P, 1])

        raw = rings("raw", [P, 2, KT, P])
        w_hi = [rings(f"w_hi{s}", [P, KT, P], F32R) for s in range(2)]
        w_lo = [rings(f"w_lo{s}", [P, KT, P], F32R) for s in range(2)]
        h_hi = acts("h_hi", [P, KT, T], F32R)
        h_lo = acts("h_lo", [P, KT, T], F32R)
        y_ssm = ssm_out("y_ssm", [P, INNER // P, T])
        y_hg = hg_out("y_hg", [P, KT, T])

        r = Region(SCR, END - SCR)
        x_tok = r("x_tok", [P, TT, D])
        x_ch = r("x_ch", [P, KT, T])
        sq0 = r("sq0", [P, 2, T])
        rstd0 = r("rstd0", [P, T])
        scaled0 = r("scaled0", [P, 2, T])
        vec_rows = r("vec_rows", [P, P])
        conv_rows = r("conv_rows", [P, P])
        dskip_bc = r("dskip_bc", [P, H])
        dtb_bc = r("dtb_bc", [P, H])
        alog_bc = r("alog_bc", [P, H])
        wdt = r("wdt", [P, KT, H])
        wdt_hi = r("wdt_hi", [P, KT, H], F32R)
        wdt_lo = r("wdt_lo", [P, KT, H], F32R)
        dtx = r("dtx", [P, TT, H])
        dte = r("dte", [P, TT, H])
        dsk_tmp = r("dsk_tmp", [P, KT])

        r = Region(SCR, END - SCR)
        hq = r("hq", [P, T])
        hf = r("hf", [P, T])
        hi_ = r("hi_", [P, T])
        hog = r("hog", [P, T])
        hsig = r("hsig", [P, T])
        hk = r("hk", [P, T])
        hb = r("hb", [P, T])
        hd2 = hsig
        e_q = r("e_q", [P, T])
        hd = r("hd", [P, T])
        e_k = r("e_k", [P, T])
        e_i = r("e_i", [P, T])
        e_l = r("e_l", [P, T])
        hdc = r("hdc", [P, HC])
        v_tok = r("v_tok", [P, TT, P])
        v_blk = r("v_blk", [P, 2, BC, P])
        ki_tok = r("ki_tok", [P, TT, P])
        hgA = r("hgA", [P, TT, P])
        hgS = r("hgS", [P, HC, P])
        ho = e_q
        zs = r("zs", [P, GT, T])
        xpad = r("xpad", [P, 516])
        cv = r("cv", [P, 4, T])
        csig = r("csig", [P, T])
        xdt = r("xdt", [P, GT, TT, P])
        xdo = r("xdo", [P, GT, TT, P])
        b_tok = r("b_tok", [P, TT, P])
        cbm = r("cbm", [P, TT, P])
        udta = r("udta", [P, 2, HPG, P])
        ldec = r("ldec", [P, 2, HPG, P])
        smS = r("smS", [P, NC, HPG * HD])
        smT = csig[:, 0:HPG * HD]
        dta_rep = xdo[:].rearrange("p c t d -> p (c t d)").rearrange("p (t d) -> p t d", d=HPG * HD)
        din = r("din", [P, GT, T])
        sy = xdt[:].rearrange("p c t d -> p c (t d)")
        ssq = csig
        zsig = csig
        srs = hd
        g_dta = r("g_dta", [P, TT, HPG])
        g_dt = r("g_dt", [P, TT, HPG])
        g_do = r("g_do", [P, TT, HPG])
        g_dc = r("g_dc", [P, 2, TT, HPG])

        r = Region(SCR, 16)
        m_hi = r("m_hi", [P, KT, NM], F32R)
        m_lo = r("m_lo", [P, KT, NM], F32R)
        r = Region(SCR + 18, 19)
        m_ch = r("m_ch", [P, KT, NM])
        m_sq = r("m_sq", [P, 2, NM])
        m_rstd = r("m_rstd", [P, NM])
        m_tok = r("m_tok", [P, MT, D])
        sm_gate = [Region(SCR + 26, 2)("sm_gate0", [P, T]), Region(SCR + 16, 2)("sm_gate1", [P, T])]
        r = Region(SCR + 30, 64)
        sm_hi = r("sm_hi", [P, INNER // P, T], F32R)
        sm_lo = r("sm_lo", [P, INNER // P, T], F32R)
        merged = Region(SSM_OUT, 16)("merged", [P, KT, T])
        r = Region(SCR + 16, 78)
        xa_hi = r("xa_hi", [P, KT, T], F32R)
        xa_lo = r("xa_lo", [P, KT, T], F32R)
        hg_hi = r("hg_hi", [P, KT, T], F32R)
        hg_lo = r("hg_lo", [P, KT, T], F32R)
        pT = r("pT", [P, MT, T])
        xo = r("xo", [P, T])
        gate = [r(f"gate{g}", [P, T]) for g in range(2)]
        part = r("part", [P, 2, T])
        r = Region(SSM_OUT + 16, 16)
        q_sb = r("q_sb", [P, QT, T])
        k_sb = r("k_sb", [P, QT, NM])
        v_sb = r("v_sb", [P, QT, NM])
        v_mt = r("v_mt", [P, MT, QT * P])
        prob = r("prob", [P, TT, NM])
        st_max = r("st_max", [P, TT])
        st_sum = r("st_sum", [P, TT])
        st_inv = r("st_inv", [P, TT])
        r = Region(SSM_OUT + 16, 32)
        mg_hi = r("mg_hi", [P, KT, T], F32R)
        mg_lo = r("mg_lo", [P, KT, T], F32R)
        x2 = Region(SSM_OUT, 16)("x2", [P, KT, T])
        r = Region(SCR, 64)
        x_tok2 = r("x_tok2", [P, TT, D])
        wo = r("wo", [P, KT, T])
        nsq = r("nsq", [P, 2, T])
        nrs = r("nrs", [P, T])
        nsc = r("nsc", [P, 2, T])
        nsq2 = r("nsq2", [P, 2, T])
        nrs2 = r("nrs2", [P, T])
        r = Region(SCR, 88)
        a_hi = r("a_hi", [P, FT, T], F32R)
        a_lo = r("a_lo", [P, FT, T], F32R)
        fo = Region(SSM_OUT + 16, 16)("fo", [P, KT, T])
        r = Region(HG_OUT, 16)
        up_sig = r("up_sig", [P, T])
        up_a = r("up_a", [P, T])
        fsq = r("fsq", [P, 2, T])
        frs = r("frs", [P, T])
        fsc = r("fsc", [P, 2, T])
        o_tok = Region(ACTS, 16)("o_tok", [P, TT, D])

        bank = [ctx.enter_context(nc.psum_tensor(f"bank{b}", [P, 512], F32)) for b in range(8)]

        def tiles(b, n=TT):
            return bank[b][:, 0:n * P].rearrange("p (t c) -> p t c", c=P)

        sems = {}

        def sem(name):
            if name not in sems:
                sems[name] = ctx.enter_context(nc.semaphore(name))
            return sems[name]

        def wait_alone(eng, s, value):
            eng.wait_ge(s, value)
            eng.sem_inc(sem("waits_passed"), 1)

        class Chain:

            def __init__(self, eng, name):
                self.eng, self.sem, self.n = eng, sem(name), 0

            def restart(self):
                if self.n:
                    self.settle()
                    self.eng.sem_clear(self.sem)
                self.n = 0

            def did(self, ins):
                ins.then_inc(self.sem, 1)
                self.n += 1

            def settle(self):
                self.eng.wait_ge(self.sem, self.n)

            def step(self, ins):
                self.did(ins)
                self.settle()

        def rows(w):
            return w[0].rearrange("(k p) n -> p k n", p=P)

        win_v, kv_v = rows(w_in), rows(w_mem_kv)
        bhg_v, bssm_v, bxa_v = rows(w_br_hg), rows(w_br_ssm), rows(w_br_xa)
        wo_v, up_v, down_v = rows(w_out), rows(w_ffn_up), rows(w_ffn_down)

        hg_slabs = [(win_v, C_F, P), (win_v, C_Q, P), (win_v, C_I, P), (win_v, C_OG, P)]
        ssm_slabs = [(win_v, C_Z, 2 * P), (win_v, C_Z + P, 2 * P), (win_v, C_XS, 2 * P),
                     (win_v, C_XS + P, 2 * P), (win_v, C_B, P), (win_v, C_C, P)]

        def slab(w, start, stride, k0=0, k1=KT, shift=0):
            return (w, start, stride, k0, k1, shift)

        xa_parts = [(win_v, C_XQ), (kv_v, 0), (kv_v, D)]

        SECTIONS = [
            ("hg0", 1, [slab(*s) for s in hg_slabs]),
            ("ssm0", 1, [slab(*s) for s in ssm_slabs]),
            ("mix", GROUPS - 1, [slab(*s, shift=1) for s in hg_slabs + ssm_slabs]),
            ("mssm", KT // 2, [slab(w, s + c * P, 2 * P, *k) for c in range(2) for w, s, k in
                               ((win_v, C_G + D, ()), (bssm_v, 0, (0, KT)), (bssm_v, 0, (KT, 2 * KT)))]),
            ("xa0", 1, [slab(w, s + c * P, QT * P) for w, s in xa_parts for c in range(QT)]),
            ("xa", XA_HEADS - 1, [slab(w, s + c * P, QT * P, shift=1) for w, s in xa_parts for c in range(QT)]),
            ("merge", KT, [slab(win_v, C_G, P), slab(win_v, C_G + 2 * D, P),
                           slab(bhg_v, 0, P), slab(bxa_v, 0, P)]),
            ("wout", KT // 2, [slab(wo_v, c * P, 2 * P) for c in range(2)]),
            ("up", FT, [slab(up_v, 0, P), slab(up_v, FF, P)]),
            ("down", KT // 2, [slab(down_v, c * P, 2 * P, k, min(k + KT, FT))
                               for c in range(2) for k in range(0, FT, KT)]),
        ]
        first, n = {}, 0
        for name, its, slabs in SECTIONS:
            assert n % 2 == 0 and len(slabs) % 2 == 0
            first[name] = n
            n += its * len(slabs)
        size = {name: len(slabs) for name, _, slabs in SECTIONS}
        tiles_of = {name: len(slabs) for name, _, slabs in SECTIONS} | {"mssm": 4, "down": 2}
        first_tile, n = {}, 0
        for name, its, _ in SECTIONS:
            first_tile[name] = n
            n += its * tiles_of[name]

        def slab_count(name, i, k):
            return first[name] // 2 + i * (size[name] // 2) + k // 2 + 1

        def tile_count(name, i, t):
            return first_tile[name] // 2 + i * (tiles_of[name] // 2) + t // 2 + 1

        raw_full = [sem(f"raw_full{s}") for s in range(2)]
        split_full = [sem(f"split_full{s}") for s in range(2)]
        slab_done = [sem(f"slab_done{s}") for s in range(2)]
        bank_free = [sem(f"bank_free{s}") for s in range(2)]

        def loop(eng, name, body, chain=None):
            its = next(s[1] for s in SECTIONS if s[0] == name)
            if chain:
                chain.restart()
            if its == 1:
                body(0)
            else:
                with eng.Fori(0, its) as i:
                    body(i)
                    if chain:
                        chain.restart()

        block = ctx.enter_context(nc.Block())

        x_v = x[0].rearrange("(t p) d -> p t d", p=P)
        mem_v = mem[0].rearrange("(t p) d -> p t d", p=P)
        out_v = out[0].rearrange("(t p) d -> p t d", p=P)
        V, n = {}, 0
        for name, ap in (("pre", norm_mix_pre[0]), ("post", norm_mix_post[0]), ("fpre", norm_ffn_pre[0]),
                         ("fpost", norm_ffn_post[0]), ("mem", norm_mem[0]), ("lb0", hg_lb_param[0]),
                         ("lb1", hg_lb_param[1]), ("hg", hg_norm_w[0]), ("cb", conv_b[0]),
                         ("ssm", ssm_norm_w[0])):
            V[name] = (n, ap.shape[0] // P, ap)
            n += ap.shape[0] // P
        VR = n
        assert VR <= P and TAPS * CONV // P == P

        def vcol(name, c):
            return vec_ch[:, bass.ds(V[name][0] + c, 1)]

        @block.sync
        def _(sp):
            for s in range(2):
                sp.sem_inc(bank_free[s], 1)
            sp.dma_start(x_tok[:], x_v).then_inc(sem("x_in"), 16)

            def load(name, i, k):
                w, start, stride, k0, k1, shift = next(s[2] for s in SECTIONS if s[0] == name)[k]
                c = start + stride * (i + shift)
                if not (name == "hg0" and k < 2):
                    wait_alone(sp, split_full[k % 2], slab_count(name, i, k) - 1)
                sp.dma_start(raw[:, k % 2, 0:k1 - k0, :], w[:, k0:k1, bass.ds(c, P)])\
                  .then_inc(raw_full[k % 2], 16)

            def loads(*names):
                for name in names:
                    loop(sp, name, lambda i: [load(name, i, k) for k in range(size[name])])

            loads("hg0", "ssm0", "mix")
            sp.wait_ge(sem("hg_y"), GROUPS)
            sp.dma_start(m_tok[:], mem_v).then_inc(sem("mem_in"), 16)
            loads("mssm", "xa0", "xa")
            sp.wait_ge(slab_done[1], first["merge"] // 2)
            sp.dma_start(x_tok2[:], x_v).then_inc(sem("x_again"), 16)
            loads("merge", "wout", "up", "down")
            for t in range(TT):
                sp.wait_ge(sem("o_copied"), 2 * t + 2)
                sp.dma_start(out_v[:, t, :], o_tok[:, t, :]).then_inc(sem("stored"), 16)
            sp.wait_ge(sem("stored"), 16 * TT)

        @block.gpsimd
        def _(pool):
            g = nc.gpsimd
            ch = Chain(pool, "pool_chain")
            ch.did(g.memset(ident[:], 0.0))
            ch.did(g.memset(ones[:], 1.0))
            ch.did(g.memset(eps_col[:], EPS))
            ch.did(g.memset(zero_col[:], 0.0))
            for m in (hg_mask, cum_mask, after_mask):
                ch.did(g.memset(m[:], 1.0))
            ch.did(g.memset(hg_start[:], 1.0))
            ch.settle()
            ch.did(g.affine_select(out=ident[:], in_=ident[:], compare_op=ALU.not_equal, fill=1.0,
                                   base=0, pattern=[[-1, P]], channel_multiplier=1))

            def same_chunk(m, n):
                v = m[:].rearrange("p (b c) -> p b c", c=n)
                ch.settle()
                ch.step(g.affine_select(out=v, in_=v, compare_op=ALU.is_ge, fill=0.0, base=0,
                                        pattern=[[-n, P // n], [0, n]], channel_multiplier=1))
                ch.step(g.affine_select(out=v, in_=v, compare_op=ALU.is_ge, fill=0.0, base=n - 1,
                                        pattern=[[n, P // n], [0, n]], channel_multiplier=-1))

            same_chunk(hg_mask, HG_CHUNK)
            same_chunk(cum_mask, SSM_CHUNK)
            same_chunk(after_mask, SSM_CHUNK)
            for m in (hg_mask, cum_mask):
                ch.did(g.affine_select(out=m[:], in_=m[:], compare_op=ALU.is_ge, fill=0.0, base=0,
                                       pattern=[[1, P]], channel_multiplier=-1))
            ch.did(g.affine_select(out=after_mask[:], in_=after_mask[:], compare_op=ALU.is_ge, fill=0.0,
                                   base=-1, pattern=[[-1, P]], channel_multiplier=1))
            v = hg_start[:].rearrange("p (b c) -> p b c", c=HG_CHUNK)
            g.affine_select(out=v, in_=v, compare_op=ALU.is_ge, fill=0.0, base=-1,
                            pattern=[[0, HC], [1, HG_CHUNK]], channel_multiplier=0).then_inc(sem("consts"), 1)

            def split(name, i, k):
                ks = next(s[2] for s in SECTIONS if s[0] == name)[k]
                n, s = ks[4] - ks[3], k % 2
                src = raw[:, s, 0:n, :]
                pool.wait_ge(raw_full[s], 16 * slab_count(name, i, k))
                if not (name == "hg0" and k < 2):
                    pool.wait_ge(slab_done[s], slab_count(name, i, k) - 1)
                ch.step(g.tensor_tensor(w_hi[s][:, 0:n, :], src,
                                        zero_col[:].unsqueeze(2).to_broadcast([P, n, P]), ALU.add))
                g.tensor_tensor(w_lo[s][:, 0:n, :], src, w_hi[s][:, 0:n, :].bitcast(F32), ALU.subtract)\
                 .then_inc(split_full[s], 1)

            def section(name):
                def body(i):
                    for k in range(size[name]):
                        split(name, i, k)
                loop(pool, name, body, ch)

            for name, _, _ in SECTIONS:
                section(name)

        @block.tensor
        def _(pe):
            mm = nc.tensor.matmul

            part_ready = {"sm_split": 0, "mg_split": 0, "xa_y": 1}

            def gemm_slab(name, i, k, t, rhs_hi, rhs_lo, k_first, k_last, N=T, parts=None):
                ks = next(s[2] for s in SECTIONS if s[0] == name)[k]
                s, b = k % 2, t % 2
                pe.wait_ge(split_full[s], slab_count(name, i, k))
                if k_first:
                    pe.wait_ge(bank_free[b], tile_count(name, i, t))
                k0, n = ks[3], ks[4] - ks[3]
                for kk in range(n):
                    if parts:
                        pe.wait_ge(sem(parts), k0 + kk + 1 + part_ready[parts])
                    for w, r in ((w_hi, rhs_hi), (w_hi, rhs_lo), (w_lo, rhs_hi)):
                        last = mm(bank[b][:, 0:N], w[s][:, kk, :], r[:, k0 + kk, :],
                                  start=(k_first and kk == 0 and w is w_hi and r is rhs_hi),
                                  stop=(k_last and kk == n - 1 and w is w_lo))
                last.then_inc(slab_done[s], 1)

            def one(name, i, k, hi=h_hi, lo=h_lo, N=T):
                gemm_slab(name, i, k, k, hi, lo, True, True, N)

            pe.wait_ge(sem("consts"), 1)
            pe.wait_ge(sem("vecs_in"), 16 * (1 + len(V)))
            nc.tensor.transpose(bank[2][:, 0:P], conv_rows[:], ident[:])
            nc.tensor.transpose(bank[2][:, P:2 * P], vec_rows[:], ident[:]).then_inc(sem("vecs_T"), 1)
            pe.wait_ge(sem("x_in"), 16)
            for k in range(KT):
                b = 3 + k % 2
                if k >= 2:
                    pe.wait_ge(sem("x_T_read"), k - 1)
                for t in range(TT):
                    last = nc.tensor.transpose(bank[b][:, t * P:(t + 1) * P],
                                               x_tok[:, t, k * P:(k + 1) * P], ident[:])
                last.then_inc(sem("x_T"), 1)
            for k in range(KT):
                pe.wait_ge(sem("x_sq"), k + 1)
                mm(bank[5][:], ones[:], sq0[:, k % 2, :], start=(k == 0), stop=(k == KT - 1))\
                    .then_inc(sem("x_ss"), 1)
            pe.wait_ge(sem("h_ready"), 1)
            for t in range(TT):
                for kk in range(KT):
                    for l, w in ((h_hi, wdt_hi), (h_lo, wdt_hi), (h_hi, wdt_lo)):
                        last = mm(bank[6][:, t * H:(t + 1) * H], l[:, kk, t * P:(t + 1) * P], w[:, kk, :],
                                  start=(kk == 0 and l is h_hi and w is wdt_hi),
                                  stop=(kk == KT - 1 and w is wdt_lo))
            last.then_inc(sem("dt_mm"), 1)
            pe.wait_ge(sem("dta_ready"), 1)
            dta_f = dta[:].rearrange("p t h -> p (t h)")
            mm(bank[6][:, 0:TT * H], after_mask[:], dta_f, start=True, stop=True).then_inc(sem("dt_mm"), 1)
            mm(bank[7][:, 0:TT * H], ones[0:64, :], dta[0:64].rearrange("p t h -> p (t h)"),
               start=True, stop=True)
            pe.wait_ge(sem("x_T_read"), KT)
            mm(bank[4][:, 0:TT * H], ones[64:128, :], dta[64:128].rearrange("p t h -> p (t h)"),
               start=True, stop=True).then_inc(sem("dt_mm"), 1)
            for k in range(4):
                one("hg0", 0, k)

            def hg_transposes(i):
                pe.wait_ge(sem("hg_pre"), i + 1)
                for t in range(TT):
                    nc.tensor.transpose(bank[2][:, t * P:(t + 1) * P], hi_[:, t * P:(t + 1) * P], ident[:])
                for t in range(TT):
                    last = nc.tensor.transpose(bank[3][:, t * P:(t + 1) * P],
                                               e_l[:, t * P:(t + 1) * P], ident[:])
                last.then_inc(sem("hg_T"), 1)

            def hg_scores(i):
                pe.wait_ge(sem("hg_tok"), i + 1)
                for t in range(TT):
                    c = slice(t * P, (t + 1) * P)
                    last = mm(bank[2][:, c], e_k[:, c], e_q[:, c], start=True, stop=True)
                last.then_inc(sem("hg_A"), 1)

            def hg_kv(i, t):
                pe.wait_ge(sem("hg_vblk"), 4 * i + t + 1)
                if t == 1:
                    pe.wait_ge(sem("hg_masked"), i + 1)
                if t >= 2:
                    pe.wait_ge(sem("hg_state"), 4 * i + t - 1)
                mm(bank[3 - t % 2][:], ki_tok[:, t, :], v_blk[:, t % 2].rearrange("p c v -> p (c v)"),
                   start=True, stop=True).then_inc(sem("hg_kv"), 1)

            def hg_out_mm(i):
                pe.wait_ge(sem("hg_state"), 4 * i + 4)
                for t in range(TT):
                    c0 = t * P
                    mm(bank[3][:, c0:c0 + P], v_tok[:, t, :], hgA[:, t, :], start=True, stop=False)
                    for c in range(BC):
                        a = c0 + c * HG_CHUNK
                        last = mm(bank[3][:, a:a + HG_CHUNK], hgS[:, t * BC + c, :], e_i[:, a:a + HG_CHUNK],
                                  start=False, stop=(c == BC - 1))
                last.then_inc(sem("hg_o"), 1)

            def hg_norm(i):
                pe.wait_ge(sem("hg_osq"), i + 1)
                mm(bank[2][:], ones[:], hsig[:], start=True, stop=True).then_inc(sem("hg_n"), 1)

            def sm_transposes(i):
                pe.wait_ge(sem("sm_conv"), i + 1)
                pe.wait_ge(sem("sm_done"), i + 1)
                for c in range(GT):
                    for t in range(TT):
                        nc.tensor.transpose(bank[4 + c][:, t * P:(t + 1) * P],
                                            cv[:, c, t * P:(t + 1) * P], ident[:])
                for t in range(TT):
                    last = nc.tensor.transpose(bank[6][:, t * P:(t + 1) * P],
                                               cv[:, 2, t * P:(t + 1) * P], ident[:])
                last.then_inc(sem("sm_T"), 1)
                for t in range(TT):
                    c = slice(t * P, (t + 1) * P)
                    last = mm(bank[7][:, c], cv[:, 2, c], cv[:, 3, c], start=True, stop=True)
                last.then_inc(sem("sm_cb"), 1)

            def sm_din(i):
                pe.wait_ge(sem("sm_btok"), i + 1)
                pe.wait_ge(sem("sm_masked"), i + 1)
                for c in range(GT):
                    for t in range(TT):
                        last = mm(bank[6 + c][:, t * P:(t + 1) * P], dta_rep[:, t, c * P:(c + 1) * P],
                                  cum_mask[:], start=True, stop=True)
                last.then_inc(sem("sm_cum"), 1)

            def sm_seg(i, t):
                pe.wait_ge(sem("sm_udta"), 4 * i + t + 1)
                if t < 2:
                    pe.wait_ge(sem("sm_din"), i + 1)
                else:
                    pe.wait_ge(sem("sm_ldec"), 4 * i + t - 1)
                mm(bank[6 + t % 2][:], after_mask[:], udta[:, t % 2].rearrange("p h t -> p (h t)"),
                   start=True, stop=True).then_inc(sem("sm_seg"), 1)

            def sm_diag(i, t):
                pe.wait_ge(sem("sm_M"), 4 * i + t + 1)
                for h in range(HPG):
                    c, o = h // 2, (h % 2) * HD
                    last = mm(bank[4 + c][o:o + HD, t * P:(t + 1) * P], xdt[:, c, t, o:o + HD],
                              ldec[:, t % 2, h, :], start=True, stop=True)
                last.then_inc(sem("sm_yd"), 1)

            def sm_kv(i, half):
                if half == 0:
                    pe.wait_ge(sem("hg_y"), i + 1)
                    pe.wait_ge(sem("sm_xdo"), i + 1)
                else:
                    pe.wait_ge(sem("sm_state"), 2 * i + 1)
                for c in range(4 * half, 4 * half + 4 - half):
                    p = 64 * (c % 2)
                    q = (c // 2) % 2 * HPG * HD
                    last = mm(bank[2 + c % 2][:, q:q + HPG * HD], b_tok[p:p + 64, c // 2, :],
                              xdo[p:p + 64, :, c // 2, :], start=True, stop=True)
                last.then_inc(sem("sm_kv"), 1)

            def sm_off(i):
                pe.wait_ge(sem("sm_state"), 2 * i + 2)
                pe.wait_ge(sem("sm_ldec"), 4 * i + 4)
                for c in range(GT):
                    for k in range(NC):
                        a = k * SSM_CHUNK
                        last = mm(bank[6 + c][:, a:a + SSM_CHUNK], smS[:, k, c * P:(c + 1) * P],
                                  cv[:, 3, a:a + SSM_CHUNK], start=True, stop=True)
                last.then_inc(sem("sm_yo"), 1)

            def sm_norm(i):
                for c in range(GT):
                    pe.wait_ge(sem("sm_sq"), 2 * i + c + 1)
                    last = mm(bank[6][:], ones[:], ssq[:] if c == 0 else din[:, 0, :], start=(c == 0), stop=(c == 1))
                last.then_inc(sem("sm_n"), 1)

            def hgrn_half(name, j, base, i):
                one(name, j, base)
                if base:
                    sm_off(i - 1)
                one(name, j, base + 1)
                if base:
                    sm_norm(i - 1)
                one(name, j, base + 2)
                hg_transposes(i)
                one(name, j, base + 3)
                hg_scores(i)
                hg_kv(i, 0)
                one(name, j, base + 4)
                hg_kv(i, 1)
                hg_kv(i, 2)
                one(name, j, base + 5)
                hg_kv(i, 3)

            def ssm_half(name, j, i):
                def next_slab(k):
                    if name:
                        one(name, j, k)
                next_slab(0)
                hg_out_mm(i)
                sm_transposes(i)
                next_slab(1)
                hg_norm(i)
                sm_din(i)
                next_slab(2)
                sm_seg(i, 0)
                sm_seg(i, 1)
                sm_kv(i, 0)
                sm_diag(i, 0)
                sm_seg(i, 2)
                sm_diag(i, 1)
                sm_seg(i, 3)
                next_slab(3)
                sm_kv(i, 1)
                sm_diag(i, 2)
                sm_diag(i, 3)

            hgrn_half("ssm0", 0, 0, 0)

            def mix(j):
                ssm_half("mix", j, j)
                hgrn_half("mix", j, 4, j + 1)

            loop(pe, "mix", mix)
            last_group = GROUPS - 1
            ssm_half(None, 0, last_group)

            pe.wait_ge(sem("mem_in"), 16)
            for b in range(2):
                pe.wait_ge(bank_free[b], first_tile["mssm"] // 2 + 1)
            for k in range(KT):
                if k >= 2:
                    pe.wait_ge(sem("m_T_read"), k - 1)
                for t in range(MT):
                    last = nc.tensor.transpose(bank[k % 2][:, t * P:(t + 1) * P],
                                               m_tok[:, t, k * P:(k + 1) * P], ident[:])
                last.then_inc(sem("m_T"), 1)
            sm_off(last_group)
            for k in range(KT):
                pe.wait_ge(sem("m_sq"), k + 1)
                mm(bank[2][:, 0:NM], ones[:], m_sq[:, k % 2, :], start=(k == 0), stop=(k == KT - 1))\
                    .then_inc(sem("m_ss"), 1)
            sm_norm(last_group)

            def mssm(i):
                for c in range(2):
                    gemm_slab("mssm", i, 3 * c, 2 * c, h_hi, h_lo, True, True)
                    gemm_slab("mssm", i, 3 * c + 1, 2 * c + 1, sm_hi, sm_lo, True, False, parts="sm_split")
                    gemm_slab("mssm", i, 3 * c + 2, 2 * c + 1, sm_hi, sm_lo, False, True, parts="sm_split")

            pe.wait_ge(sem("m_T_read"), KT)
            loop(pe, "mssm", mssm)

            def xa_slabs(name, i, ks):
                for k in ks:
                    if k < QT:
                        one(name, i, k)
                    else:
                        one(name, i, k, m_hi, m_lo, NM)

            def v_and_scores(h):
                pe.wait_ge(bank_free[1], tile_count("xa", h - 1, 5) + 1)
                pe.wait_ge(sem("xa_y"), 2 * h + 1)
                for c in range(QT):
                    for t in range(MT):
                        last = nc.tensor.transpose(bank[2][:, (t * QT + c) * P:(t * QT + c + 1) * P],
                                                   v_sb[:, c, t * P:(t + 1) * P], ident[:])
                last.then_inc(sem("xa_vT"), 1)
                for t in range(TT):
                    for c in range(QT):
                        last = mm(bank[4 + t][:, 0:NM], q_sb[:, c, t * P:(t + 1) * P], k_sb[:, c, :],
                                  start=(c == 0), stop=(c == QT - 1))
                    last.then_inc(sem("xa_s"), 1)

            def probs_T(h, t):
                pe.wait_ge(sem("xa_norm"), 4 * h + t + 1)
                for m in range(MT):
                    last = nc.tensor.transpose(bank[4 + t][:, m * P:(m + 1) * P],
                                               prob[:, t, m * P:(m + 1) * P], ident[:])
                last.then_inc(sem("xa_pT"), 1)

            def values(h):
                pe.wait_ge(sem("xa_p"), 4 * h + 4)
                for c in range(QT):
                    for m in range(MT):
                        last = mm(bank[2 + c][:], v_mt[:, m, c * P:(c + 1) * P], pT[:, m, :],
                                  start=(m == 0), stop=(m == MT - 1))
                    last.then_inc(sem("xa_o"), 1)

            def attend(name, i, h):
                v_and_scores(h)
                if name:
                    xa_slabs(name, i, (0,))
                probs_T(h, 0)
                probs_T(h, 1)
                if name:
                    xa_slabs(name, i, (1,))
                probs_T(h, 2)
                probs_T(h, 3)
                if name:
                    xa_slabs(name, i, (2, 3))
                values(h)
                if name:
                    xa_slabs(name, i, (4, 5))

            pe.wait_ge(sem("m_ready"), 1)
            xa_slabs("xa0", 0, range(6))
            loop(pe, "xa", lambda h: attend("xa", h, h))
            attend(None, 0, XA_HEADS - 1)

            def merge(i):
                one("merge", i, 0)
                one("merge", i, 1)
                gemm_slab("merge", i, 2, 2, hg_hi, hg_lo, True, True)
                gemm_slab("merge", i, 3, 3, xa_hi, xa_lo, True, True, parts="xa_y")

            pe.wait_ge(sem("hg_split"), KT)
            loop(pe, "merge", merge)

            pe.wait_ge(sem("x_again"), 16)
            for k in range(KT):
                b = 4 + k % 2
                if k >= 2:
                    pe.wait_ge(sem("x2_read"), k - 1)
                for t in range(TT):
                    last = nc.tensor.transpose(bank[b][:, t * P:(t + 1) * P],
                                               x_tok2[:, t, k * P:(k + 1) * P], ident[:])
                last.then_inc(sem("x2_T"), 1)

            def wout(i):
                for c in range(2):
                    gemm_slab("wout", i, c, c, mg_hi, mg_lo, True, True, parts="mg_split")

            loop(pe, "wout", wout)

            def square_sum(b, sq, squares, sums):
                for k in range(KT):
                    pe.wait_ge(sem(squares), k + 1)
                    mm(bank[b][:], ones[:], sq[:, k % 2, :], start=(k == 0), stop=(k == KT - 1))\
                        .then_inc(sem(sums), 1)

            square_sum(2, nsq, "wo_sq", "wo_ss")
            square_sum(3, nsq2, "x2_sq", "x2_ss")
            pe.wait_ge(sem("h2_ready"), 1)
            loop(pe, "up", lambda i: [one("up", i, c) for c in range(2)])
            pe.wait_ge(sem("act_ready"), FT + 1)

            def down(i):
                n = size["down"] // 2
                for c in range(2):
                    for k in range(n):
                        gemm_slab("down", i, n * c + k, c, a_hi, a_lo, k == 0, k == n - 1)

            loop(pe, "down", down)
            square_sum(2, fsq, "fo_sq", "fo_ss")
            for t in range(TT):
                for half in range(2):
                    pe.wait_ge(sem("y_ready"), KT)
                    b = 4 + (2 * t + half) % 4
                    if 2 * t + half >= 4:
                        pe.wait_ge(sem("o_copied"), 2 * t + half - 3)
                    for k in range(4):
                        last = nc.tensor.transpose(bank[b][:, k * P:(k + 1) * P],
                                                   x2[:, 4 * half + k, t * P:(t + 1) * P], ident[:])
                    last.then_inc(sem("o_T"), 1)

        @block.scalar
        def _(act):
            f = nc.scalar.activation
            ch = Chain(act, "act_chain")
            act.dma_start(conv_rows[:], conv_w[0].rearrange("k (c p) -> (k c) p", p=P)).then_inc(sem("vecs_in"), 16)
            act.wait_ge(sem("vec_zero"), 1)
            for at, n, ap in V.values():
                act.dma_start(vec_rows[at:at + n, :], ap.rearrange("(c p) -> c p", p=P)).then_inc(sem("vecs_in"), 16)
            act.dma_start(dtb_bc[:], dt_bias.to_broadcast([P, H])).then_inc(sem("dtv_in"), 16)
            act.dma_start(alog_bc[:], a_log.to_broadcast([P, H])).then_inc(sem("dtv_in"), 16)
            act.dma_start(dskip_bc[:], d_skip.to_broadcast([P, H])).then_inc(sem("dtv_in"), 16)
            act.dma_start(wdt[:], win_v[:, :, C_DT:C_DT + H]).then_inc(sem("wdt_in"), 16)

            def rstd(dst, src, n):
                ch.step(f(dst, src, ACT.Ln, scale=1.0 / n, bias=eps_col[:]))
                return f(dst, dst, ACT.Exp, scale=-0.5)

            act.wait_ge(sem("consts"), 1)
            act.wait_ge(sem("dtv_in"), 48)
            ch.step(f(alog_bc[:], alog_bc[:], ACT.Exp))
            for k in range(KT):
                act.wait_ge(sem("x_T_read"), k + 1)
                if k >= 2:
                    act.wait_ge(sem("x_ss"), k - 1)
                f(sq0[:, k % 2, :], x_ch[:, k, :], ACT.Square).then_inc(sem("x_sq"), 1)
            act.wait_ge(sem("x_ss"), KT)
            rstd(rstd0[:], bank[5][:], D).then_inc(sem("x_rstd"), 1)
            act.wait_ge(sem("lb_diff"), 1)
            f(dsk_tmp[:], dsk_tmp[:], ACT.Exp).then_inc(sem("lb_exp"), 1)
            act.wait_ge(sem("dt_abs"), 1)
            ch.step(f(dte[:], dte[:], ACT.Exp, scale=-1.0))
            f(dte[:], dte[:], ACT.Ln, bias=ones[:, 0:1]).then_inc(sem("dt_ln"), 1)
            act.wait_ge(sem("dt_mm"), 2)
            f(dout_dt[:].rearrange("p t h -> p (t h)"), bank[6][:, 0:TT * H], ACT.Exp)\
                .then_inc(sem("dout_exp"), 1)
            act.wait_ge(sem("dt_mm"), 3)
            ch.did(f(dchunk[:, 0].rearrange("p t h -> p (t h)"), bank[7][:, 0:TT * H], ACT.Exp))
            f(dchunk[:, 1].rearrange("p t h -> p (t h)"), bank[4][:, 0:TT * H], ACT.Exp)\
                .then_inc(sem("dchunk_exp"), 1)

            def read_tile(name, i, k, dst, N=T, before=None):
                if before:
                    act.wait_ge(*before)
                act.wait_ge(slab_done[k % 2], slab_count(name, i, k))
                f(dst, bank[k % 2][:, 0:N], ACT.Copy).then_inc(bank_free[k % 2], 1)

            hg_dst = (hf, hq, hi_, hog)

            def hg_sigmoids(u):
                for k, (src, name) in enumerate(((hf, "hg_sf"), (hq, "hg_sq"), (hog, "hg_sog"))):
                    if k:
                        act.wait_ge(sem("hg_sig_used"), 3 * u + k)
                    f(hsig[:], src[:], ACT.Sigmoid).then_inc(sem("hg_sig"), 1)

            def hg_exps(i):
                act.wait_ge(sem("hg_f"), i + 1)
                f(hf[:], hf[:], ACT.Ln).then_inc(sem("hg_g"), 1)
                act.wait_ge(sem("hg_b"), i + 1)
                ch.did(f(e_i[:], hb[:], ACT.Exp))
                ch.did(f(e_q[:], hd[:], ACT.Exp))
                ch.did(f(e_k[:], hd[:], ACT.Exp, scale=-1.0))
                f(e_l[:], hd2[:], ACT.Exp).then_inc(sem("hg_e"), 1)

            act.wait_ge(sem("start_done"), 1)
            for k in range(4):
                read_tile("hg0", 0, k, hg_dst[k][:])
            ch.settle()
            act.wait_ge(bank_free[1], tile_count("hg0", 0, 3) + 1)
            hg_sigmoids(0)

            def v_by_chunk(i, t):
                for c in range(BC):
                    p = c * HG_CHUNK
                    last = f(v_blk[p:p + HG_CHUNK, t % 2, c, :], v_tok[p:p + HG_CHUNK, t, :], ACT.Copy)
                    if c < BC - 1:
                        ch.did(last)
                last.then_inc(sem("hg_vblk"), 1)

            def sm_squares(i):
                act.wait_ge(sem("sm_y"), i + 1)
                ch.did(f(ssq[:], sy[:, 0, :], ACT.Square))
                f(din[:, 0, :], sy[:, 1, :], ACT.Square).then_inc(sem("sm_sq"), 2)

            def sm_rstd(i):
                act.wait_ge(sem("sm_n"), i + 1)
                rstd(srs[:], bank[6][:], GT * P).then_inc(sem("sm_rs"), 1)

            def hgrn_half(name, j, base, i):
                hg_exps(i)
                act.wait_ge(sem("hg_e"), i + 1)
                if base:
                    sm_squares(i - 1)
                for k in range(2):
                    read_tile(name, j, base + k, zs[:, k, :])
                if base:
                    sm_rstd(i - 1)
                for k in range(2):
                    if k:
                        act.wait_ge(sem("sm_z"), 2 * i + k)
                    act.wait_ge(bank_free[1], tile_count(name, j, base + 1) + 1)
                    f(zsig[:], zs[:, k, :], ACT.Sigmoid).then_inc(sem("sm_zsig"), 1)

                def conv_in(k):
                    before = (sem("sm_cv"), 4 * i + k) if k else None
                    read_tile(name, j, base + 2 + k, xpad[:, 3:3 + T], before=before)

                def conv_sig(k):
                    act.wait_ge(sem("sm_cv"), 4 * i + k + 1)
                    if k:
                        act.wait_ge(sem("sm_cx"), 3 * i + k)
                    else:
                        act.wait_ge(sem("sm_z"), 2 * i + 2)
                    f(csig[:], cv[:, k, :], ACT.Sigmoid).then_inc(sem("sm_csig"), 1)

                conv_in(0)
                act.wait_ge(sem("hg_T"), i + 1)
                ch.did(f(v_tok[:].rearrange("p t c -> p (t c)"), bank[2][:], ACT.Copy))
                f(ki_tok[:].rearrange("p t c -> p (t c)"), bank[3][:], ACT.Copy).then_inc(sem("hg_tok"), 1)
                act.wait_ge(sem("hg_tok"), i + 1)
                v_by_chunk(i, 0)
                v_by_chunk(i, 1)
                conv_sig(0)
                conv_in(1)
                act.wait_ge(sem("hg_kv"), 4 * i + 1)
                v_by_chunk(i, 2)
                conv_sig(1)
                conv_in(2)
                act.wait_ge(sem("hg_kv"), 4 * i + 2)
                v_by_chunk(i, 3)
                conv_sig(2)
                conv_in(3)
                conv_sig(3)

            def ssm_half(name, j, i):
                if name:
                    read_tile(name, j, 0, hf[:])
                act.wait_ge(sem("hg_o"), i + 1)
                f(hsig[:], bank[3][:], ACT.Square).then_inc(sem("hg_osq"), 1)
                act.wait_ge(sem("sm_T"), i + 1)
                f(b_tok[:].rearrange("p t c -> p (t c)"), bank[6][:], ACT.Copy).then_inc(sem("sm_btok"), 1)
                if name:
                    read_tile(name, j, 1, hq[:])
                act.wait_ge(sem("hg_n"), i + 1)
                act.wait_ge(sem("sm_done"), i + 1)
                rstd(hd[:], bank[2][:], P).then_inc(sem("hg_rs"), 1)
                act.wait_ge(sem("sm_cum"), i + 1)
                ch.did(f(din[:, 0, :], bank[6][:], ACT.Exp))
                f(din[:, 1, :], bank[7][:], ACT.Exp).then_inc(sem("sm_din"), 1)

                def decay(t):
                    act.wait_ge(sem("sm_seg"), 4 * i + t + 1)
                    if t >= 2:
                        act.wait_ge(sem("sm_yd"), 4 * i + t - 1)
                    f(ldec[:, t % 2].rearrange("p h t -> p (h t)"), bank[6 + t % 2][:], ACT.Exp)\
                        .then_inc(sem("sm_ldec"), 1)

                decay(0)
                decay(1)
                if name:
                    read_tile(name, j, 2, hi_[:])
                decay(2)
                decay(3)
                if name:
                    read_tile(name, j, 3, hog[:], before=(sem("hg_y"), i + 1))
                    act.wait_ge(bank_free[1], tile_count(name, j, 3) + 1)
                    hg_sigmoids(i + 1)

            hgrn_half("ssm0", 0, 0, 0)

            def mix(j):
                ssm_half("mix", j, j)
                hgrn_half("mix", j, 4, j + 1)

            loop(act, "mix", mix, ch)
            last_group = GROUPS - 1
            ssm_half(None, 0, last_group)

            for k in range(KT):
                act.wait_ge(sem("m_T_read"), k + 1)
                if k >= 2:
                    act.wait_ge(sem("m_ss"), k - 1)
                f(m_sq[:, k % 2, :], m_ch[:, k, :], ACT.Square).then_inc(sem("m_sq"), 1)
            sm_squares(last_group)
            act.wait_ge(sem("m_ss"), KT)
            rstd(m_rstd[:], bank[2][:, 0:NM], D).then_inc(sem("m_rs"), 1)
            sm_rstd(last_group)
            act.wait_ge(sem("sm_done"), GROUPS + 1)
            for k in range(INNER // P):
                f(sm_hi[:, k, :], y_ssm[:, k, :], ACT.Copy).then_inc(sem("sm_hi_ready"), 1)

            def gated(name, i, k, t, dst, user):
                act.wait_ge(slab_done[k % 2], slab_count(name, i, k))
                act.wait_ge(bank_free[user % 2], tile_count(name, i, user) - 1)
                f(dst[:], bank[t % 2][:], ACT.Sigmoid).then_inc(bank_free[t % 2], 1)

            def mssm(i):
                gated("mssm", i, 0, 0, sm_gate[0], 1)
                gated("mssm", i, 3, 2, sm_gate[1], 3)

            loop(act, "mssm", mssm, ch)

            xa_dst = [(t, c, n) for t, n in ((q_sb, T), (k_sb, NM), (v_sb, NM)) for c in range(QT)]

            def xa_in(name, i, ks):
                for k in ks:
                    t, c, n = xa_dst[k]
                    read_tile(name, i, k, t[:, c, :], n)

            def attend(name, i, h):
                act.wait_ge(sem("xa_vT"), h + 1)
                ch.did(f(v_mt[:].rearrange("p m c -> p (m c)"), bank[2][:], ACT.Copy))
                for t in range(TT):
                    act.wait_ge(sem("xa_max"), 4 * h + t + 1)
                    f(prob[:, t, :], bank[4 + t][:, 0:NM], ACT.Exp, scale=SCALE,
                      bias=st_max[:, t:t + 1], accum_out=st_sum[:, t:t + 1]).then_inc(sem("xa_exp"), 1)
                if name:
                    xa_in(name, i, range(6))

            xa_in("xa0", 0, range(6))
            act.wait_ge(slab_done[1], first["xa0"] // 2)
            for k in range(KT):
                f(hg_hi[:, k, :], y_hg[:, k, :], ACT.Copy).then_inc(sem("hg_hi_ready"), 1)
            loop(act, "xa", lambda h: attend("xa", h, h), ch)
            attend(None, 0, XA_HEADS - 1)

            def merge(i):
                gated("merge", i, 0, 0, gate[0], 2)
                gated("merge", i, 1, 1, gate[1], 3)

            loop(act, "merge", merge, ch)
            for k in range(KT):
                if k == 0:
                    act.wait_ge(bank_free[1], tile_count("wout", KT // 2 - 1, 1) + 1)
                if k >= 2:
                    act.wait_ge(sem("wo_ss"), k - 1)
                f(nsq[:, k % 2, :], wo[:, k, :], ACT.Square).then_inc(sem("wo_sq"), 1)
            act.wait_ge(sem("wo_ss"), KT)
            rstd(nrs[:], bank[2][:], D).then_inc(sem("wo_rs"), 1)
            for k in range(KT):
                act.wait_ge(sem("x2_new"), k + 1)
                if k >= 2:
                    act.wait_ge(sem("x2_ss"), k - 1)
                f(nsq2[:, k % 2, :], x2[:, k, :], ACT.Square).then_inc(sem("x2_sq"), 1)
            act.wait_ge(sem("x2_ss"), KT)
            rstd(nrs2[:], bank[3][:], D).then_inc(sem("x2_rs"), 1)

            def up(i):
                act.wait_ge(slab_done[0], slab_count("up", i, 0))
                act.wait_ge(bank_free[0], tile_count("up", i, 0))
                f(up_sig[:], bank[0][:], ACT.Sigmoid).then_inc(sem("up_sg"), 1)

            act.wait_ge(sem("h2_ready"), 1)
            loop(act, "up", up, ch)
            for k in range(KT):
                if k == 0:
                    act.wait_ge(bank_free[1], tile_count("down", KT // 2 - 1, 1) + 1)
                if k >= 2:
                    act.wait_ge(sem("fo_ss"), k - 1)
                f(fsq[:, k % 2, :], fo[:, k, :], ACT.Square).then_inc(sem("fo_sq"), 1)
            act.wait_ge(sem("fo_ss"), KT)
            ch.settle()
            rstd(frs[:], bank[2][:], D).then_inc(sem("fo_rs"), 1)
            for n in range(2 * TT):
                act.wait_ge(sem("o_T"), n + 1)
                f(o_tok[:, n // 2, (n % 2) * 512:(n % 2 + 1) * 512], bank[4 + n % 4][:], ACT.Copy)\
                    .then_inc(sem("o_copied"), 1)

        @block.vector
        def _(dve):
            v = nc.vector
            TTO, TS, STT = v.tensor_tensor, v.tensor_scalar, v.scalar_tensor_tensor
            ch = Chain(dve, "dve_chain")

            def split(hi, lo, src, w=None):
                ch.step(TS(hi, src, 1.0 if w is None else w, None, ALU.mult))
                if w is None:
                    return TTO(lo, src, hi.bitcast(F32), ALU.subtract)
                return STT(lo, src, w, hi.bitcast(F32), ALU.mult, ALU.subtract)

            v.memset(vec_rows[:], 0.0).then_inc(sem("vec_zero"), 1)
            dve.wait_ge(sem("wdt_in"), 16)
            ch.did(split(wdt_hi[:], wdt_lo[:], wdt[:]))
            dve.wait_ge(sem("vecs_T"), 1)
            ch.did(v.tensor_copy(conv_ch[:], bank[2][:, 0:P]))
            ch.step(v.tensor_copy(vec_ch[:], bank[2][:, P:2 * P]))
            for k in range(KT):
                dve.wait_ge(sem("x_T"), k + 1)
                v.tensor_copy(x_ch[:, k, :], bank[3 + k % 2][:]).then_inc(sem("x_T_read"), 1)
            a0, n0, _ = V["lb0"]
            a1, _, _ = V["lb1"]
            dve.wait_ge(sem("consts"), 1)
            ch.step(TTO(lb[:], vec_ch[:, a0:a0 + KT], vec_ch[:, a1:a1 + KT], ALU.subtract))
            ch.step(TS(one_lb[:], lb[:], -1.0, None, ALU.mult))
            TTO(dsk_tmp[:], lb[:], one_lb[:], ALU.min).then_inc(sem("lb_diff"), 1)
            dve.wait_ge(sem("x_rstd"), 1)
            for k in range(KT):
                ch.step(TTO(scaled0[:, k % 2, :], x_ch[:, k, :], rstd0[:], ALU.mult))
                last = split(h_hi[:, k, :], h_lo[:, k, :], scaled0[:, k % 2, :], vcol("pre", k))
                if k < KT - 1:
                    ch.did(last)
                else:
                    last.then_inc(sem("h_ready"), 1)
            dve.wait_ge(sem("lb_exp"), 1)
            ch.step(TS(one_lb[:], dsk_tmp[:], 1.0, None, ALU.add))
            ch.step(v.reciprocal(one_lb[:], one_lb[:]))
            ch.step(TTO(dsk_tmp[:], dsk_tmp[:], one_lb[:], ALU.mult))
            ch.step(TS(lb[:], lb[:], 0.0, None, ALU.is_ge))
            ch.step(TTO(one_lb[:], one_lb[:], dsk_tmp[:], ALU.subtract))
            ch.step(TTO(lb[:], lb[:], one_lb[:], ALU.mult))
            ch.step(TTO(lb[:], lb[:], dsk_tmp[:], ALU.add))
            ch.step(TS(one_lb[:], lb[:], -1.0, 1.0, ALU.mult, ALU.add))
            dve.wait_ge(sem("dtv_in"), 48)
            for o in range(2):
                ch.step(v.tensor_copy(dskip_ch[64 * o:64 * o + 64, :],
                                      dskip_bc[64 * o:64 * o + 64, :].rearrange("p (c o) -> p o c", o=2)[:, o, :]))
            dve.wait_ge(sem("dt_mm"), 1)
            ch.step(TTO(dtx[:], bank[6][:, 0:TT * H].rearrange("p (t h) -> p t h", h=H),
                        dtb_bc[:].unsqueeze(1).to_broadcast([P, TT, H]), ALU.add))
            ch.step(TS(dte[:], dtx[:], -1.0, None, ALU.mult))
            TTO(dte[:], dte[:], dtx[:], ALU.max).then_inc(sem("dt_abs"), 1)
            dve.wait_ge(sem("dt_ln"), 1)
            ch.step(STT(dt_tok[:], dtx[:], 0.0, dte[:], ALU.max, ALU.add))
            STT(dta[:], dt_tok[:], -1.0, alog_bc[:].unsqueeze(1).to_broadcast([P, TT, H]),
                ALU.mult, ALU.mult).then_inc(sem("dta_ready"), 1)
            dve.wait_ge(sem("dout_exp"), 1)
            ch.step(TTO(dout_dt[:], dout_dt[:], dt_tok[:], ALU.mult))
            dve.wait_ge(sem("dchunk_exp"), 1)
            dve.wait_ge(sem("dta_ready"), 1)
            for name in ("sm_done", "xa_y", "act_ready"):
                dve.sem_inc(sem(name), 1)
            for t in (hgA, v_blk, hgS, smS, cbm):
                ch.step(v.memset(t[:], 0.0))
            v.memset(xpad[:], 0.0).then_inc(sem("start_done"), 1)
            dve.wait_ge(sem("start_done"), 1)

            def chunked(t):
                return t[:].rearrange("p (c l) -> p c l", l=HG_CHUNK)

            def hg_pre(u):
                dve.wait_ge(sem("hg_sig"), 3 * u + 1)
                TS(hf[:], hsig[:], one_lb[:, bass.ds(u, 1)], lb[:, bass.ds(u, 1)], ALU.mult, ALU.add)\
                    .then_inc(sem("hg_sig_used"), 1)
                dve.wait_ge(sem("hg_sig_used"), 3 * u + 1)
                TS(hk[:], hf[:], -1.0, 1.0, ALU.mult, ALU.add).then_inc(sem("hg_f"), 1)
                dve.wait_ge(sem("hg_sig"), 3 * u + 2)
                TTO(hq[:], hq[:], hsig[:], ALU.mult).then_inc(sem("hg_sig_used"), 1)
                dve.wait_ge(sem("hg_sig"), 3 * u + 3)
                TTO(hog[:], hog[:], hsig[:], ALU.mult).then_inc(sem("hg_sig_used"), 1)

            hg_pre(0)
            ch.settle()

            def sm_y(i):
                dve.wait_ge(sem("sm_yo"), i + 1)
                for c in range(GT):
                    y = sy[:, c, :]
                    ch.step(TTO(y, bank[6 + c][:], din[:, c, :], ALU.mult))
                    ch.step(TTO(y, y, bank[4 + c][:], ALU.add))
                    ch.step(STT(y, cv[:, c, :], dskip_ch[:, bass.ds(2 * i + c, 1)], y, ALU.mult, ALU.add))
                    last = TTO(y, y, zs[:, c, :], ALU.mult)
                    if c == 0:
                        ch.did(last)
                last.then_inc(sem("sm_y"), 1)

            def sm_final(i):
                dve.wait_ge(sem("sm_rs"), i + 1)
                for c in range(GT):
                    last = STT(flat(y_ssm, 2 * i + c), sy[:, c, :], vcol("ssm", 2 * i + c), srs[:],
                               ALU.mult, ALU.mult)
                    if c == 0:
                        ch.did(last)
                last.then_inc(sem("sm_done"), 1)

            def hgrn_half(name, j, base, i):
                dve.wait_ge(sem("hg_g"), i + 1)
                ch.step(v.tensor_tensor_scan(hb[:], hg_start[:], hf[:], 0.0, ALU.mult, ALU.add))
                b3 = chunked(hb)
                ref = b3[:, :, HG_CHUNK // 2:HG_CHUNK // 2 + 1].to_broadcast([P, HC, HG_CHUNK])
                lst = b3[:, :, HG_CHUNK - 1:HG_CHUNK].to_broadcast([P, HC, HG_CHUNK])
                dve.wait_ge(sem("hg_sig_used"), 3 * i + 3)
                ch.did(TTO(chunked(hd), b3, ref, ALU.subtract))
                TTO(chunked(hd2), lst, b3, ALU.subtract).then_inc(sem("hg_b"), 1)
                if base:
                    sm_y(i - 1)
                dve.wait_ge(sem("hg_e"), i + 1)
                ch.step(v.tensor_copy(hdc[:].unsqueeze(2), chunked(e_i)[:, :, HG_CHUNK - 1:HG_CHUNK]))
                ch.did(TTO(e_i[:], e_i[:], hq[:], ALU.mult))
                ch.did(TTO(e_q[:], e_q[:], hq[:], ALU.mult))
                ch.did(TTO(e_k[:], e_k[:], hk[:], ALU.mult))
                TTO(e_l[:], e_l[:], hk[:], ALU.mult).then_inc(sem("hg_pre"), 1)
                if base:
                    sm_final(i - 1)
                for k in range(2):
                    dve.wait_ge(sem("sm_zsig"), 2 * i + k + 1)
                    TTO(zs[:, k, :], zs[:, k, :], zsig[:], ALU.mult).then_inc(sem("sm_z"), 1)

                def conv(k, ct):
                    dve.wait_ge(bank_free[k % 2], tile_count(name, j, base + 2 + k) + 1)

                    def tap(n):
                        return conv_ch[:, bass.ds(n * (CONV // P) + ct, 1)]
                    ch.step(TS(cv[:, k, :], xpad[:, 0:T], tap(0), vcol("cb", ct), ALU.mult, ALU.add))
                    for n in range(1, TAPS):
                        last = STT(cv[:, k, :], xpad[:, n:n + T], tap(n), cv[:, k, :], ALU.mult, ALU.add)
                        if n < TAPS - 1:
                            ch.step(last)
                    last.then_inc(sem("sm_cv"), 1)

                def conv_silu(k):
                    dve.wait_ge(sem("sm_csig"), 4 * i + k + 1)
                    TTO(cv[:, k, :], cv[:, k, :], csig[:], ALU.mult).then_inc(sem("sm_cx" if k < 3 else "sm_conv"), 1)

                def hg_states(t):
                    dve.wait_ge(sem("hg_kv"), 4 * i + t + 1)
                    b = 3 - t % 2
                    steps = BC if t < TT - 1 else BC - 1
                    for c in range(steps):
                        n = t * BC + c
                        ins = STT(hgS[:, n + 1, :], hgS[:, n, :], hdc[:, n:n + 1],
                                  bank[b][:, c * P:(c + 1) * P], ALU.mult, ALU.add)
                        if c < steps - 1:
                            ch.step(ins)
                    ins.then_inc(sem("hg_state"), 1)
                    dve.wait_ge(sem("hg_state"), 4 * i + t + 1)

                conv(0, 2 * i)
                wait_alone(dve, sem("hg_A"), i + 1)
                v.copy_predicated(hgA[:], hg_mask[:].bitcast(U32).unsqueeze(1).to_broadcast([P, TT, P]), tiles(2))\
                    .then_inc(sem("hg_masked"), 1)
                conv_silu(0)
                hg_states(0)
                conv(1, 2 * i + 1)
                conv_silu(1)
                hg_states(1)
                hg_states(2)
                conv(2, 2 * GROUPS + i)
                conv_silu(2)
                conv(3, 3 * GROUPS + i)
                hg_states(3)
                conv_silu(3)

            def ssm_half(name, j, i):
                cols = bass.ds(i * HPG, HPG)
                ch.did(v.tensor_copy(g_dta[:], dta[:, :, cols]))
                ch.did(v.tensor_copy(g_dt[:], dt_tok[:, :, cols]))
                ch.did(v.tensor_copy(g_do[:], dout_dt[:, :, cols]))
                ch.did(v.tensor_copy(g_dc[:], dchunk[:, :, :, cols]))
                ch.settle()
                ch.did(v.tensor_copy(dta_rep.rearrange("p t (h d) -> p t h d", d=HD),
                                     g_dta[:].unsqueeze(3).to_broadcast([P, TT, HPG, HD])))
                wait_alone(dve, sem("sm_cb"), i + 1)
                v.copy_predicated(cbm[:], cum_mask[:].bitcast(U32).unsqueeze(1).to_broadcast([P, TT, P]), tiles(7))\
                    .then_inc(sem("sm_masked"), 1)

                def u_dta(t):
                    if t >= 2:
                        dve.wait_ge(sem("sm_seg"), 4 * i + t - 1)
                    TTO(udta[:, t % 2], cum_mask[:].unsqueeze(1).to_broadcast([P, HPG, P]),
                        g_dta[:, t, :].unsqueeze(2).to_broadcast([P, HPG, P]), ALU.mult)\
                        .then_inc(sem("sm_udta"), 1)

                def decay_cb(t):
                    dve.wait_ge(sem("sm_ldec"), 4 * i + t + 1)
                    TTO(ldec[:, t % 2], ldec[:, t % 2], cbm[:, t, :].unsqueeze(1).to_broadcast([P, HPG, P]),
                        ALU.mult).then_inc(sem("sm_M"), 1)

                def by_head(dst, g, c):
                    return TTO(dst[:, c].rearrange("p t (h d) -> p t h d", d=HD),
                               bank[4 + c][:].rearrange("p (t h d) -> p t h d", t=TT, d=HD),
                               g[:, :, 2 * c:2 * c + 2].unsqueeze(3).to_broadcast([P, TT, 2, HD]), ALU.mult)

                def states(half):
                    dve.wait_ge(sem("sm_kv"), 2 * i + half + 1)
                    for c in range(4 * half, 4 * half + 4 - half):
                        q = (c // 2) % 2 * HPG * HD
                        src = bank[2 + c % 2][:, q:q + HPG * HD]
                        if c == 0:
                            ch.step(v.tensor_copy(smS[:, 1, :], src))
                            continue
                        ch.step(TTO(smT.rearrange("p (h d) -> p h d", d=HD),
                                    smS[:, c, :].rearrange("p (h d) -> p h d", d=HD),
                                    g_dc[:, c % 2, c // 2, :].unsqueeze(2).to_broadcast([P, HPG, HD]), ALU.mult))
                        last = TTO(smS[:, c + 1, :], smT, src, ALU.add)
                        if c < 4 * half + 3 - half:
                            ch.step(last)
                    last.then_inc(sem("sm_state"), 1)
                    dve.wait_ge(sem("sm_state"), 2 * i + half + 1)

                u_dta(0)
                u_dta(1)
                dve.wait_ge(sem("hg_rs"), i + 1)
                ch.step(TTO(ho[:], bank[3][:], hd[:], ALU.mult))
                STT(flat(y_hg, i), ho[:], vcol("hg", i), hog[:], ALU.mult, ALU.mult).then_inc(sem("hg_y"), 1)
                for c in range(GT):
                    ch.did(by_head(xdt, g_dt, c))
                dve.wait_ge(sem("sm_cum"), i + 1)
                ch.did(by_head(xdo, g_do, 0))
                by_head(xdo, g_do, 1).then_inc(sem("sm_xdo"), 1)
                decay_cb(0)
                u_dta(2)
                decay_cb(1)
                u_dta(3)
                states(0)
                decay_cb(2)
                decay_cb(3)
                states(1)
                if name:
                    hg_pre(i + 1)

            def flat(t, i):
                return t[:, bass.ds(i, 1), :].rearrange("p a t -> p (a t)")

            hgrn_half("ssm0", 0, 0, 0)

            def mix(j):
                ssm_half("mix", j, j)
                hgrn_half("mix", j, 4, j + 1)

            loop(dve, "mix", mix, ch)
            last_group = GROUPS - 1
            ssm_half(None, 0, last_group)
            dve.wait_ge(sem("hg_y"), GROUPS)
            for k in range(KT):
                dve.wait_ge(sem("m_T"), k + 1)
                v.tensor_copy(m_ch[:, k, :], bank[k % 2][:, 0:NM]).then_inc(sem("m_T_read"), 1)
            sm_y(last_group)
            sm_final(last_group)
            dve.wait_ge(sem("sm_done"), GROUPS + 1)
            ch.restart()
            for k in range(INNER // P):
                dve.wait_ge(sem("sm_hi_ready"), k + 1)
                TTO(sm_lo[:, k, :], y_ssm[:, k, :], sm_hi[:, k, :].bitcast(F32), ALU.subtract)\
                    .then_inc(sem("sm_split"), 1)
            dve.wait_ge(sem("m_rs"), 1)
            dve.wait_ge(sem("m_T_read"), KT)
            for k in range(KT):
                ch.step(TTO(m_ch[:, k, :], m_ch[:, k, :], m_rstd[:], ALU.mult))
                last = split(m_hi[:, k, :], m_lo[:, k, :], m_ch[:, k, :], vcol("mem", k))
                if k < KT - 1:
                    ch.did(last)
            last.then_inc(sem("m_ready"), 1)
            dve.wait_ge(sem("sm_split"), INNER // P)

            def mssm(i):
                for c in range(2):
                    k, t = 3 * c + 2, 2 * c + 1
                    dve.wait_ge(slab_done[k % 2], slab_count("mssm", i, k))
                    dve.wait_ge(bank_free[0], tile_count("mssm", i, t - 1) + 1)
                    TTO(flat(merged, 2 * i + c), bank[1][:], sm_gate[c][:], ALU.mult).then_inc(bank_free[1], 1)

            loop(dve, "mssm", mssm, ch)

            for k in range(KT):
                dve.wait_ge(sem("hg_hi_ready"), k + 1)
                TTO(hg_lo[:, k, :], y_hg[:, k, :], hg_hi[:, k, :].bitcast(F32), ALU.subtract)\
                    .then_inc(sem("hg_split"), 1)

            def probs_in(h, t):
                dve.wait_ge(sem("xa_pT"), 4 * h + t + 1)
                v.tensor_copy(pT[:, :, t * P:(t + 1) * P],
                              bank[4 + t][:, 0:NM].rearrange("p (m t) -> p m t", t=P)).then_inc(sem("xa_p"), 1)

            def attend(name, i, h):
                for t in range(TT):
                    dve.wait_ge(sem("xa_s"), 4 * h + t + 1)
                    ch.step(v.reduce_max(st_inv[:, t:t + 1], bank[4 + t][:, 0:NM], mybir.AxisListType.X))
                    TS(st_max[:, t:t + 1], st_inv[:, t:t + 1], -SCALE, None, ALU.mult).then_inc(sem("xa_max"), 1)
                for t in range(TT):
                    dve.wait_ge(sem("xa_exp"), 4 * h + t + 1)
                    ch.step(v.reciprocal(st_inv[:, t:t + 1], st_sum[:, t:t + 1]))
                    TS(prob[:, t, :], prob[:, t, :], st_inv[:, t:t + 1], None, ALU.mult).then_inc(sem("xa_norm"), 1)
                for t in range(TT):
                    probs_in(h, t)
                for c in range(QT):
                    dve.wait_ge(sem("xa_o"), 2 * h + c + 1)
                    dve.wait_ge(sem("xa_y"), 2 * h + c + 1)
                    ch.step(v.tensor_copy(xo[:], bank[2 + c][:]))
                    split(flat(xa_hi, 2 * h + c), flat(xa_lo, 2 * h + c), xo[:]).then_inc(sem("xa_y"), 1)

            loop(dve, "xa", lambda h: attend("xa", h, h), ch)
            attend(None, 0, XA_HEADS - 1)
            dve.wait_ge(sem("xa_y"), 2 * XA_HEADS + 1)

            def merge(i):
                for c in range(2):
                    dve.wait_ge(slab_done[c], slab_count("merge", i, 2 + c))
                    dve.wait_ge(bank_free[c], tile_count("merge", i, c) + 1)
                    TTO(part[:, c, :], bank[c][:], gate[c][:], ALU.mult).then_inc(bank_free[c], 1)
                    dve.wait_ge(bank_free[c], tile_count("merge", i, 2 + c) + 1)
                    ch.step(TTO(part[:, 0, :], part[:, c, :], flat(merged, i) if c == 0 else part[:, 0, :], ALU.add))
                split(flat(mg_hi, i), flat(mg_lo, i), part[:, 0, :]).then_inc(sem("mg_split"), 1)
                wait_alone(dve, sem("mg_split"), i + 1)

            loop(dve, "merge", merge, ch)
            for k in range(KT):
                dve.wait_ge(sem("x2_T"), k + 1)
                v.tensor_copy(x2[:, k, :], bank[4 + k % 2][:]).then_inc(sem("x2_read"), 1)

            def copy_out(name, dst):
                def body(i):
                    n = size[name] // 2
                    for c in range(2):
                        k = n * c + n - 1
                        dve.wait_ge(slab_done[k % 2], slab_count(name, i, k))
                        TS(flat(dst, 2 * i + c), bank[c][:], 1.0, None, ALU.mult).then_inc(bank_free[c], 1)
                return body

            loop(dve, "wout", copy_out("wout", wo), ch)
            dve.wait_ge(sem("wo_rs"), 1)
            dve.wait_ge(sem("x2_read"), KT)
            for k in range(KT):
                ch.step(TTO(nsc[:, k % 2, :], wo[:, k, :], nrs[:], ALU.mult))
                STT(x2[:, k, :], nsc[:, k % 2, :], vcol("post", k), x2[:, k, :], ALU.mult, ALU.add)\
                    .then_inc(sem("x2_new"), 1)
            dve.wait_ge(sem("x2_rs"), 1)
            dve.wait_ge(sem("x2_new"), KT)
            for k in range(KT):
                ch.step(TTO(nsc[:, k % 2, :], x2[:, k, :], nrs2[:], ALU.mult))
                last = split(h_hi[:, k, :], h_lo[:, k, :], nsc[:, k % 2, :], vcol("fpre", k))
                if k < KT - 1:
                    ch.did(last)
            last.then_inc(sem("h2_ready"), 1)
            dve.wait_ge(sem("h2_ready"), 1)

            def up(i):
                dve.wait_ge(sem("act_ready"), i + 1)
                dve.wait_ge(sem("up_sg"), i + 1)
                TTO(up_a[:], bank[0][:], up_sig[:], ALU.mult).then_inc(bank_free[0], 1)
                dve.wait_ge(bank_free[0], tile_count("up", i, 0) + 1)
                dve.wait_ge(slab_done[1], slab_count("up", i, 1))
                TTO(up_a[:], up_a[:], bank[1][:], ALU.mult).then_inc(bank_free[1], 1)
                dve.wait_ge(bank_free[1], tile_count("up", i, 1) + 1)
                split(flat(a_hi, i), flat(a_lo, i), up_a[:]).then_inc(sem("act_ready"), 1)

            loop(dve, "up", up, ch)
            dve.wait_ge(sem("act_ready"), FT + 1)
            loop(dve, "down", copy_out("down", fo), ch)
            dve.wait_ge(bank_free[1], tile_count("down", KT // 2 - 1, 1) + 1)
            dve.wait_ge(sem("fo_rs"), 1)
            for k in range(KT):
                ch.step(TTO(fsc[:, k % 2, :], fo[:, k, :], frs[:], ALU.mult))
                STT(x2[:, k, :], fsc[:, k % 2, :], vcol("fpost", k), x2[:, k, :], ALU.mult, ALU.add)\
                    .then_inc(sem("y_ready"), 1)


_OUT = (1, 512, 1024)


def kernel(**inputs):
    import numpy as np
    import concourse.bacc as bacc
    from concourse.bass_utils import run_bass_kernel_spmd as run

    nc = bacc.Bacc("TRN2", target_bir_lowering=False, num_devices=1)
    arrays, args = {}, {}
    for name, value in inputs.items():
        a = np.ascontiguousarray(value)
        arrays[f"in_{name}"] = a
        args[name] = nc.dram_tensor(f"in_{name}", a.shape, mybir.dt.from_np(a.dtype), kind="ExternalInput").ap()
    args["out"] = nc.dram_tensor("out_0", _OUT, F32, kind="ExternalOutput").ap()
    hybrid_layer(nc, **args)
    result = run(nc, [arrays], core_ids=[0])
    return result.results[0]["out_0"]
```

```python
from contextlib import ExitStack

import concourse.bass as bass
from concourse import mybir

ALU = mybir.AluOpType
ACT = mybir.ActivationFunctionType
F32 = mybir.dt.float32
F32R = mybir.dt.float32r
U32 = mybir.dt.uint32

P = 128
KB = 1024
EPS = 1e-6
HG_CHUNK = 32
SSM_CHUNK = 64
GROUPS = 8
XA_HEADS = 4


def hybrid_layer(nc, x, mem, norm_mix_pre, norm_mix_post, norm_ffn_pre, norm_ffn_post, norm_mem,
                 w_in, hg_lb_param, hg_norm_w, conv_w, conv_b, dt_bias, a_log, d_skip,
                 ssm_norm_w, w_mem_kv, w_br_hg, w_br_ssm, w_br_xa, w_out, w_ffn_up, w_ffn_down, out):
    T, D = x.shape[1], x.shape[2]
    NM = mem.shape[1]
    HG = hg_norm_w.shape[1]
    INNER = ssm_norm_w.shape[1]
    CONV = conv_b.shape[1]
    TAPS = conv_w.shape[1]
    H = dt_bias.shape[1]
    FF = w_ffn_down.shape[1]
    KT = D // P
    TT = T // P
    NC = T // SSM_CHUNK
    HC = T // HG_CHUNK
    BC = P // HG_CHUNK
    HPG = H // GROUPS
    HD = INNER // H
    GT = INNER // GROUPS // P
    MT = NM // P
    QT = D // XA_HEADS // P
    FT = FF // P
    SCALE = float(D // XA_HEADS) ** -0.5
    assert T == 512 and D == 1024 and HG == D and HPG * HD == 2 * P and GT == 2 and QT == 2 and MT == 2

    C_Q, C_F, C_I, C_OG = 0, HG, 2 * HG, 3 * HG
    C_Z = 4 * HG
    C_XS = C_Z + INNER
    C_B = C_XS + INNER
    C_C = C_B + GROUPS * P
    C_DT = C_XS + CONV
    C_XQ = C_DT + H
    C_G = C_XQ + D

    with ExitStack() as ctx:
        base = -(-nc.sbuf_base // 32) * 32
        arena = ctx.enter_context(nc.sbuf_tensor("arena", [P, (207 * KB) // 4], F32))

        class Region:
            def __init__(self, start, size):
                self.at, self.end = base + start * KB, base + (start + size) * KB

            def __call__(self, name, shape, dt=F32):
                n = 4
                for s in shape[1:]:
                    n *= s
                t = nc.alloc_sbuf_tensor_at(name, shape, dt, offset=self.at)
                self.at += -(-n // 32) * 32
                assert self.at <= self.end, (name, self.at - self.end)
                return t

        RINGS, ACTS, SSM_OUT, HG_OUT, SCR, END = 9, 33, 65, 97, 113, 207
        const = Region(0, RINGS)
        rings = Region(RINGS, ACTS - RINGS)
        acts = Region(ACTS, SSM_OUT - ACTS)
        ssm_out = Region(SSM_OUT, HG_OUT - SSM_OUT)
        hg_out = Region(HG_OUT, SCR - HG_OUT)

        ident = const("ident", [P, P])
        ones = const("ones", [P, P])
        hg_mask = const("hg_mask", [P, P])
        cum_mask = const("cum_mask", [P, P])
        after_mask = const("after_mask", [P, P])
        hg_start = const("hg_start", [P, T])
        conv_ch = const("conv_ch", [P, TAPS * CONV // P])
        vec_ch = const("vec_ch", [P, P])
        lb = const("lb", [P, KT])
        one_lb = const("one_lb", [P, KT])
        dskip_ch = const("dskip_ch", [P, INNER // P])
        dt_tok = const("dt_tok", [P, TT, H])
        dta = const("dta", [P, TT, H])
        dout_dt = const("dout_dt", [P, TT, H])
        dchunk = const("dchunk", [P, 2, TT, H])
        eps_col = const("eps_col", [P, 1])
        zero_col = const("zero_col", [P, 1])
        hdc = const("hdc", [P, HC])
        col_ss = const("col_ss", [P, 5, TT])
        col_rs = const("col_rs", [P, 5, TT])

        raw = rings("raw", [P, 2, KT, P])
        w_hi = [rings(f"w_hi{s}", [P, KT, P], F32R) for s in range(2)]
        w_lo = [rings(f"w_lo{s}", [P, KT, P], F32R) for s in range(2)]
        h_hi = acts("h_hi", [P, KT, T], F32R)
        h_lo = acts("h_lo", [P, KT, T], F32R)
        y_ssm = ssm_out("y_ssm", [P, INNER // P, T])
        y_hg = hg_out("y_hg", [P, KT, T])

        r = Region(SSM_OUT, 32)
        x_tok = r("x_tok", [P, TT, D])
        xn = r("xn", [P, 2, D])
        pre_bc = r("pre_bc", [P, D])
        sq_out0 = r("sq_out0", [P, D])
        r = Region(HG_OUT, 16)
        vec_rows = r("vec_rows", [P, P])
        conv_rows = r("conv_rows", [P, P])
        dskip_bc = r("dskip_bc", [P, H])
        dtb_bc = r("dtb_bc", [P, H])
        alog_bc = r("alog_bc", [P, H])
        wdt = r("wdt", [P, KT, H])
        wdt_hi = r("wdt_hi", [P, KT, H], F32R)
        wdt_lo = r("wdt_lo", [P, KT, H], F32R)
        dtT = r("dtT", [H, T])
        dtx = r("dtx", [P, TT, H])
        dte = r("dte", [P, TT, H])
        lb_tmp = r("lb_tmp", [P, KT])

        r = Region(SCR, END - SCR)
        hf = r("hf", [P, T])
        hq = r("hq", [P, T])
        hi_ = r("hi_", [P, T])
        hk = r("hk", [P, T])
        hb = r("hb", [P, T])
        e_k = r("e_k", [P, T])
        e_l = r("e_l", [P, T])
        ki_tok = r("ki_tok", [P, TT, P])
        hog = r("hog", [P, T])
        hsig = r("hsig", [P, T])
        hd2 = hsig
        e_q = r("e_q", [P, T])
        e_i = r("e_i", [P, T])
        v_tok = r("v_tok", [P, TT, P])
        hgA = r("hgA", [P, TT, P])
        v_blk = r("v_blk", [P, 2, BC, P])
        hgS = r("hgS", [P, HC, P])
        ho = e_q
        assert r.at == base + (SCR + 40) * KB
        zs = r("zs", [P, GT, T])
        cv = r("cv", [P, 4, T])
        xdo = r("xdo", [P, GT, TT, P])
        b_tok = r("b_tok", [P, TT, P])
        cbm = r("cbm", [P, TT, P])
        udta = r("udta", [P, 2, HPG, P])
        ldec = r("ldec", [P, 2, HPG, P])
        smS = r("smS", [P, NC, HPG * HD])
        xpad = r("xpad", [P, 516])
        g_dta = r("g_dta", [P, TT, HPG])
        g_dt = r("g_dt", [P, TT, HPG])
        g_do = r("g_do", [P, TT, HPG])
        g_dc = r("g_dc", [P, 2, TT, HPG])
        csig = r("csig", [P, T])
        xdt = r("xdt", [P, GT, TT, P])
        din = r("din", [P, GT, T])
        hd = r("hd", [P, T])
        smT = csig[:, 0:HPG * HD]
        dta_rep = xdo[:].rearrange("p c t d -> p (c t d)").rearrange("p (t d) -> p t d", d=HPG * HD)
        sy = xdt[:].rearrange("p c t d -> p c (t d)")
        ssq = csig
        zsig = csig
        srs = hd

        gates = Region(SCR, 16)("gates", [P, KT, T])
        mem_bc = Region(SCR + 8, 4)("mem_bc", [P, D])
        sq_out1 = Region(SCR + 12, 4)("sq_out1", [P, D])
        r = Region(SCR + 16, 24)
        m_hi = r("m_hi", [P, KT, NM], F32R)
        m_lo = r("m_lo", [P, KT, NM], F32R)
        m_tok = r("m_tok", [P, MT, D])
        r = Region(SCR + 40, 48)
        sm_hi = r("sm_hi", [P, INNER // P, T], F32R)
        merged = r("merged", [P, KT, T])
        sm_lo = Region(SSM_OUT, 32)("sm_lo", [P, INNER // P, T], F32R)
        hg_hi = Region(SCR, 16)("hg_hi", [P, KT, T], F32R)
        hg_lo = Region(HG_OUT, 16)("hg_lo", [P, KT, T], F32R)
        r = Region(SCR + 40, 32)
        xa_hi = r("xa_hi", [P, KT, T], F32R)
        xa_lo = r("xa_lo", [P, KT, T], F32R)
        r = Region(SSM_OUT, 24)
        q_sb = r("q_sb", [P, QT, T])
        k_sb = r("k_sb", [P, QT, NM])
        v_sb = r("v_sb", [P, QT, NM])
        v_mt = r("v_mt", [P, MT, QT * P])
        prob = r("prob", [P, TT, NM])
        st_max = r("st_max", [P, TT])
        st_sum = r("st_sum", [P, TT])
        st_inv = r("st_inv", [P, TT])
        pT = r("pT", [P, MT, T])
        xo = r("xo", [P, T])
        r = Region(SSM_OUT + 24, 8)
        gate = [r(f"gate{g}", [P, T]) for g in range(2)]
        part = r("part", [P, 2, T])
        mg_hi = Region(SCR + 16, 16)("mg_hi", [P, KT, T], F32R)
        mg_lo = Region(SSM_OUT, 16)("mg_lo", [P, KT, T], F32R)
        wo_stage = Region(SCR + 32, 8)("wo_stage", [P, 2, 2, T], F32R)
        r = Region(SSM_OUT + 16, 8)
        post_bc = r("post_bc", [P, D])
        fpre_bc = r("fpre_bc", [P, D])
        r = Region(SCR + 40, 32)
        x_tok2 = r("x_tok2", [P, TT, D])
        wo_y = r("wo_y", [P, 2, D])
        xn2 = r("xn2", [P, 2, D])
        sq_out = Region(SCR, 4)("sq_out", [P, D])
        x2 = Region(HG_OUT, 16)("x2", [P, TT, D])
        r = Region(SCR, 88)
        a_hi = r("a_hi", [P, FT, T], F32R)
        a_lo = r("a_lo", [P, FT, T], F32R)
        r = Region(SSM_OUT, 32)
        up_sig = r("up_sig", [P, T])
        up_a = r("up_a", [P, T])
        dn_stage = r("dn_stage", [P, 2, 2, T], F32R)
        fpost_bc = r("fpost_bc", [P, D])
        dn_y = r("dn_y", [P, 2, D])
        sq_out3 = r("sq_out3", [P, D])
        o_tok = Region(ACTS, 16)("o_tok", [P, TT, D])

        bank = [ctx.enter_context(nc.psum_tensor(f"bank{b}", [P, 512], F32)) for b in range(8)]

        def tiles(b, n=TT):
            return bank[b][:, 0:n * P].rearrange("p (t c) -> p t c", c=P)

        sems = {}

        def sem(name):
            if name not in sems:
                sems[name] = ctx.enter_context(nc.semaphore(name))
            return sems[name]

        def wait_alone(eng, s, value):
            eng.wait_ge(s, value)
            eng.sem_inc(sem("waits_passed"), 1)

        class Chain:

            def __init__(self, eng, name):
                self.eng, self.sem, self.n = eng, sem(name), 0

            def restart(self):
                if self.n:
                    self.settle()
                    self.eng.sem_clear(self.sem)
                self.n = 0

            def did(self, ins):
                ins.then_inc(self.sem, 1)
                self.n += 1

            def settle(self):
                self.eng.wait_ge(self.sem, self.n)

            def step(self, ins):
                self.did(ins)
                self.settle()

        def rows(w):
            return w[0].rearrange("(k p) n -> p k n", p=P)

        win_v, kv_v = rows(w_in), rows(w_mem_kv)
        bhg_v, bssm_v, bxa_v = rows(w_br_hg), rows(w_br_ssm), rows(w_br_xa)
        wo_v, up_v, down_v = rows(w_out), rows(w_ffn_up), rows(w_ffn_down)

        hg_slabs = [(win_v, C_F, P), (win_v, C_Q, P), (win_v, C_I, P), (win_v, C_OG, P)]
        ssm_slabs = [(win_v, C_Z, 2 * P), (win_v, C_Z + P, 2 * P), (win_v, C_XS, 2 * P),
                     (win_v, C_XS + P, 2 * P), (win_v, C_B, P), (win_v, C_C, P)]

        def slab(w, start, stride, k0=0, k1=KT, shift=0):
            return (w, start, stride, k0, k1, shift)

        def wide(w, row):
            return (w, row)

        xa_parts = [(win_v, C_XQ, 0), (kv_v, 0, 0), (win_v, C_XQ, 1), (kv_v, 0, 1), (kv_v, D, 0), (kv_v, D, 1)]

        SECTIONS = [
            ("hg0", 1, [slab(*s) for s in hg_slabs]),
            ("ssm0", 1, [slab(*s) for s in ssm_slabs]),
            ("mix", GROUPS - 1, [slab(*s, shift=1) for s in hg_slabs + ssm_slabs]),
            ("gates", 1, [slab(win_v, C_G + D + c * P, P) for c in range(KT)]),
            ("mssm", KT // 2, [slab(bssm_v, c * P, 2 * P, k, k + KT) for c in range(2) for k in (0, KT)]),
            ("xa0", 1, [slab(w, s + c * P, QT * P) for w, s, c in xa_parts]),
            ("xa", XA_HEADS - 1, [slab(w, s + c * P, QT * P, shift=1) for w, s, c in xa_parts]),
            ("merge", KT, [slab(win_v, C_G, P), slab(win_v, C_G + 2 * D, P),
                           slab(bhg_v, 0, P), slab(bxa_v, 0, P)]),
            ("wout0", 1, [wide(wo_v, k) for k in range(2)]),
            ("wout", KT // 2 - 2, [wide(wo_v, 2 + k) for k in range(2)]),
            ("wout1", 1, [wide(wo_v, KT - 2 + k) for k in range(2)]),
            ("up", FT, [slab(up_v, 0, P), slab(up_v, FF, P)]),
            ("down0", 1, [wide(down_v, k) for k in range(2)]),
            ("down", FT // 2 - 2, [wide(down_v, 2 + k) for k in range(2)]),
            ("down1", 1, [wide(down_v, FT - 2 + k) for k in range(2)]),
        ]
        first, n = {}, 0
        for name, its, slabs in SECTIONS:
            assert n % 2 == 0 and len(slabs) % 2 == 0
            first[name] = n
            n += its * len(slabs)
        size = {name: len(slabs) for name, _, slabs in SECTIONS}
        its_of = {name: its for name, its, _ in SECTIONS}
        tiles_of = {name: len(slabs) for name, _, slabs in SECTIONS} | {"mssm": 2, "wout0": 0, "wout": 0, "wout1": 0, "down0": 0, "down": 0, "down1": 0}
        first_tile, n = {}, 0
        for name, its, _ in SECTIONS:
            first_tile[name] = n
            n += its * tiles_of[name]

        def slab_count(name, i, k):
            return first[name] // 2 + i * (size[name] // 2) + k // 2 + 1

        def tile_count(name, i, t):
            return first_tile[name] // 2 + i * (tiles_of[name] // 2) + t // 2 + 1

        raw_full = [sem(f"raw_full{s}") for s in range(2)]
        split_full = [sem(f"split_full{s}") for s in range(2)]
        slab_done = [sem(f"slab_done{s}") for s in range(2)]
        bank_free = [sem(f"bank_free{s}") for s in range(2)]

        def loop(eng, name, body, chain=None):
            its = next(s[1] for s in SECTIONS if s[0] == name)
            if chain:
                chain.restart()
            if its == 1:
                body(0)
            else:
                with eng.Fori(0, its) as i:
                    body(i)
                    if chain:
                        chain.restart()

        block = ctx.enter_context(nc.Block())

        x_v = x[0].rearrange("(t p) d -> p t d", p=P)
        mem_v = mem[0].rearrange("(t p) d -> p t d", p=P)
        out_v = out[0].rearrange("(t p) d -> p t d", p=P)
        V, n = {}, 0
        for name, ap in (("lb0", hg_lb_param[0]),
                         ("lb1", hg_lb_param[1]), ("hg", hg_norm_w[0]), ("cb", conv_b[0]),
                         ("ssm", ssm_norm_w[0])):
            V[name] = (n, ap.shape[0] // P, ap)
            n += ap.shape[0] // P
        VR = n
        assert VR <= P and TAPS * CONV // P == P

        def vcol(name, c):
            return vec_ch[:, bass.ds(V[name][0] + c, 1)]

        @block.sync
        def _(sp):
            for s in range(2):
                sp.sem_inc(bank_free[s], 1)
            for t in range(TT):
                sp.dma_start(x_tok[:, t, :], x_v[:, t, :]).then_inc(sem(f"x_in{t}"), 16)
                if t == 0:
                    sp.dma_start(pre_bc[:], norm_mix_pre.to_broadcast([P, D])).then_inc(sem("pre_in"), 16)

            def load(name, i, k):
                desc = next(s[2] for s in SECTIONS if s[0] == name)[k]
                if not (name == "hg0" and k < 2):
                    wait_alone(sp, split_full[k % 2], slab_count(name, i, k) - 1)
                if len(desc) == 2:
                    w, row = desc
                    src = w[:, bass.ds(row + 2 * i, 1), :].rearrange("p a (k c) -> p (a k) c", c=P)
                    sp.dma_start(raw[:, k % 2], src).then_inc(raw_full[k % 2], 16)
                    return
                w, start, stride, k0, k1, shift = desc
                c = start + stride * (i + shift)
                sp.dma_start(raw[:, k % 2, 0:k1 - k0, :], w[:, k0:k1, bass.ds(c, P)])\
                  .then_inc(raw_full[k % 2], 16)

            def loads(*names):
                for name in names:
                    loop(sp, name, lambda i: [load(name, i, k) for k in range(size[name])])

            load("hg0", 0, 0)
            load("hg0", 0, 1)
            sp.dma_start(wdt[:], win_v[:, :, C_DT:C_DT + H]).then_inc(sem("wdt_in"), 16)
            sp.dma_start(conv_rows[:], conv_w[0].rearrange("k (c p) -> (k c) p", p=P)).then_inc(sem("vecs_in"), 16)
            sp.wait_ge(sem("vec_zero"), 1)
            for at, n, ap in V.values():
                sp.dma_start(vec_rows[at:at + n, :], ap.rearrange("(c p) -> c p", p=P)).then_inc(sem("vecs_in"), 16)
            sp.dma_start(dtb_bc[:], dt_bias.to_broadcast([P, H])).then_inc(sem("dtv_in"), 16)
            sp.dma_start(alog_bc[:], a_log.to_broadcast([P, H])).then_inc(sem("dtv_in"), 16)
            sp.dma_start(dskip_bc[:], d_skip.to_broadcast([P, H])).then_inc(sem("dtv_in"), 16)
            load("hg0", 0, 2)
            load("hg0", 0, 3)
            loads("ssm0", "mix")
            for k in range(3):
                load("gates", 0, k)
            sp.wait_ge(sem("hg_A"), GROUPS)
            sp.dma_start(mem_bc[:], norm_mem.to_broadcast([P, D])).then_inc(sem("mem_in"), 16)
            sp.wait_ge(sem("hg_o"), GROUPS)
            sp.dma_start(m_tok[:], mem_v).then_inc(sem("mem_in"), 16)
            for k in range(3, KT):
                load("gates", 0, k)
            loads("mssm", "xa0", "xa")
            loads("merge", "wout0")
            sp.wait_ge(sem("xa_y"), 2 * XA_HEADS + 1)
            sp.dma_start(post_bc[:], norm_mix_post.to_broadcast([P, D])).then_inc(sem("wo_in"), 16)
            sp.dma_start(fpre_bc[:], norm_ffn_pre.to_broadcast([P, D])).then_inc(sem("wo_in"), 16)
            sp.wait_ge(slab_done[1], first["wout0"] // 2)
            sp.dma_start(x_tok2[:], x_v).then_inc(sem("wo_in"), 16)
            loads("wout", "wout1", "up")
            sp.wait_ge(slab_done[1], first["up"] // 2)
            sp.dma_start(fpost_bc[:], norm_ffn_post.to_broadcast([P, D])).then_inc(sem("fpost_in"), 16)
            loads("down0", "down", "down1")
            for t in range(TT):
                sp.wait_ge(sem("fo_new"), t + 1)
                sp.dma_start(out_v[:, t, :], o_tok[:, t, :]).then_inc(sem("stored"), 16)
            sp.wait_ge(sem("stored"), 16 * TT)

        @block.gpsimd
        def _(pool):
            g = nc.gpsimd
            ch = Chain(pool, "pool_chain")
            ch.did(g.memset(ident[:], 0.0))
            ch.did(g.memset(ones[:], 1.0))
            ch.did(g.memset(eps_col[:], EPS))
            ch.did(g.memset(zero_col[:], 0.0))
            for m in (hg_mask, cum_mask, after_mask):
                ch.did(g.memset(m[:], 1.0))
            ch.did(g.memset(hg_start[:], 1.0))
            ch.settle()
            ch.did(g.affine_select(out=ident[:], in_=ident[:], compare_op=ALU.not_equal, fill=1.0,
                                   base=0, pattern=[[-1, P]], channel_multiplier=1))

            def same_chunk(m, n):
                v = m[:].rearrange("p (b c) -> p b c", c=n)
                ch.settle()
                ch.step(g.affine_select(out=v, in_=v, compare_op=ALU.is_ge, fill=0.0, base=0,
                                        pattern=[[-n, P // n], [0, n]], channel_multiplier=1))
                ch.step(g.affine_select(out=v, in_=v, compare_op=ALU.is_ge, fill=0.0, base=n - 1,
                                        pattern=[[n, P // n], [0, n]], channel_multiplier=-1))

            same_chunk(hg_mask, HG_CHUNK)
            same_chunk(cum_mask, SSM_CHUNK)
            same_chunk(after_mask, SSM_CHUNK)
            for m in (hg_mask, cum_mask):
                ch.did(g.affine_select(out=m[:], in_=m[:], compare_op=ALU.is_ge, fill=0.0, base=0,
                                       pattern=[[1, P]], channel_multiplier=-1))
            ch.did(g.affine_select(out=after_mask[:], in_=after_mask[:], compare_op=ALU.is_ge, fill=0.0,
                                   base=-1, pattern=[[-1, P]], channel_multiplier=1))
            v = hg_start[:].rearrange("p (b c) -> p b c", c=HG_CHUNK)
            g.affine_select(out=v, in_=v, compare_op=ALU.is_ge, fill=0.0, base=-1,
                            pattern=[[0, HC], [1, HG_CHUNK]], channel_multiplier=0).then_inc(sem("consts"), 1)

            def split(name, i, k):
                n, s = KT, k % 2
                src = raw[:, s, 0:n, :]
                pool.wait_ge(raw_full[s], 16 * slab_count(name, i, k))
                if not (name == "hg0" and k < 2):
                    pool.wait_ge(slab_done[s], slab_count(name, i, k) - 1)
                ch.step(g.tensor_tensor(w_hi[s][:, 0:n, :], src,
                                        zero_col[:].unsqueeze(2).to_broadcast([P, n, P]), ALU.add))
                g.tensor_tensor(w_lo[s][:, 0:n, :], src, w_hi[s][:, 0:n, :].bitcast(F32), ALU.subtract)\
                 .then_inc(split_full[s], 1)

            def section(name):
                def body(i):
                    for k in range(size[name]):
                        split(name, i, k)
                loop(pool, name, body, ch)

            def add_tokens(dst, y, y_sem, x, done):
                for t in range(TT):
                    pool.wait_ge(sem(y_sem), t + 1)
                    g.tensor_tensor(dst[:, t, :], y[:, t % 2, :], x[:, t, :], ALU.add).then_inc(sem(done), 1)

            for name, _, _ in SECTIONS:
                section(name)
                if name == "wout1":
                    pool.wait_ge(sem("wo_in"), 48)
                    add_tokens(x2, wo_y, "wo_y", x_tok2, "x2_new")
            pool.wait_ge(sem("x2_new"), TT)
            add_tokens(o_tok, dn_y, "fo_y", x2, "fo_new")

        @block.tensor
        def _(pe):
            mm = nc.tensor.matmul

            part_ready = {"sm_split": 0, "mg_split": 0, "xa_y": 1}

            def gemm_slab(name, i, k, t, rhs_hi, rhs_lo, k_first, k_last, N=T, parts=None,
                          part=None):
                ks = next(s[2] for s in SECTIONS if s[0] == name)[k]
                s, b = k % 2, t % 2
                k0, n = ks[3], ks[4] - ks[3]
                start_kk, end_kk = part or (0, n)
                if start_kk == 0:
                    pe.wait_ge(split_full[s], slab_count(name, i, k))
                if k_first and start_kk == 0:
                    pe.wait_ge(bank_free[b], tile_count(name, i, t))
                for kk in range(start_kk, end_kk):
                    if parts:
                        pe.wait_ge(sem(parts), k0 + kk + 1 + part_ready[parts])
                    for w, r in ((w_hi, rhs_hi), (w_hi, rhs_lo), (w_lo, rhs_hi)):
                        last = mm(bank[b][:, 0:N], w[s][:, kk, :], r[:, k0 + kk, :],
                                  start=(k_first and kk == 0 and w is w_hi and r is rhs_hi),
                                  stop=(k_last and kk == n - 1 and w is w_lo))
                if end_kk == n:
                    last.then_inc(slab_done[s], 1)

            def one(name, i, k, hi=h_hi, lo=h_lo, N=T, part=None):
                gemm_slab(name, i, k, k, hi, lo, True, True, N, part=part)

            def token_transposes(n, src, ready, done, b0=0):
                for t in range(n):
                    pe.wait_ge(sem(ready), t + 1)
                    for k in range(KT):
                        last = nc.tensor.transpose(bank[b0 + 2 * t + k // 4][:, (k % 4) * P:(k % 4 + 1) * P],
                                                   src[:, t % 2, k * P:(k + 1) * P], ident[:])
                    last.then_inc(sem(done), 1)

            pe.wait_ge(sem("consts"), 1)
            token_transposes(TT, xn, "xn", "x_T")
            pe.wait_ge(sem("h_ready"), 2 * TT)
            one("hg0", 0, 0)
            pe.wait_ge(sem("vecs_in"), 16 * (1 + len(V)))
            nc.tensor.transpose(bank[3][:, 0:P], conv_rows[:], ident[:])
            nc.tensor.transpose(bank[3][:, P:2 * P], vec_rows[:], ident[:]).then_inc(sem("vecs_T"), 1)
            one("hg0", 0, 1)
            pe.wait_ge(sem("wdt_ready"), 1)
            for kk in range(KT):
                for w, r in ((wdt_hi, h_hi), (wdt_hi, h_lo), (wdt_lo, h_hi)):
                    last = mm(bank[2][0:H, :], w[:, kk, :], r[:, kk, :],
                              start=(kk == 0 and w is wdt_hi and r is h_hi), stop=(kk == KT - 1 and w is wdt_lo))
            last.then_inc(sem("dt_mm"), 1)
            one("hg0", 0, 2)
            pe.wait_ge(sem("dtT_ready"), 1)
            for t in range(TT):
                last = nc.tensor.transpose(bank[6][:, t * H:(t + 1) * H], dtT[:, t * P:(t + 1) * P], ident[0:H, 0:H])
            last.then_inc(sem("dt_mm"), 1)
            one("hg0", 0, 3)
            pe.wait_ge(sem("dta_ready"), 1)
            dta_f = dta[:].rearrange("p t h -> p (t h)")
            mm(bank[6][:, 0:TT * H], after_mask[:], dta_f, start=True, stop=True).then_inc(sem("dt_mm"), 1)
            mm(bank[7][:, 0:TT * H], ones[0:64, :], dta[0:64].rearrange("p t h -> p (t h)"),
               start=True, stop=True)
            mm(bank[4][:, 0:TT * H], ones[64:128, :], dta[64:128].rearrange("p t h -> p (t h)"),
               start=True, stop=True).then_inc(sem("dt_mm"), 1)

            def hg_transposes(i):
                pe.wait_ge(sem("hg_pre"), i + 1)
                for t in range(TT):
                    nc.tensor.transpose(bank[2][:, t * P:(t + 1) * P], hi_[:, t * P:(t + 1) * P], ident[:])
                for t in range(TT):
                    last = nc.tensor.transpose(bank[3][:, t * P:(t + 1) * P],
                                               e_l[:, t * P:(t + 1) * P], ident[:])
                last.then_inc(sem("hg_T"), 1)

            def hg_scores(i):
                pe.wait_ge(sem("hg_tok"), i + 1)
                for t in range(TT):
                    c = slice(t * P, (t + 1) * P)
                    last = mm(bank[2][:, c], e_k[:, c], e_q[:, c], start=True, stop=True)
                last.then_inc(sem("hg_A"), 1)

            def hg_kv(i, t):
                pe.wait_ge(sem("hg_vblk"), 4 * i + t + 1)
                if t == 1:
                    pe.wait_ge(sem("hg_masked"), i + 1)
                if t >= 2:
                    pe.wait_ge(sem("hg_state"), 4 * i + t - 1)
                mm(bank[3 - t % 2][:], ki_tok[:, t, :], v_blk[:, t % 2].rearrange("p c v -> p (c v)"),
                   start=True, stop=True).then_inc(sem("hg_kv"), 1)

            def hg_out_mm(i):
                pe.wait_ge(sem("hg_state"), 4 * i + 4)
                for t in range(TT):
                    c0 = t * P
                    mm(bank[3][:, c0:c0 + P], v_tok[:, t, :], hgA[:, t, :], start=True, stop=False)
                    for c in range(BC):
                        a = c0 + c * HG_CHUNK
                        last = mm(bank[3][:, a:a + HG_CHUNK], hgS[:, t * BC + c, :], e_i[:, a:a + HG_CHUNK],
                                  start=False, stop=(c == BC - 1))
                last.then_inc(sem("hg_o"), 1)

            def hg_norm(i):
                pe.wait_ge(sem("hg_osq"), i + 1)
                mm(bank[2][:], ones[:], hsig[:], start=True, stop=True).then_inc(sem("hg_n"), 1)

            def sm_transposes(i):
                pe.wait_ge(sem("sm_conv"), i + 1)
                pe.wait_ge(sem("sm_done"), i + 1)
                for c in range(GT):
                    for t in range(TT):
                        nc.tensor.transpose(bank[4 + c][:, t * P:(t + 1) * P],
                                            cv[:, c, t * P:(t + 1) * P], ident[:])
                for t in range(TT):
                    last = nc.tensor.transpose(bank[6][:, t * P:(t + 1) * P],
                                               cv[:, 2, t * P:(t + 1) * P], ident[:])
                last.then_inc(sem("sm_T"), 1)
                for t in range(TT):
                    c = slice(t * P, (t + 1) * P)
                    last = mm(bank[7][:, c], cv[:, 2, c], cv[:, 3, c], start=True, stop=True)
                last.then_inc(sem("sm_cb"), 1)

            def sm_din(i):
                pe.wait_ge(sem("sm_btok"), i + 1)
                pe.wait_ge(sem("sm_masked"), i + 1)
                for c in range(GT):
                    for t in range(TT):
                        last = mm(bank[6 + c][:, t * P:(t + 1) * P], dta_rep[:, t, c * P:(c + 1) * P],
                                  cum_mask[:], start=True, stop=True)
                last.then_inc(sem("sm_cum"), 1)

            def sm_seg(i, t):
                pe.wait_ge(sem("sm_udta"), 4 * i + t + 1)
                if t < 2:
                    pe.wait_ge(sem("sm_din"), i + 1)
                else:
                    pe.wait_ge(sem("sm_ldec"), 4 * i + t - 1)
                mm(bank[6 + t % 2][:], after_mask[:], udta[:, t % 2].rearrange("p h t -> p (h t)"),
                   start=True, stop=True).then_inc(sem("sm_seg"), 1)

            def sm_diag(i, t):
                pe.wait_ge(sem("sm_M"), 4 * i + t + 1)
                for h in range(HPG):
                    c, o = h // 2, (h % 2) * HD
                    last = mm(bank[4 + c][o:o + HD, t * P:(t + 1) * P], xdt[:, c, t, o:o + HD],
                              ldec[:, t % 2, h, :], start=True, stop=True)
                last.then_inc(sem("sm_yd"), 1)

            def sm_kv(i, half):
                if half == 0:
                    pe.wait_ge(sem("hg_y"), i + 1)
                    pe.wait_ge(sem("sm_xdo"), i + 1)
                else:
                    pe.wait_ge(sem("sm_state"), 2 * i + 1)
                for c in range(4 * half, 4 * half + 4 - half):
                    p = 64 * (c % 2)
                    q = (c // 2) % 2 * HPG * HD
                    last = mm(bank[2 + c % 2][:, q:q + HPG * HD], b_tok[p:p + 64, c // 2, :],
                              xdo[p:p + 64, :, c // 2, :], start=True, stop=True)
                last.then_inc(sem("sm_kv"), 1)

            def sm_off(i):
                pe.wait_ge(sem("sm_state"), 2 * i + 2)
                pe.wait_ge(sem("sm_ldec"), 4 * i + 4)
                for c in range(GT):
                    for k in range(NC):
                        a = k * SSM_CHUNK
                        last = mm(bank[6 + c][:, a:a + SSM_CHUNK], smS[:, k, c * P:(c + 1) * P],
                                  cv[:, 3, a:a + SSM_CHUNK], start=True, stop=True)
                last.then_inc(sem("sm_yo"), 1)

            def sm_norm(i):
                for c in range(GT):
                    pe.wait_ge(sem("sm_sq"), 2 * i + c + 1)
                    last = mm(bank[6][:], ones[:], ssq[:] if c == 0 else din[:, 0, :], start=(c == 0), stop=(c == 1))
                last.then_inc(sem("sm_n"), 1)

            def hgrn_half(name, j, base, i):
                one(name, j, base)
                one(name, j, base + 1)
                one(name, j, base + 2)
                if base:
                    sm_norm(i - 1)
                hg_transposes(i)
                one(name, j, base + 3)
                one(name, j, base + 4, part=(0, KT // 2))
                hg_scores(i)
                hg_kv(i, 0)
                one(name, j, base + 4, part=(KT // 2, KT))
                hg_kv(i, 1)
                one(name, j, base + 5, part=(0, KT // 2))
                hg_kv(i, 2)
                one(name, j, base + 5, part=(KT // 2, KT))

            def ssm_half(name, j, i):
                def next_slab(k, part=None):
                    one(name, j, k, part=part)
                next_slab(0)
                hg_kv(i, 3)
                next_slab(1)
                hg_out_mm(i)
                sm_transposes(i)
                hg_norm(i)
                sm_din(i)
                next_slab(2)
                sm_seg(i, 0)
                sm_seg(i, 1)
                sm_kv(i, 0)
                sm_diag(i, 0)
                sm_seg(i, 2)
                sm_diag(i, 1)
                sm_seg(i, 3)
                next_slab(3, (0, KT // 2))
                sm_kv(i, 1)
                next_slab(3, (KT // 2, KT))
                sm_diag(i, 2)
                sm_diag(i, 3)
                sm_off(i)

            hgrn_half("ssm0", 0, 0, 0)

            def mix(j):
                ssm_half("mix", j, j)
                hgrn_half("mix", j, 4, j + 1)

            loop(pe, "mix", mix)
            last_group = GROUPS - 1
            ssm_half("gates", 0, last_group)
            one("gates", 0, 4)
            one("gates", 0, 5, part=(0, KT // 2))
            sm_norm(last_group)
            one("gates", 0, 5, part=(KT // 2, KT))
            token_transposes(MT, m_tok, "m_scaled", "m_T", 2)
            one("gates", 0, 6)
            one("gates", 0, 7)

            def mssm(i):
                for c in range(2):
                    gemm_slab("mssm", i, 2 * c, c, sm_hi, sm_lo, True, False, parts="sm_split")
                    gemm_slab("mssm", i, 2 * c + 1, c, sm_hi, sm_lo, False, True, parts="sm_split")

            loop(pe, "mssm", mssm)

            def xa_slabs(name, i, ks):
                for k in ks:
                    if k in (0, 2):
                        one(name, i, k)
                    else:
                        one(name, i, k, m_hi, m_lo, NM)

            def scores_and_v(h):
                for b in range(2):
                    pe.wait_ge(bank_free[b], tile_count("xa", h - 1, 2 + b) + 1)
                for t in range(TT):
                    for c in range(QT):
                        last = mm(bank[4 + t][:, 0:NM], q_sb[:, c, t * P:(t + 1) * P], k_sb[:, c, :],
                                  start=(c == 0), stop=(c == QT - 1))
                    last.then_inc(sem("xa_s"), 1)
                for b in range(2):
                    pe.wait_ge(bank_free[b], tile_count("xa", h - 1, 4 + b) + 1)
                pe.wait_ge(sem("xa_y"), 2 * h + 1)
                for c in range(QT):
                    for t in range(MT):
                        last = nc.tensor.transpose(bank[2][:, (t * QT + c) * P:(t * QT + c + 1) * P],
                                                   v_sb[:, c, t * P:(t + 1) * P], ident[:])
                last.then_inc(sem("xa_vT"), 1)

            def probs_T(h, t):
                pe.wait_ge(sem("xa_norm"), 4 * h + t + 1)
                for m in range(MT):
                    last = nc.tensor.transpose(bank[4 + t][:, m * P:(m + 1) * P],
                                               prob[:, t, m * P:(m + 1) * P], ident[:])
                last.then_inc(sem("xa_pT"), 1)

            def values(h):
                pe.wait_ge(sem("xa_p"), 4 * h + 4)
                pe.wait_ge(sem("xa_v"), h + 1)
                for c in range(QT):
                    for m in range(MT):
                        last = mm(bank[2 + c][:], v_mt[:, m, c * P:(c + 1) * P], pT[:, m, :],
                                  start=(m == 0), stop=(m == MT - 1))
                    last.then_inc(sem("xa_o"), 1)

            def attend(name, i, h):
                scores_and_v(h)
                if name:
                    xa_slabs(name, i, (0,))
                probs_T(h, 0)
                probs_T(h, 1)
                if name:
                    xa_slabs(name, i, (1,))
                probs_T(h, 2)
                probs_T(h, 3)
                if name:
                    xa_slabs(name, i, (2, 3))
                values(h)
                if name:
                    xa_slabs(name, i, (4, 5))

            pe.wait_ge(sem("m_ready"), 2 * MT)
            xa_slabs("xa0", 0, range(6))
            loop(pe, "xa", lambda h: attend("xa", h, h))
            attend(None, 0, XA_HEADS - 1)

            def merge(i):
                one("merge", i, 0)
                one("merge", i, 1)
                gemm_slab("merge", i, 2, 2, hg_hi, hg_lo, True, True)
                gemm_slab("merge", i, 3, 3, xa_hi, xa_lo, True, True, parts="xa_y")

            pe.wait_ge(sem("hg_split"), KT)
            loop(pe, "merge", merge)

            def wide_slab(name, i, k, parts, ready):
                s = k % 2
                pe.wait_ge(split_full[s], slab_count(name, i, k))
                pe.wait_ge(*ready)
                start, stop = name[-1] == "0" and k == 0, name[-1] == "1" and k == 1
                for t in range(TT):
                    c = slice(t * P, (t + 1) * P)
                    for half in range(2):
                        cols = slice(4 * half, 4 * half + 4)
                        for l, w in ((0, w_hi), (1, w_hi), (0, w_lo)):
                            last = mm(bank[2 * t + half][:], parts[l][:, c],
                                      w[s][:, cols, :].rearrange("p k c -> p (k c)"),
                                      start=start and l == 0 and w is w_hi, stop=stop and w is w_lo)
                    if stop and t < TT - 1:
                        last.then_inc(sem(name + "_tile"), 1)
                last.then_inc(slab_done[s], 1)

            def wide_product(name, stage, n0, hi, lo, made, before):
                def own(row):
                    return (hi[:, row, :], lo[:, row, :]), (sem(made), before + row + 1)
                for b in range(2):
                    pe.wait_ge(bank_free[b], first_tile[name + "0"] // 2 + 1)
                for k in range(2):
                    wide_slab(name + "0", 0, k, *own(k))
                loop(pe, name, lambda i: [wide_slab(name, i, k, (stage[:, k, 0, :], stage[:, k, 1, :]),
                                                    (sem("staged"), n0 + 2 * i + k + 1)) for k in range(2)])
                for k in range(2):
                    wide_slab(name + "1", 0, k, *own(2 * its_of[name] + 2 + k))

            wide_product("wout", wo_stage, 0, mg_hi, mg_lo, "mg_split", 0)
            token_transposes(TT, xn2, "xn2", "h2_T")
            pe.wait_ge(sem("h2_ready"), 2 * TT)
            loop(pe, "up", lambda i: [one("up", i, c) for c in range(2)])
            wide_product("down", dn_stage, 2 * its_of["wout"], a_hi, a_lo, "act_ready", 1)

        @block.scalar
        def _(act):
            f = nc.scalar.activation
            ch = Chain(act, "act_chain")
            def ln_exp_tables():
                act.preload_act_table_set("natural_log_exp_and_others")

            ln_exp_tables()

            def rstd(dst, src, n):
                ch.step(f(dst, src, ACT.Ln, scale=1.0 / n, bias=eps_col[:]))
                return f(dst, dst, ACT.Exp, scale=-0.5)

            def rms_of_row(n, t, row, junk, done):
                ss = col_ss[:, n, t:t + 1]
                ch.step(f(junk[:], row, ACT.Square, scale=D ** -0.5, accum_out=ss))
                ch.step(f(ss, ss, ACT.Ln, bias=eps_col[:]))
                f(col_rs[:, n, t:t + 1], ss, ACT.Exp, scale=-0.5).then_inc(sem(done), 1)

            def row_hi(t, hi, ready, done, b0=0):
                act.wait_ge(sem(ready), t + 1)
                for half in range(2):
                    f(hi[:, 4 * half:4 * half + 4, t * P:(t + 1) * P], tiles(b0 + 2 * t + half), ACT.Copy)\
                        .then_inc(sem(done), 1)

            act.wait_ge(sem("consts"), 1)
            for t in range(TT + 1):
                if t < TT:
                    act.wait_ge(sem(f"x_in{t}"), 16)
                    rms_of_row(3, t, x_tok[:, t, :], sq_out0, "x_rs")
                if t >= 1:
                    row_hi(t - 1, h_hi, "x_T", "h_hi_ready")
            act.wait_ge(sem("dtv_in"), 48)
            ch.step(f(alog_bc[:], alog_bc[:], ACT.Exp))

            def read_tile(name, i, k, dst, N=T, before=None):
                if before:
                    act.wait_ge(*before)
                act.wait_ge(slab_done[k % 2], slab_count(name, i, k))
                f(dst, bank[k % 2][:, 0:N], ACT.Copy).then_inc(bank_free[k % 2], 1)

            hg_dst = (hf, hq, hi_, hog)

            def hg_sigmoids(u):
                for k, (src, name) in enumerate(((hf, "hg_sf"), (hq, "hg_sq"), (hog, "hg_sog"))):
                    if k:
                        act.wait_ge(sem("hg_sig_used"), 3 * u + k)
                    f(hsig[:], src[:], ACT.Sigmoid).then_inc(sem("hg_sig"), 1)
                ln_exp_tables()

            def hg_exps(i):
                act.wait_ge(sem("hg_f"), i + 1)
                f(hf[:], hf[:], ACT.Ln).then_inc(sem("hg_g"), 1)
                act.wait_ge(sem("hg_b"), i + 1)
                ch.did(f(e_i[:], hb[:], ACT.Exp))
                ch.did(f(e_q[:], hd[:], ACT.Exp))
                ch.did(f(e_k[:], hd[:], ACT.Exp, scale=-1.0))
                f(e_l[:], hd2[:], ACT.Exp).then_inc(sem("hg_e"), 1)

            for k in range(3):
                read_tile("hg0", 0, k, hg_dst[k][:])
            act.wait_ge(sem("lb_diff"), 1)
            f(lb_tmp[:], lb_tmp[:], ACT.Exp).then_inc(sem("lb_exp"), 1)
            act.wait_ge(sem("dt_abs"), 1)
            ch.step(f(dte[:], dte[:], ACT.Exp, scale=-1.0))
            f(dte[:], dte[:], ACT.Ln, bias=ones[:, 0:1]).then_inc(sem("dt_ln"), 1)
            read_tile("hg0", 0, 3, hg_dst[3][:])
            act.wait_ge(sem("dt_mm"), 3)
            f(dout_dt[:].rearrange("p t h -> p (t h)"), bank[6][:, 0:TT * H], ACT.Exp)\
                .then_inc(sem("dout_exp"), 1)
            act.wait_ge(sem("dt_mm"), 4)
            ch.did(f(dchunk[:, 0].rearrange("p t h -> p (t h)"), bank[7][:, 0:TT * H], ACT.Exp))
            f(dchunk[:, 1].rearrange("p t h -> p (t h)"), bank[4][:, 0:TT * H], ACT.Exp)\
                .then_inc(sem("dchunk_exp"), 1)
            act.wait_ge(sem("start_done"), 1)
            ch.settle()
            act.wait_ge(bank_free[1], tile_count("hg0", 0, 3) + 1)
            hg_sigmoids(0)

            def v_by_chunk(i, t):
                for c in range(BC):
                    p = c * HG_CHUNK
                    last = f(v_blk[p:p + HG_CHUNK, t % 2, c, :], v_tok[p:p + HG_CHUNK, t, :], ACT.Copy)
                    if c < BC - 1:
                        ch.did(last)
                last.then_inc(sem("hg_vblk"), 1)

            def sm_squares(i):
                act.wait_ge(sem("sm_y"), i + 1)
                ch.did(f(ssq[:], sy[:, 0, :], ACT.Square))
                f(din[:, 0, :], sy[:, 1, :], ACT.Square).then_inc(sem("sm_sq"), 2)

            def sm_rstd(i):
                act.wait_ge(sem("sm_n"), i + 1)
                rstd(srs[:], bank[6][:], GT * P).then_inc(sem("sm_rs"), 1)

            def hgrn_half(name, j, base, i):
                if base:
                    sm_squares(i - 1)
                read_tile(name, j, base, zs[:, 0, :])
                hg_exps(i)
                act.wait_ge(sem("hg_e"), i + 1)
                read_tile(name, j, base + 1, zs[:, 1, :])
                if base:
                    sm_rstd(i - 1)
                for k in range(2):
                    if k:
                        act.wait_ge(sem("sm_z"), 2 * i + k)
                    act.wait_ge(bank_free[1], tile_count(name, j, base + 1) + 1)
                    f(zsig[:], zs[:, k, :], ACT.Sigmoid).then_inc(sem("sm_zsig"), 1)

                def conv_in(k):
                    before = (sem("sm_cv"), 4 * i + k) if k else None
                    read_tile(name, j, base + 2 + k, xpad[:, 3:3 + T], before=before)

                def conv_sig(k):
                    act.wait_ge(sem("sm_cv"), 4 * i + k + 1)
                    if k:
                        act.wait_ge(sem("sm_cx"), 3 * i + k)
                    else:
                        act.wait_ge(sem("sm_z"), 2 * i + 2)
                    f(csig[:], cv[:, k, :], ACT.Sigmoid).then_inc(sem("sm_csig"), 1)

                conv_in(0)
                act.wait_ge(sem("hg_T"), i + 1)
                ch.did(f(v_tok[:].rearrange("p t c -> p (t c)"), bank[2][:], ACT.Copy))
                f(ki_tok[:].rearrange("p t c -> p (t c)"), bank[3][:], ACT.Copy).then_inc(sem("hg_tok"), 1)
                act.wait_ge(sem("hg_tok"), i + 1)
                v_by_chunk(i, 0)
                v_by_chunk(i, 1)
                conv_sig(0)
                conv_in(1)
                act.wait_ge(sem("hg_kv"), 4 * i + 1)
                v_by_chunk(i, 2)
                conv_sig(1)
                conv_in(2)
                act.wait_ge(sem("hg_kv"), 4 * i + 2)
                v_by_chunk(i, 3)
                conv_sig(2)
                conv_in(3)
                conv_sig(3)
                ln_exp_tables()

            def ssm_half(name, j, i):
                last = name == "gates"
                dst = [gates[:, k, :] for k in range(4)] if last else [hf[:], hq[:], hi_[:], hog[:]]
                read_tile(name, j, 0, dst[0])
                act.wait_ge(sem("hg_o"), i + 1)
                f(hsig[:], bank[3][:], ACT.Square).then_inc(sem("hg_osq"), 1)
                act.wait_ge(sem("sm_T"), i + 1)
                f(b_tok[:].rearrange("p t c -> p (t c)"), bank[6][:], ACT.Copy).then_inc(sem("sm_btok"), 1)
                read_tile(name, j, 1, dst[1])
                act.wait_ge(sem("hg_n"), i + 1)
                act.wait_ge(sem("sm_done"), i + 1)
                rstd(hd[:], bank[2][:], P).then_inc(sem("hg_rs"), 1)
                act.wait_ge(sem("sm_cum"), i + 1)
                ch.did(f(din[:, 0, :], bank[6][:], ACT.Exp))
                f(din[:, 1, :], bank[7][:], ACT.Exp).then_inc(sem("sm_din"), 1)

                def decay(t):
                    act.wait_ge(sem("sm_seg"), 4 * i + t + 1)
                    if t >= 2:
                        act.wait_ge(sem("sm_yd"), 4 * i + t - 1)
                    f(ldec[:, t % 2].rearrange("p h t -> p (h t)"), bank[6 + t % 2][:], ACT.Exp)\
                        .then_inc(sem("sm_ldec"), 1)

                decay(0)
                decay(1)
                read_tile(name, j, 2, dst[2])
                decay(2)
                decay(3)
                if last:
                    read_tile(name, j, 3, dst[3])
                    act.wait_ge(sem("mem_in"), 32)
                    for t in range(MT):
                        rms_of_row(4, t, m_tok[:, t, :], sq_out1, "m_rs")
                    return
                read_tile(name, j, 3, dst[3], before=(sem("hg_y"), i + 1))
                act.wait_ge(bank_free[1], tile_count(name, j, 3) + 1)
                hg_sigmoids(i + 1)

            hgrn_half("ssm0", 0, 0, 0)

            def mix(j):
                ssm_half("mix", j, j)
                hgrn_half("mix", j, 4, j + 1)

            loop(act, "mix", mix, ch)
            last_group = GROUPS - 1
            ssm_half("gates", 0, last_group)

            read_tile("gates", 0, 4, gates[:, 4, :], before=(sem("m_scaled"), MT))
            sm_squares(last_group)
            sm_rstd(last_group)
            read_tile("gates", 0, 5, gates[:, 5, :])
            for t in range(MT):
                row_hi(t, m_hi, "m_T", "m_hi_ready", 2)
            read_tile("gates", 0, 6, gates[:, 6, :])

            def y_ssm_hi(tiles):
                for k in tiles:
                    f(sm_hi[:, k, :], y_ssm[:, k, :], ACT.Copy).then_inc(sem("sm_hi_ready"), 1)

            act.wait_ge(sem("sm_done"), GROUPS + 1)
            y_ssm_hi(range(KT))
            read_tile("gates", 0, 7, gates[:, 7, :])
            y_ssm_hi(range(KT, INNER // P))
            act.wait_ge(bank_free[1], tile_count("gates", 0, 7) + 1)
            for k in range(KT):
                f(gates[:, k, :], gates[:, k, :], ACT.Sigmoid).then_inc(sem("gates_ready"), 1)
            ln_exp_tables()

            def gated(name, i, k, t, dst, user):
                act.wait_ge(slab_done[k % 2], slab_count(name, i, k))
                act.wait_ge(bank_free[user % 2], tile_count(name, i, user) - 1)
                f(dst[:], bank[t % 2][:], ACT.Sigmoid).then_inc(bank_free[t % 2], 1)

            xa_dst = [(q_sb, 0, T), (k_sb, 0, NM), (q_sb, 1, T), (k_sb, 1, NM), (v_sb, 0, NM), (v_sb, 1, NM)]

            def xa_in(name, i, ks):
                for k in ks:
                    t, c, n = xa_dst[k]
                    read_tile(name, i, k, t[:, c, :], n)

            def attend(name, i, h):
                for t in range(TT):
                    act.wait_ge(sem("xa_max"), 4 * h + t + 1)
                    f(prob[:, t, :], bank[4 + t][:, 0:NM], ACT.Exp, scale=SCALE,
                      bias=st_max[:, t:t + 1], accum_out=st_sum[:, t:t + 1]).then_inc(sem("xa_exp"), 1)
                act.wait_ge(sem("xa_vT"), h + 1)
                f(v_mt[:].rearrange("p m c -> p (m c)"), bank[2][:], ACT.Copy).then_inc(sem("xa_v"), 1)
                if name:
                    xa_in(name, i, range(6))

            xa_in("xa0", 0, range(6))
            for c in range(2):
                act.wait_ge(bank_free[c], tile_count("mssm", KT // 2 - 1, c) + 1)
            for k in range(KT):
                f(hg_hi[:, k, :], y_hg[:, k, :], ACT.Copy).then_inc(sem("hg_hi_ready"), 1)
            loop(act, "xa", lambda h: attend("xa", h, h), ch)
            attend(None, 0, XA_HEADS - 1)

            def merge(i):
                gated("merge", i, 0, 0, gate[0], 2)
                gated("merge", i, 1, 1, gate[1], 3)

            loop(act, "merge", merge, ch)
            ln_exp_tables()

            def rms_of_banks(n, name, t, junk, done):
                if t < TT - 1:
                    act.wait_ge(sem(name + "_tile"), t + 1)
                else:
                    act.wait_ge(slab_done[1], slab_count(name, 0, 1))
                ss, rs = col_ss[:, n, t:t + 1], col_rs[:, n, t:t + 1]
                ch.step(f(junk[:, 0:512], bank[2 * t][:], ACT.Square, scale=D ** -0.5, accum_out=ss))
                ch.step(f(junk[:, 512:], bank[2 * t + 1][:], ACT.Square, scale=D ** -0.5, accum_out=rs))
                ch.step(f(rs, rs, ACT.Identity, bias=eps_col[:]))
                ch.step(f(rs, ss, ACT.Ln, bias=rs))
                f(rs, rs, ACT.Exp, scale=-0.5).then_inc(sem(done), 1)

            for t in range(TT + 2):
                if t < TT:
                    rms_of_banks(0, "wout1", t, sq_out, "wo_rs")
                if 1 <= t <= TT:
                    act.wait_ge(sem("x2_new"), t)
                    rms_of_row(1, t - 1, x2[:, t - 1, :], sq_out, "x2_rs")
                if t >= 2:
                    row_hi(t - 2, h_hi, "h2_T", "h2_hi")

            def up(i):
                act.wait_ge(slab_done[0], slab_count("up", i, 0))
                act.wait_ge(bank_free[0], tile_count("up", i, 0))
                f(up_sig[:], bank[0][:], ACT.Sigmoid).then_inc(sem("up_sg"), 1)

            act.wait_ge(sem("h2_ready"), 2 * TT)
            loop(act, "up", up, ch)
            ln_exp_tables()
            for t in range(TT):
                rms_of_banks(2, "down1", t, sq_out3, "fo_rs")

        @block.vector
        def _(dve):
            v = nc.vector
            TTO, TS, STT = v.tensor_tensor, v.tensor_scalar, v.scalar_tensor_tensor
            ch = Chain(dve, "dve_chain")

            def split(hi, lo, src, w=None):
                ch.step(TS(hi, src, 1.0 if w is None else w, None, ALU.mult))
                if w is None:
                    return TTO(lo, src, hi.bitcast(F32), ALU.subtract)
                return STT(lo, src, w, hi.bitcast(F32), ALU.mult, ALU.subtract)

            def scaled_row(n, t, dst, src, w, rs_ready, dst_free, done):
                dve.wait_ge(sem(rs_ready), t + 1)
                if t >= 2:
                    dve.wait_ge(sem(dst_free), t - 1)
                STT(dst[:, t % 2, :], src[:, t, :], col_rs[:, n, t:t + 1], w[:], ALU.mult, ALU.mult)\
                    .then_inc(sem(done), 1)

            def row_lo(t, hi, lo, ready, done, b0=0):
                for half in range(2):
                    at = (slice(None), slice(4 * half, 4 * half + 4), slice(t * P, (t + 1) * P))
                    dve.wait_ge(sem(ready), 2 * t + half + 1)
                    TTO(lo[at], tiles(b0 + 2 * t + half), hi[at].bitcast(F32), ALU.subtract).then_inc(sem(done), 1)

            v.memset(vec_rows[:], 0.0).then_inc(sem("vec_zero"), 1)
            for t in range(TT + 1):
                if t == 0:
                    dve.wait_ge(sem("pre_in"), 16)
                if t < TT:
                    scaled_row(3, t, xn, x_tok, pre_bc, "x_rs", "x_T", "xn")
                if t >= 1:
                    row_lo(t - 1, h_hi, h_lo, "h_hi_ready", "h_ready")
            dve.wait_ge(sem("wdt_in"), 16)
            split(wdt_hi[:], wdt_lo[:], wdt[:]).then_inc(sem("wdt_ready"), 1)
            for t in (hgA, v_blk, hgS, smS, cbm, xpad):
                ch.did(v.memset(t[:], 0.0))
            dve.wait_ge(sem("vecs_T"), 1)
            ch.did(v.tensor_copy(conv_ch[:], bank[3][:, 0:P]))
            ch.step(v.tensor_copy(vec_ch[:], bank[3][:, P:2 * P]))
            a0, n0, _ = V["lb0"]
            a1, _, _ = V["lb1"]
            ch.step(TTO(lb[:], vec_ch[:, a0:a0 + KT], vec_ch[:, a1:a1 + KT], ALU.subtract))
            ch.step(TS(one_lb[:], lb[:], -1.0, None, ALU.mult))
            TTO(lb_tmp[:], lb[:], one_lb[:], ALU.min).then_inc(sem("lb_diff"), 1)
            dve.wait_ge(sem("dt_mm"), 1)
            v.tensor_copy(dtT[:], bank[2][0:H, :]).then_inc(sem("dtT_ready"), 1)
            dve.wait_ge(sem("lb_exp"), 1)
            ch.step(TS(one_lb[:], lb_tmp[:], 1.0, None, ALU.add))
            ch.step(v.reciprocal(one_lb[:], one_lb[:]))
            ch.step(TTO(lb_tmp[:], lb_tmp[:], one_lb[:], ALU.mult))
            ch.step(TS(lb[:], lb[:], 0.0, None, ALU.is_ge))
            ch.step(TTO(one_lb[:], one_lb[:], lb_tmp[:], ALU.subtract))
            ch.step(TTO(lb[:], lb[:], one_lb[:], ALU.mult))
            ch.step(TTO(lb[:], lb[:], lb_tmp[:], ALU.add))
            ch.step(TS(one_lb[:], lb[:], -1.0, 1.0, ALU.mult, ALU.add))
            dve.wait_ge(sem("dtv_in"), 48)
            for o in range(2):
                ch.step(v.tensor_copy(dskip_ch[64 * o:64 * o + 64, :],
                                      dskip_bc[64 * o:64 * o + 64, :].rearrange("p (c o) -> p o c", o=2)[:, o, :]))
            dve.wait_ge(sem("dt_mm"), 2)
            ch.step(TTO(dtx[:], bank[6][:, 0:TT * H].rearrange("p (t h) -> p t h", h=H),
                        dtb_bc[:].unsqueeze(1).to_broadcast([P, TT, H]), ALU.add))
            ch.step(TS(dte[:], dtx[:], -1.0, None, ALU.mult))
            TTO(dte[:], dte[:], dtx[:], ALU.max).then_inc(sem("dt_abs"), 1)
            dve.wait_ge(sem("dt_ln"), 1)
            ch.step(STT(dt_tok[:], dtx[:], 0.0, dte[:], ALU.max, ALU.add))
            STT(dta[:], dt_tok[:], -1.0, alog_bc[:].unsqueeze(1).to_broadcast([P, TT, H]),
                ALU.mult, ALU.mult).then_inc(sem("dta_ready"), 1)
            dve.wait_ge(sem("dout_exp"), 1)
            ch.step(TTO(dout_dt[:], dout_dt[:], dt_tok[:], ALU.mult))
            dve.wait_ge(sem("dchunk_exp"), 1)
            dve.wait_ge(sem("dta_ready"), 1)
            for name in ("sm_done", "xa_y", "act_ready"):
                dve.sem_inc(sem(name), 1)
            dve.sem_inc(sem("start_done"), 1)

            def chunked(t):
                return t[:].rearrange("p (c l) -> p c l", l=HG_CHUNK)

            def hg_pre(u):
                dve.wait_ge(sem("hg_sig"), 3 * u + 1)
                TS(hf[:], hsig[:], one_lb[:, bass.ds(u, 1)], lb[:, bass.ds(u, 1)], ALU.mult, ALU.add)\
                    .then_inc(sem("hg_sig_used"), 1)
                dve.wait_ge(sem("hg_sig_used"), 3 * u + 1)
                TS(hk[:], hf[:], -1.0, 1.0, ALU.mult, ALU.add).then_inc(sem("hg_f"), 1)
                dve.wait_ge(sem("hg_sig"), 3 * u + 2)
                TTO(hq[:], hq[:], hsig[:], ALU.mult).then_inc(sem("hg_sig_used"), 1)
                dve.wait_ge(sem("hg_sig"), 3 * u + 3)
                TTO(hog[:], hog[:], hsig[:], ALU.mult).then_inc(sem("hg_sig_used"), 1)

            hg_pre(0)
            ch.settle()

            def sm_y(i):
                dve.wait_ge(sem("sm_yo"), i + 1)
                for c in range(GT):
                    y = sy[:, c, :]
                    ch.step(TTO(y, bank[6 + c][:], din[:, c, :], ALU.mult))
                    ch.step(TTO(y, y, bank[4 + c][:], ALU.add))
                    ch.step(STT(y, cv[:, c, :], dskip_ch[:, bass.ds(2 * i + c, 1)], y, ALU.mult, ALU.add))
                    last = TTO(y, y, zs[:, c, :], ALU.mult)
                    if c == 0:
                        ch.did(last)
                last.then_inc(sem("sm_y"), 1)

            def sm_final(i):
                dve.wait_ge(sem("sm_rs"), i + 1)
                for c in range(GT):
                    last = STT(flat(y_ssm, 2 * i + c), sy[:, c, :], vcol("ssm", 2 * i + c), srs[:],
                               ALU.mult, ALU.mult)
                    if c == 0:
                        ch.did(last)
                last.then_inc(sem("sm_done"), 1)

            def hgrn_half(name, j, base, i):
                if base:
                    sm_y(i - 1)
                dve.wait_ge(sem("hg_g"), i + 1)
                ch.step(v.tensor_tensor_scan(hb[:], hg_start[:], hf[:], 0.0, ALU.mult, ALU.add))
                b3 = chunked(hb)
                ref = b3[:, :, HG_CHUNK // 2:HG_CHUNK // 2 + 1].to_broadcast([P, HC, HG_CHUNK])
                lst = b3[:, :, HG_CHUNK - 1:HG_CHUNK].to_broadcast([P, HC, HG_CHUNK])
                dve.wait_ge(sem("hg_sig_used"), 3 * i + 3)
                ch.did(TTO(chunked(hd), b3, ref, ALU.subtract))
                TTO(chunked(hd2), lst, b3, ALU.subtract).then_inc(sem("hg_b"), 1)
                dve.wait_ge(sem("hg_e"), i + 1)
                ch.step(v.tensor_copy(hdc[:].unsqueeze(2), chunked(e_i)[:, :, HG_CHUNK - 1:HG_CHUNK]))
                ch.did(TTO(e_i[:], e_i[:], hq[:], ALU.mult))
                ch.did(TTO(e_q[:], e_q[:], hq[:], ALU.mult))
                ch.did(TTO(e_k[:], e_k[:], hk[:], ALU.mult))
                TTO(e_l[:], e_l[:], hk[:], ALU.mult).then_inc(sem("hg_pre"), 1)
                if base:
                    sm_final(i - 1)
                for k in range(2):
                    dve.wait_ge(sem("sm_zsig"), 2 * i + k + 1)
                    TTO(zs[:, k, :], zs[:, k, :], zsig[:], ALU.mult).then_inc(sem("sm_z"), 1)

                def conv(k, ct):
                    dve.wait_ge(bank_free[k % 2], tile_count(name, j, base + 2 + k) + 1)

                    def tap(n):
                        return conv_ch[:, bass.ds(n * (CONV // P) + ct, 1)]
                    ch.step(TS(cv[:, k, :], xpad[:, 0:T], tap(0), vcol("cb", ct), ALU.mult, ALU.add))
                    for n in range(1, TAPS):
                        last = STT(cv[:, k, :], xpad[:, n:n + T], tap(n), cv[:, k, :], ALU.mult, ALU.add)
                        if n < TAPS - 1:
                            ch.step(last)
                    last.then_inc(sem("sm_cv"), 1)

                def conv_silu(k):
                    dve.wait_ge(sem("sm_csig"), 4 * i + k + 1)
                    TTO(cv[:, k, :], cv[:, k, :], csig[:], ALU.mult).then_inc(sem("sm_cx" if k < 3 else "sm_conv"), 1)

                def hg_states(t):
                    dve.wait_ge(sem("hg_kv"), 4 * i + t + 1)
                    b = 3 - t % 2
                    steps = BC if t < TT - 1 else BC - 1
                    for c in range(steps):
                        n = t * BC + c
                        ins = STT(hgS[:, n + 1, :], hgS[:, n, :], hdc[:, n:n + 1],
                                  bank[b][:, c * P:(c + 1) * P], ALU.mult, ALU.add)
                        if c < steps - 1:
                            ch.step(ins)
                    ins.then_inc(sem("hg_state"), 1)
                    dve.wait_ge(sem("hg_state"), 4 * i + t + 1)

                conv(0, 2 * i)
                wait_alone(dve, sem("hg_A"), i + 1)
                v.copy_predicated(hgA[:], hg_mask[:].bitcast(U32).unsqueeze(1).to_broadcast([P, TT, P]), tiles(2))\
                    .then_inc(sem("hg_masked"), 1)
                conv_silu(0)
                hg_states(0)
                conv(1, 2 * i + 1)
                conv_silu(1)
                hg_states(1)
                hg_states(2)
                conv(2, 2 * GROUPS + i)
                conv_silu(2)
                conv(3, 3 * GROUPS + i)
                hg_states(3)
                conv_silu(3)

            def ssm_half(name, j, i):
                cols = bass.ds(i * HPG, HPG)
                ch.did(v.tensor_copy(g_dta[:], dta[:, :, cols]))
                ch.did(v.tensor_copy(g_dt[:], dt_tok[:, :, cols]))
                ch.did(v.tensor_copy(g_do[:], dout_dt[:, :, cols]))
                ch.did(v.tensor_copy(g_dc[:], dchunk[:, :, :, cols]))
                ch.settle()
                ch.did(v.tensor_copy(dta_rep.rearrange("p t (h d) -> p t h d", d=HD),
                                     g_dta[:].unsqueeze(3).to_broadcast([P, TT, HPG, HD])))
                wait_alone(dve, sem("sm_cb"), i + 1)
                v.copy_predicated(cbm[:], cum_mask[:].bitcast(U32).unsqueeze(1).to_broadcast([P, TT, P]), tiles(7))\
                    .then_inc(sem("sm_masked"), 1)

                def u_dta(t):
                    if t >= 2:
                        dve.wait_ge(sem("sm_seg"), 4 * i + t - 1)
                    TTO(udta[:, t % 2], cum_mask[:].unsqueeze(1).to_broadcast([P, HPG, P]),
                        g_dta[:, t, :].unsqueeze(2).to_broadcast([P, HPG, P]), ALU.mult)\
                        .then_inc(sem("sm_udta"), 1)

                def decay_cb(t):
                    dve.wait_ge(sem("sm_ldec"), 4 * i + t + 1)
                    TTO(ldec[:, t % 2], ldec[:, t % 2], cbm[:, t, :].unsqueeze(1).to_broadcast([P, HPG, P]),
                        ALU.mult).then_inc(sem("sm_M"), 1)

                def by_head(dst, g, c):
                    return TTO(dst[:, c].rearrange("p t (h d) -> p t h d", d=HD),
                               bank[4 + c][:].rearrange("p (t h d) -> p t h d", t=TT, d=HD),
                               g[:, :, 2 * c:2 * c + 2].unsqueeze(3).to_broadcast([P, TT, 2, HD]), ALU.mult)

                def states(half):
                    dve.wait_ge(sem("sm_kv"), 2 * i + half + 1)
                    for c in range(4 * half, 4 * half + 4 - half):
                        q = (c // 2) % 2 * HPG * HD
                        src = bank[2 + c % 2][:, q:q + HPG * HD]
                        if c == 0:
                            ch.step(v.tensor_copy(smS[:, 1, :], src))
                            continue
                        ch.step(TTO(smT.rearrange("p (h d) -> p h d", d=HD),
                                    smS[:, c, :].rearrange("p (h d) -> p h d", d=HD),
                                    g_dc[:, c % 2, c // 2, :].unsqueeze(2).to_broadcast([P, HPG, HD]), ALU.mult))
                        last = TTO(smS[:, c + 1, :], smT, src, ALU.add)
                        if c < 4 * half + 3 - half:
                            ch.step(last)
                    last.then_inc(sem("sm_state"), 1)
                    dve.wait_ge(sem("sm_state"), 2 * i + half + 1)

                u_dta(0)
                u_dta(1)
                dve.wait_ge(sem("hg_rs"), i + 1)
                ch.step(TTO(ho[:], bank[3][:], hd[:], ALU.mult))
                STT(flat(y_hg, i), ho[:], vcol("hg", i), hog[:], ALU.mult, ALU.mult).then_inc(sem("hg_y"), 1)
                for c in range(GT):
                    ch.did(by_head(xdt, g_dt, c))
                dve.wait_ge(sem("sm_cum"), i + 1)
                ch.did(by_head(xdo, g_do, 0))
                by_head(xdo, g_do, 1).then_inc(sem("sm_xdo"), 1)
                decay_cb(0)
                u_dta(2)
                decay_cb(1)
                u_dta(3)
                states(0)
                decay_cb(2)
                decay_cb(3)
                states(1)
                if name == "gates":
                    dve.wait_ge(sem("mem_in"), 32)
                    for t in range(MT):
                        scaled_row(4, t, m_tok, m_tok, mem_bc, "m_rs", None, "m_scaled")
                else:
                    hg_pre(i + 1)

            def flat(t, i):
                return t[:, bass.ds(i, 1), :].rearrange("p a t -> p (a t)")

            hgrn_half("ssm0", 0, 0, 0)

            def mix(j):
                ssm_half("mix", j, j)
                hgrn_half("mix", j, 4, j + 1)

            loop(dve, "mix", mix, ch)
            last_group = GROUPS - 1
            ssm_half("gates", 0, last_group)
            sm_y(last_group)
            sm_final(last_group)
            for t in range(MT):
                row_lo(t, m_hi, m_lo, "m_hi_ready", "m_ready", 2)
            dve.wait_ge(sem("sm_done"), GROUPS + 1)
            for k in range(INNER // P):
                dve.wait_ge(sem("sm_hi_ready"), k + 1)
                TTO(sm_lo[:, k, :], y_ssm[:, k, :], sm_hi[:, k, :].bitcast(F32), ALU.subtract)\
                    .then_inc(sem("sm_split"), 1)
            dve.wait_ge(sem("gates_ready"), KT)

            def mssm(i):
                for c in range(2):
                    dve.wait_ge(slab_done[1], slab_count("mssm", i, 2 * c + 1))
                    TTO(flat(merged, 2 * i + c), bank[c][:], flat(gates, 2 * i + c), ALU.mult)\
                        .then_inc(bank_free[c], 1)

            loop(dve, "mssm", mssm, ch)

            for k in range(KT):
                dve.wait_ge(sem("hg_hi_ready"), k + 1)
                TTO(hg_lo[:, k, :], y_hg[:, k, :], hg_hi[:, k, :].bitcast(F32), ALU.subtract)\
                    .then_inc(sem("hg_split"), 1)

            def probs_in(h, t):
                dve.wait_ge(sem("xa_pT"), 4 * h + t + 1)
                v.tensor_copy(pT[:, :, t * P:(t + 1) * P],
                              bank[4 + t][:, 0:NM].rearrange("p (m t) -> p m t", t=P)).then_inc(sem("xa_p"), 1)

            def attend(name, i, h):
                for t in range(TT):
                    dve.wait_ge(sem("xa_s"), 4 * h + t + 1)
                    ch.step(v.reduce_max(st_inv[:, t:t + 1], bank[4 + t][:, 0:NM], mybir.AxisListType.X))
                    TS(st_max[:, t:t + 1], st_inv[:, t:t + 1], -SCALE, None, ALU.mult).then_inc(sem("xa_max"), 1)
                for t in range(TT):
                    dve.wait_ge(sem("xa_exp"), 4 * h + t + 1)
                    ch.step(v.reciprocal(st_inv[:, t:t + 1], st_sum[:, t:t + 1]))
                    TS(prob[:, t, :], prob[:, t, :], st_inv[:, t:t + 1], None, ALU.mult).then_inc(sem("xa_norm"), 1)
                for t in range(TT):
                    probs_in(h, t)
                for c in range(QT):
                    dve.wait_ge(sem("xa_o"), 2 * h + c + 1)
                    dve.wait_ge(sem("xa_y"), 2 * h + c + 1)
                    ch.step(v.tensor_copy(xo[:], bank[2 + c][:]))
                    split(flat(xa_hi, 2 * h + c), flat(xa_lo, 2 * h + c), xo[:]).then_inc(sem("xa_y"), 1)

            loop(dve, "xa", lambda h: attend("xa", h, h), ch)
            attend(None, 0, XA_HEADS - 1)
            dve.wait_ge(sem("xa_y"), 2 * XA_HEADS + 1)

            def merge(i):
                for c in range(2):
                    dve.wait_ge(slab_done[c], slab_count("merge", i, 2 + c))
                    dve.wait_ge(bank_free[c], tile_count("merge", i, c) + 1)
                    TTO(part[:, c, :], bank[c][:], gate[c][:], ALU.mult).then_inc(bank_free[c], 1)
                    dve.wait_ge(bank_free[c], tile_count("merge", i, 2 + c) + 1)
                    ch.step(TTO(part[:, 0, :], part[:, c, :], flat(merged, i) if c == 0 else part[:, 0, :], ALU.add))
                split(flat(mg_hi, i), flat(mg_lo, i), part[:, 0, :]).then_inc(sem("mg_split"), 1)
                wait_alone(dve, sem("mg_split"), i + 1)

            loop(dve, "merge", merge, ch)

            def stage(name, i, k, dst, hi, lo, row):
                s = k % 2
                wait_alone(dve, slab_done[s], slab_count(name, i, k) - 1)
                ch.did(TS(dst[:, s, 0, :], flat(hi, row), 1.0, None, ALU.mult))
                ch.did(TS(dst[:, s, 1, :], flat(lo, row), 1.0, None, ALU.mult))
                ch.settle()
                dve.sem_inc(sem("staged"), 1)

            def stage_all(name, dst, hi, lo):
                loop(dve, name, lambda i: [stage(name, i, k, dst, hi, lo, 2 + 2 * i + k) for k in range(2)], ch)

            def scaled_banks(n, t, y, w, rs_ready, y_free, done):
                dve.wait_ge(sem(rs_ready), t + 1)
                if t >= 2:
                    dve.wait_ge(sem(y_free), t - 1)
                for half in range(2):
                    c = slice(512 * half, 512 * half + 512)
                    last = STT(y[:, t % 2, c], bank[2 * t + half][:], col_rs[:, n, t:t + 1], w[:, c],
                               ALU.mult, ALU.mult)
                    if half == 0:
                        ch.did(last)
                last.then_inc(sem(done), 1)

            stage_all("wout", wo_stage, mg_hi, mg_lo)
            dve.wait_ge(sem("wo_in"), 48)
            for t in range(TT + 2):
                if t < TT:
                    scaled_banks(0, t, wo_y, post_bc, "wo_rs", "x2_new", "wo_y")
                if 1 <= t <= TT:
                    scaled_row(1, t - 1, xn2, x2, fpre_bc, "x2_rs", "h2_T", "xn2")
                if t >= 2:
                    row_lo(t - 2, h_hi, h_lo, "h2_hi", "h2_ready")
            dve.wait_ge(sem("h2_ready"), 2 * TT)

            def up(i):
                dve.wait_ge(sem("act_ready"), i + 1)
                dve.wait_ge(sem("up_sg"), i + 1)
                TTO(up_a[:], bank[0][:], up_sig[:], ALU.mult).then_inc(bank_free[0], 1)
                dve.wait_ge(bank_free[0], tile_count("up", i, 0) + 1)
                dve.wait_ge(slab_done[1], slab_count("up", i, 1))
                TTO(up_a[:], up_a[:], bank[1][:], ALU.mult).then_inc(bank_free[1], 1)
                dve.wait_ge(bank_free[1], tile_count("up", i, 1) + 1)
                split(flat(a_hi, i), flat(a_lo, i), up_a[:]).then_inc(sem("act_ready"), 1)

            loop(dve, "up", up, ch)
            dve.wait_ge(sem("act_ready"), FT + 1)
            stage_all("down", dn_stage, a_hi, a_lo)
            dve.wait_ge(sem("fpost_in"), 16)
            for t in range(TT):
                scaled_banks(2, t, dn_y, fpost_bc, "fo_rs", "fo_new", "fo_y")


_OUT = (1, 512, 1024)


def kernel(**inputs):
    import numpy as np
    import concourse.bacc as bacc
    from concourse.bass_utils import run_bass_kernel_spmd as run

    nc = bacc.Bacc("TRN2", target_bir_lowering=False, num_devices=1)
    arrays, args = {}, {}
    for name, value in inputs.items():
        a = np.ascontiguousarray(value)
        arrays[f"in_{name}"] = a
        args[name] = nc.dram_tensor(f"in_{name}", a.shape, mybir.dt.from_np(a.dtype), kind="ExternalInput").ap()
    args["out"] = nc.dram_tensor("out_0", _OUT, F32, kind="ExternalOutput").ap()
    hybrid_layer(nc, **args)
    result = run(nc, [arrays], core_ids=[0])
    return result.results[0]["out_0"]
```
